# Optimizing a Trainium2 kernel written in Bass

```python
import math
import jax, jax.numpy as jnp
from jax import lax
import numpy as np

D_MODEL = 1024
BATCH = 1
SEQ = 2048
DEPTH = 1

CTX_LEN = 256
GRID_W = 64

M_WIDTH = D_MODEL
M_HEADDIM = 64
M_HEADS = M_WIDTH // M_HEADDIM
M_GROUPS = 4
M_HEADS_PER_GROUP = M_HEADS // M_GROUPS
M_STATE = 128
M_XBC = M_WIDTH + 2 * M_GROUPS * M_STATE
M_CONV = 3
M_CHUNK = 128
DT_MIN = 1e-3
DT_MAX = 1e-1

H_WIDTH = D_MODEL
H_ORDER = 2
H_CONV = 3
H_EMB = 33
H_FILTER_HIDDEN = 64
H_DECAY_TARGET = 1e-2
H_FAST_DECAY_PCT = 0.3
H_SLOW_DECAY_PCT = 1.5

NORM_EPS = 1e-6

IN_LAYOUT = (
    ("m_z", M_WIDTH),
    ("m_xbc", M_XBC),
    ("m_dt", 2 * M_HEADS),
    ("h_gate", H_WIDTH),
    ("h_proj", (H_ORDER + 1) * H_WIDTH),
    ("g_m", D_MODEL),
    ("g_h", D_MODEL),
)
ALL_IN_NAMES = ("m_z", "m_xbc", "m_dt", "h_gate", "h_proj", "g_m", "g_h")
IN_TOTAL = M_WIDTH + M_XBC + 2 * M_HEADS + H_WIDTH + (H_ORDER + 1) * H_WIDTH + 2 * D_MODEL

kernel_name = "hybrid_ssd_hyena_gated_prefix_block"

def rmsnorm(x, w):
    x32 = x.astype(jnp.float32)
    y = x32 * lax.rsqrt(jnp.mean(x32 * x32, axis=-1, keepdims=True) + NORM_EPS)
    return (y * w.astype(jnp.float32)).astype(x.dtype)

def depthwise_conv_centred(u, w, b):
    width = w.shape[0]
    y = lax.conv_general_dilated(
        u, w[:, None, :].astype(u.dtype), window_strides=(1,),
        padding=[((width - 1) // 2, width // 2)],
        dimension_numbers=("NWC", "WIO", "NWC"),
        feature_group_count=u.shape[-1])
    return y + b.astype(u.dtype)

def in_projection(h, w_in, names):
    sel, off = [], 0
    for name, width in IN_LAYOUT:
        if name in names:
            sel.append((name, off, width))
        off += width
    w = jnp.concatenate([w_in[:, o:o + wd] for _, o, wd in sel], axis=1)
    y = h @ w
    out, pos = {}, 0
    for name, _, wd in sel:
        out[name] = y[..., pos:pos + wd]
        pos += wd
    return out

def ssd_chunked(xdt, a, bmat, cmat, init_state, with_output):
    bsz, seqlen = xdt.shape[:2]
    nc = seqlen // M_CHUNK
    xdt = xdt.reshape(bsz, nc, M_CHUNK, *xdt.shape[2:])
    a = a.reshape(bsz, nc, M_CHUNK, *a.shape[2:])
    bmat = bmat.reshape(bsz, nc, M_CHUNK, *bmat.shape[2:])
    a_cs = jnp.cumsum(a, axis=2)
    a_tot = a_cs[:, :, -1]
    chunk_states = jnp.einsum("bcsgn,bcsgr,bcsgrp->bcgrpn",
                              bmat, jnp.exp(a_tot[:, :, None] - a_cs), xdt)

    def carry_step(state, inp):
        s_chunk, a_chunk = inp
        return state * jnp.exp(a_chunk)[..., None, None] + s_chunk, state

    final_state, start_states = lax.scan(
        carry_step, init_state,
        (jnp.moveaxis(chunk_states, 1, 0), jnp.moveaxis(a_tot, 1, 0)))
    if not with_output:
        return None, final_state
    cmat = cmat.reshape(bsz, nc, M_CHUNK, *cmat.shape[2:])
    start_states = jnp.moveaxis(start_states, 0, 1)
    idx = jnp.arange(M_CHUNK)
    lower_tri = (idx[:, None] >= idx[None, :])[None, None, :, :, None, None]
    seg = a_cs[:, :, :, None] - a_cs[:, :, None, :]
    decay = jnp.exp(jnp.where(lower_tri, seg, -jnp.inf))
    scores = jnp.einsum("bcqgn,bcsgn->bcqsg", cmat, bmat)
    y_diag = jnp.einsum("bcqsg,bcqsgr,bcsgrp->bcqgrp", scores, decay, xdt)
    y_off = jnp.einsum("bcqgn,bcgrpn,bcqgr->bcqgrp", cmat, start_states, jnp.exp(a_cs))
    y = (y_diag + y_off).reshape(bsz, seqlen, *xdt.shape[3:])
    return y, final_state

def mamba_prep(xbc_raw, dt_raw, conv_w, conv_b, dt_bias, a_log):
    bsz, seqlen = xbc_raw.shape[:2]
    xbc = jax.nn.silu(depthwise_conv_centred(xbc_raw, conv_w, conv_b)).astype(jnp.float32)
    nb = M_GROUPS * M_STATE
    xs = xbc[..., :M_WIDTH].reshape(bsz, seqlen, M_GROUPS, M_HEADS_PER_GROUP, M_HEADDIM)
    bmat = xbc[..., M_WIDTH:M_WIDTH + nb].reshape(bsz, seqlen, M_GROUPS, M_STATE)
    cmat = xbc[..., M_WIDTH + nb:].reshape(bsz, seqlen, M_GROUPS, M_STATE)
    dt = jax.nn.softplus(
        dt_raw.astype(jnp.float32).reshape(bsz, seqlen, 2, M_GROUPS, M_HEADS_PER_GROUP)
        + dt_bias.astype(jnp.float32).reshape(2, M_GROUPS, M_HEADS_PER_GROUP))
    a_cont = -jnp.exp(a_log.astype(jnp.float32)).reshape(2, M_GROUPS, M_HEADS_PER_GROUP)
    return xs, bmat, cmat, dt, dt * a_cont

def mamba_mixer(xbc_l, dt_l, xbc_c, dt_c, conv_w, conv_b, dt_bias, a_log, d_skip, with_ctx_output):
    xs_l, b_l, c_l, dtd_l, a_l = mamba_prep(xbc_l, dt_l, conv_w, conv_b, dt_bias, a_log)
    xs_c, b_c, c_c, dtd_c, a_c = mamba_prep(xbc_c, dt_c, conv_w, conv_b, dt_bias, a_log)
    bsz, seqlen = xs_l.shape[:2]
    d_skip = d_skip.astype(jnp.float32).reshape(M_GROUPS, M_HEADS_PER_GROUP, 1)
    zero_state = jnp.zeros((bsz, M_GROUPS, M_HEADS_PER_GROUP, M_HEADDIM, M_STATE), jnp.float32)
    y_l = d_skip * xs_l
    y_c = d_skip * xs_c if with_ctx_output else None
    for direction in range(2):
        order = (lambda t: t) if direction == 0 else (lambda t: jnp.flip(t, axis=1))
        yc_dir, s_ctx = ssd_chunked(
            order(xs_c * dtd_c[:, :, direction, ..., None]), order(a_c[:, :, direction]),
            order(b_c), order(c_c), zero_state, with_ctx_output)
        yl_dir, _ = ssd_chunked(
            order(xs_l * dtd_l[:, :, direction, ..., None]), order(a_l[:, :, direction]),
            order(b_l), order(c_l), s_ctx, True)
        y_l = y_l + order(yl_dir)
        if with_ctx_output:
            y_c = y_c + order(yc_dir)
    y_l = y_l.reshape(bsz, seqlen, M_WIDTH)
    if with_ctx_output:
        y_c = y_c.reshape(bsz, xs_c.shape[1], M_WIDTH)
    return y_l, y_c

def gated_group_rmsnorm(y, z, w):
    g = y * jax.nn.silu(z.astype(jnp.float32))
    shape = g.shape
    g = g.reshape(*shape[:-1], M_GROUPS, M_WIDTH // M_GROUPS)
    g = g * lax.rsqrt(jnp.mean(g * g, axis=-1, keepdims=True) + NORM_EPS)
    return (g.reshape(shape) * w.astype(jnp.float32)).astype(z.dtype)

def hyena_filters(seqlen, w1, b1, w2, b2, w3, b3, freq, w_out):
    t = jnp.linspace(0.0, 1.0, seqlen, dtype=jnp.float32)[:, None]
    bands = (H_EMB - 1) // 2
    f = jnp.linspace(1e-4, bands - 1, bands, dtype=jnp.float32)[None, :]
    w = (2.0 * math.pi / seqlen) * jnp.arange(seqlen, dtype=jnp.float32)[:, None]
    feats = jnp.concatenate([t, jnp.cos(f * w), -jnp.sin(f * w)], axis=-1)
    freq = freq.astype(jnp.float32)
    hid = jnp.sin(freq * (feats @ w1.astype(jnp.float32) + b1.astype(jnp.float32)))
    hid = jnp.sin(freq * (hid @ w2.astype(jnp.float32) + b2.astype(jnp.float32)))
    hid = jnp.sin(freq * (hid @ w3.astype(jnp.float32) + b3.astype(jnp.float32)))
    filt = (hid @ w_out.astype(jnp.float32)).reshape(seqlen, 2, H_ORDER, H_WIDTH)
    min_decay = math.log(H_DECAY_TARGET) / H_SLOW_DECAY_PCT
    max_decay = math.log(H_DECAY_TARGET) / H_FAST_DECAY_PCT
    deltas = jnp.abs(jnp.linspace(min_decay, max_decay, H_WIDTH, dtype=jnp.float32))
    window = jnp.exp(-t[:, :, None, None] * deltas)
    return filt * window

def bidir_long_conv(u, h_fwd, h_bwd):
    seqlen = u.shape[1]
    k = jnp.concatenate([h_fwd[:1] + h_bwd[:1], h_fwd[1:], jnp.zeros_like(h_fwd[:1]),
                         jnp.flip(h_bwd[1:], axis=0)], axis=0)
    u_f = jnp.fft.rfft(u, n=2 * seqlen, axis=1)
    k_f = jnp.fft.rfft(k, n=2 * seqlen, axis=0)
    return jnp.fft.irfft(u_f * k_f[None], n=2 * seqlen, axis=1)[:, :seqlen]

def hyena_mixer(proj, conv_w, conv_b, w1, b1, w2, b2, w3, b3, freq, w_out, h_bias):
    seqlen = proj.shape[1]
    u = depthwise_conv_centred(proj, conv_w, conv_b).astype(jnp.float32)
    v, x1, x2 = jnp.split(u, 3, axis=-1)
    filt = hyena_filters(seqlen, w1, b1, w2, b2, w3, b3, freq, w_out)
    h_bias = h_bias.astype(jnp.float32)
    z = v
    for o, gate in enumerate((x1, x2)):
        z = gate * (bidir_long_conv(z, filt[:, 0, o], filt[:, 1, o]) + h_bias[o] * z)
    return z

def mixer_output(cols, y_m, y_h, m_norm_w, w_branch_m, w_branch_h, w_out):
    dtype = cols["m_z"].dtype
    ym = gated_group_rmsnorm(y_m, cols["m_z"], m_norm_w)
    yh = (y_h * jax.nn.silu(cols["h_gate"].astype(jnp.float32))).astype(dtype)
    merged = (jax.nn.sigmoid(cols["g_m"]) * (ym @ w_branch_m)
              + jax.nn.sigmoid(cols["g_h"]) * (yh @ w_branch_h))
    return merged @ w_out

def hybrid_layer(x, ctx, c, c_ctx, ada_w, ada_b, norm_w, w_in, m_conv_w, m_conv_b, m_dt_bias,
                 m_a_log, m_d, m_norm_w, h_conv_w, h_conv_b, h_w1, h_b1, h_w2, h_b2, h_w3, h_b3,
                 h_freq, h_w_out, h_bias, w_branch_m, w_branch_h, w_out, update_ctx):
    shift, scale, gate = jnp.split(jax.nn.silu(c) @ ada_w + ada_b, 3, axis=-1)
    shift_c, scale_c, gate_c = jnp.split(jax.nn.silu(c_ctx) @ ada_w + ada_b, 3, axis=-1)
    h = rmsnorm(x, norm_w) * (1.0 + scale[:, None]) + shift[:, None]
    hc = rmsnorm(ctx, norm_w) * (1.0 + scale_c) + shift_c
    cols = in_projection(h, w_in, ALL_IN_NAMES)
    cols_c = in_projection(hc, w_in, ALL_IN_NAMES if update_ctx else ("m_xbc", "m_dt"))
    y_m, y_m_c = mamba_mixer(cols["m_xbc"], cols["m_dt"], cols_c["m_xbc"], cols_c["m_dt"],
                             m_conv_w, m_conv_b, m_dt_bias, m_a_log, m_d, update_ctx)
    y_h = hyena_mixer(cols["h_proj"], h_conv_w, h_conv_b, h_w1, h_b1, h_w2, h_b2, h_w3, h_b3,
                      h_freq, h_w_out, h_bias)
    x_new = x + gate[:, None] * mixer_output(cols, y_m, y_h, m_norm_w, w_branch_m, w_branch_h, w_out)
    if update_ctx:
        y_h_c = hyena_mixer(cols_c["h_proj"], h_conv_w, h_conv_b, h_w1, h_b1, h_w2, h_b2, h_w3,
                            h_b3, h_freq, h_w_out, h_bias)
        ctx = ctx + gate_c * mixer_output(cols_c, y_m_c, y_h_c, m_norm_w, w_branch_m, w_branch_h, w_out)
    return x_new, ctx

def setup_inputs(seed: int = 0) -> dict:
    key = jax.random.key(seed)
    ks = iter(jax.random.split(key, 40))

    def nrm(shape, scale):
        return jax.random.normal(next(ks), shape, jnp.float32) * scale

    x = nrm((BATCH, SEQ, D_MODEL), 1.0)
    c = nrm((BATCH, D_MODEL), 1.0)
    ctx = nrm((BATCH, CTX_LEN, D_MODEL), 1.0)
    c_ctx = nrm((D_MODEL,), 1.0)
    ada_w = nrm((DEPTH, D_MODEL, 3 * D_MODEL), 0.5 * D_MODEL ** -0.5)
    ada_b = nrm((DEPTH, 3 * D_MODEL), 0.02)
    norm_w = 1.0 + nrm((DEPTH, D_MODEL), 0.02)
    w_in = nrm((DEPTH, D_MODEL, IN_TOTAL), D_MODEL ** -0.5)
    m_conv_w = nrm((DEPTH, M_CONV, M_XBC), M_CONV ** -0.5)
    m_conv_b = nrm((DEPTH, M_XBC), 0.02)
    dt0 = jnp.exp(jax.random.uniform(next(ks), (DEPTH, 2, M_HEADS), jnp.float32,
                                     minval=math.log(DT_MIN), maxval=math.log(DT_MAX)))
    m_dt_bias = dt0 + jnp.log(-jnp.expm1(-dt0))
    m_a_log = jnp.log(jax.random.uniform(next(ks), (DEPTH, 2, M_HEADS), jnp.float32,
                                         minval=1.0, maxval=16.0))
    m_d = 1.0 + nrm((DEPTH, M_HEADS), 0.02)
    m_norm_w = 1.0 + nrm((DEPTH, M_WIDTH), 0.02)
    h_conv_w = nrm((DEPTH, H_CONV, (H_ORDER + 1) * H_WIDTH), H_CONV ** -0.5)
    h_conv_b = nrm((DEPTH, (H_ORDER + 1) * H_WIDTH), 0.02)
    h_w1 = nrm((DEPTH, H_EMB, H_FILTER_HIDDEN), H_EMB ** -0.5)
    h_b1 = nrm((DEPTH, H_FILTER_HIDDEN), 0.02)
    h_w2 = nrm((DEPTH, H_FILTER_HIDDEN, H_FILTER_HIDDEN), H_FILTER_HIDDEN ** -0.5)
    h_b2 = nrm((DEPTH, H_FILTER_HIDDEN), 0.02)
    h_w3 = nrm((DEPTH, H_FILTER_HIDDEN, H_FILTER_HIDDEN), H_FILTER_HIDDEN ** -0.5)
    h_b3 = nrm((DEPTH, H_FILTER_HIDDEN), 0.02)
    h_freq = 1.0 + nrm((DEPTH, H_FILTER_HIDDEN), 0.02)
    h_w_out = nrm((DEPTH, H_FILTER_HIDDEN, 2 * H_ORDER * H_WIDTH), 0.02 * H_FILTER_HIDDEN ** -0.5)
    h_bias = nrm((DEPTH, H_ORDER, H_WIDTH), 1.0)
    w_branch_m = nrm((DEPTH, M_WIDTH, D_MODEL), M_WIDTH ** -0.5)
    w_branch_h = nrm((DEPTH, H_WIDTH, D_MODEL), H_WIDTH ** -0.5)
    w_out = nrm((DEPTH, D_MODEL, D_MODEL), D_MODEL ** -0.5)
    final_norm_w = 1.0 + nrm((D_MODEL,), 0.02)
    return {"x": x, "c": c, "ctx": ctx, "c_ctx": c_ctx, "ada_w": ada_w, "ada_b": ada_b,
            "norm_w": norm_w, "w_in": w_in, "m_conv_w": m_conv_w, "m_conv_b": m_conv_b,
            "m_dt_bias": m_dt_bias, "m_a_log": m_a_log, "m_d": m_d, "m_norm_w": m_norm_w,
            "h_conv_w": h_conv_w, "h_conv_b": h_conv_b, "h_w1": h_w1, "h_b1": h_b1,
            "h_w2": h_w2, "h_b2": h_b2, "h_w3": h_w3, "h_b3": h_b3, "h_freq": h_freq,
            "h_w_out": h_w_out, "h_bias": h_bias, "w_branch_m": w_branch_m,
            "w_branch_h": w_branch_h, "w_out": w_out, "final_norm_w": final_norm_w}

def reference(x, c, ctx, c_ctx, ada_w, ada_b, norm_w, w_in, m_conv_w, m_conv_b, m_dt_bias,
              m_a_log, m_d, m_norm_w, h_conv_w, h_conv_b, h_w1, h_b1, h_w2, h_b2, h_w3, h_b3,
              h_freq, h_w_out, h_bias, w_branch_m, w_branch_h, w_out, final_norm_w):
    for li in range(DEPTH):
        x, ctx = hybrid_layer(
            x, ctx, c, c_ctx, ada_w[li], ada_b[li], norm_w[li], w_in[li], m_conv_w[li],
            m_conv_b[li], m_dt_bias[li], m_a_log[li], m_d[li], m_norm_w[li], h_conv_w[li],
            h_conv_b[li], h_w1[li], h_b1[li], h_w2[li], h_b2[li], h_w3[li], h_b3[li],
            h_freq[li], h_w_out[li], h_bias[li], w_branch_m[li], w_branch_h[li], w_out[li],
            update_ctx=li + 1 < DEPTH)
    return rmsnorm(x, final_norm_w)


_drawn_inputs = setup_inputs


def setup_inputs(seed=0):
    import zlib

    import numpy as np

    out = dict(_drawn_inputs(seed))
    spreads = {}
    factors = {'ctx': 64.0,
     'c_ctx': 64.0,
     'ada_b': 3.057,
     'norm_w': 7.353,
     'm_conv_b': 64.0,
     'm_d': 64.0,
     'm_norm_w': 64.0,
     'h_conv_b': 8.0,
     'h_b1': 8.0,
     'h_b2': 8.0,
     'h_b3': 8.0,
     'h_freq': 8.0,
     'final_norm_w': 2.734,
     'm_conv_w': 8.0,
     'm_dt_bias': 8.0,
     'm_a_log': 8.0,
     'w_branch_m': 8.0}
    for name, (base, spread) in spreads.items():
        noise = np.random.default_rng([zlib.crc32(name.encode()), seed]).standard_normal(out[name].shape)
        drawn = base * np.exp(spread * noise) if base else spread * noise
        out[name] = __import__('jax').numpy.asarray(drawn.astype(out[name].dtype))
    for name, factor in factors.items():
        out[name] = (out[name] * factor).astype(out[name].dtype)
    return out
```

```python
from contextlib import ExitStack

import numpy as np
import concourse.bass as bass
from concourse import mybir

F32 = mybir.dt.float32
F32R = mybir.dt.float32r
ALU = mybir.AluOpType
ACT = mybir.ActivationFunctionType
AX_X = mybir.AxisListType.X

P = 128
D = 1024
KT = D // P
SEQ = 2048
CTX = 256
EPS = 1e-6
CHUNK = 128
NCH = SEQ // CHUNK
NCC = CTX // CHUNK
HEADS = 16
GROUPS = 4
HPG = HEADS // GROUPS
HD = 64
WREC = D + 4

NF = 2 * SEQ
N2 = 128
N1 = NF // N2
N1D = SEQ // N2
NK1 = N1 // 2 + 1
NR = N1
CB = 256
CG = 8
NG = CB // CG
FH = 64
H_EMB = 33
NBK = D // CB
NQ = NG // 4
NC = NG // 16
IM0, IM16 = NR, NR + 1
NPL = NR + 2


def plane(k1, part):
    if part == 0:
        return k1
    return {0: IM0, N1 // 2: IM16}.get(k1, N1 // 2 + k1)


def banks(ph, n):
    return [ph.ps(f"bank{i}", [P, 512]) for i in range(n)]


class Phase:

    def __init__(self, nc, tag, ctx):
        self.nc, self.tag, self.ctx, self.used = nc, tag, ctx, []
        ctx.callback(self.release)

    def release(self):
        if self.used:
            self.nc.clear_and_free_semaphores(self.used)
            self.nc.all_engine_barrier()

    def sb(self, name, shape, dt=F32):
        return self.ctx.enter_context(self.nc.sbuf_tensor(f"{self.tag}_{name}", shape, dt))

    def ps(self, name, shape, dt=F32):
        return self.ctx.enter_context(self.nc.psum_tensor(f"{self.tag}_{name}", shape, dt))

    def sem(self, name):
        self.used.append(self.nc.alloc_semaphore(f"{self.tag}_{name}"))
        return self.used[-1]

    def sems(self, name, n):
        return [self.sem(f"{name}{i}") for i in range(n)]


def phase_modulation(nc, t, keep):
    with ExitStack() as ctx:
        ph = Phase(nc, "ada", ctx)
        c_sb = ph.sb("c", [P, KT, 2])
        sc = ph.sb("silu", [P, KT, 2])
        sc_rep = ph.sb("silu_rep", [P, KT, P])
        aw = ph.sb("w", [P, 2, KT, D])
        gate_b = ph.sb("gate_bias", [P, D])
        one = ph.sb("scale1", [P, KT, 2])
        cols = ph.ps("cols", [P, 16, 2])
        gps = ph.ps("gate", [P, 2, 512])
        s_in, s_aw, s_silu, s_rep = ph.sem("in"), ph.sems("w", 2), ph.sem("silu"), ph.sem("rep")
        s_mm, s_dve = ph.sem("mm"), ph.sem("dve")
        aw_v = t["ada_w"].rearrange("(p k) n -> p k n", k=KT)
        block = ctx.enter_context(nc.Block())

        @block.sync
        def _(sp):
            sp.dma_start(c_sb[:], t["c_cols"]).then_inc(s_in, 16)
            sp.dma_start(keep["par"][:], t["par"]).then_inc(s_in, 16)
            sp.dma_start(gate_b[:], t["gate_bias"].to_broadcast([P, D])).then_inc(s_in, 16)
            for n in range(3):
                if n == 2:
                    sp.wait_ge(s_mm, 1)
                sp.dma_start(aw[:, n % 2], aw_v[:, :, n * D:(n + 1) * D]).then_inc(s_aw[n % 2], 16)

        @block.scalar
        def _(act):
            act.wait_ge(s_in, 48)
            nc.scalar.activation(sc[:], c_sb[:], ACT.Silu).then_inc(s_silu, 1)

        @block.tensor
        def _(pe):
            pe.wait_ge(s_silu, 1)
            for n in range(2):
                pe.wait_ge(s_aw[n], 16)
                for m in range(KT):
                    for k in range(KT):
                        mm = pe.matmul(cols[:, n * KT + m, :], aw[:, n, k, m * P:(m + 1) * P],
                                       sc[:, k, :], start=(k == 0), stop=(k == KT - 1))
                mm.then_inc(s_mm, 1)
            pe.wait_ge(s_aw[0], 32)
            pe.wait_ge(s_rep, 1)
            for h in range(2):
                for k in range(KT):
                    mm = pe.matmul(gps[:, h, :], sc_rep[:, k, :], aw[:, 0, k, h * 512:(h + 1) * 512],
                                   start=(k == 0), stop=(k == KT - 1))
            mm.then_inc(s_mm, 1)

        @block.vector
        def _(dve):
            dve.wait_ge(s_silu, 1)
            nc.vector.tensor_copy(sc_rep[:], sc[:, :, 0:1].to_broadcast([P, KT, P])).then_inc(s_rep, 1)
            dve.wait_ge(s_mm, 2)
            par = keep["par"]
            for v in range(2):
                nc.vector.tensor_tensor(keep["mod"][:, v, 1, :], cols[:, 0:KT, v],
                                        par[:, PAR["shift_b"]:PAR["shift_b"] + KT], ALU.add).then_inc(s_dve, 1)
                nc.vector.tensor_tensor(one[:, :, v], cols[:, KT:2 * KT, v],
                                        par[:, PAR["scale_b"]:PAR["scale_b"] + KT], ALU.add).then_inc(s_dve, 1)
                dve.wait_ge(s_dve, 2 + 3 * v)
                nc.vector.scalar_tensor_tensor(out=keep["mod"][:, v, 0, :], in0=one[:, :, v], scalar=1.0,
                                               in1=par[:, PAR["norm_w"]:PAR["norm_w"] + KT],
                                               op0=ALU.add, op1=ALU.mult).then_inc(s_dve, 1)
            dve.wait_ge(s_mm, 3)
            nc.vector.tensor_tensor(keep["gate"][:], gps[:].rearrange("p a n -> p (a n)"), gate_b[:], ALU.add)


def phase_norm(nc, tag, xT, T, G, scale, shift, h_hi, h_lo):
    BW = min(512, T)
    NB = T // BW
    NU = KT // G
    with ExitStack() as ctx:
        ph = Phase(nc, tag, ctx)
        x = ph.sb("x", [P, 2, KT, BW])
        sq = ph.sb("sq", [P, 2, BW])
        ms = ph.sb("ms", [P, 2, BW])
        rstd = ph.sb("rstd", [P, 2, BW])
        xn = ph.sb("xn", [P, 2, BW])
        val = ph.sb("val", [P, 2, BW])
        ones = ph.sb("ones", [P, P])
        ssq = ph.ps("ssq", [P, 2, 512])
        s_one, s_x, s_sq, s_mm = ph.sem("one"), ph.sems("x", 2), ph.sem("sq"), ph.sem("mm")
        s_ms, s_root, s_rstd, s_xn = ph.sem("ms"), ph.sem("root"), ph.sem("rstd"), ph.sem("xn")
        s_hi, s_val, s_lo = ph.sem("hi"), ph.sem("val"), ph.sem("lo")
        xv = xT.rearrange("(k p) t -> p k t", p=P)
        block = ctx.enter_context(nc.Block())

        @block.sync
        def _(sp):
            for b in range(NB):
                if b >= 2:
                    sp.wait_ge(s_xn, KT * (b - 1))
                sp.dma_start(x[:, b % 2], xv[:, :, b * BW:(b + 1) * BW]).then_inc(s_x[b % 2], 16)

        @block.scalar
        def _(act):
            def squares(u):
                b = u // NU
                act.wait_ge(s_x[b % 2], 16 * (b // 2 + 1))
                for k in range(G):
                    n = u * G + k
                    if n >= 2:
                        act.wait_ge(s_mm, n - 1)
                    nc.scalar.activation(sq[:, n % 2, :], x[:, b % 2, n % KT, :], ACT.Square).then_inc(s_sq, 1)
                act.wait_ge(s_ms, u + 1)
                if u >= 2:
                    act.wait_ge(s_xn, G * (u - 1))
                nc.scalar.activation(rstd[:, u % 2, :], ms[:, u % 2, :], ACT.Sqrt).then_inc(s_root, 1)

            squares(0)
            for u in range(NB * NU):
                if u + 1 < NB * NU:
                    squares(u + 1)
                b = u // NU
                for n in range(u * G, (u + 1) * G):
                    k = n % KT
                    act.wait_ge(s_xn, n + 1)
                    nc.scalar.activation(h_hi[:, k, b * BW:(b + 1) * BW], xn[:, n % 2, :], ACT.Identity,
                                         bias=shift[:, k:k + 1], scale=scale[:, k:k + 1]).then_inc(s_hi, 1)

        @block.tensor
        def _(pe):
            pe.wait_ge(s_one, 1)
            for u in range(NB * NU):
                if u >= 2:
                    pe.wait_ge(s_ms, u - 1)
                for k in range(G):
                    n = u * G + k
                    pe.wait_ge(s_sq, n + 1)
                    pe.matmul(ssq[:, u % 2, 0:BW], ones[:], sq[:, n % 2, :], start=(k == 0),
                              stop=(k == G - 1)).then_inc(s_mm, 1)

        @block.vector
        def _(dve):
            nc.vector.memset(ones[:], 1.0).then_inc(s_one, 1)

            def mean(u):
                dve.wait_ge(s_mm, G * (u + 1))
                if u >= 2:
                    dve.wait_ge(s_root, u - 1)
                nc.vector.tensor_scalar(ms[:, u % 2, :], ssq[:, u % 2, 0:BW], 1.0 / (G * P), EPS, ALU.mult,
                                        ALU.add).then_inc(s_ms, 1)

            mean(0)
            for u in range(NB * NU):
                if u + 1 < NB * NU:
                    mean(u + 1)
                b = u // NU
                dve.wait_ge(s_root, u + 1)
                nc.vector.reciprocal(rstd[:, u % 2, :], rstd[:, u % 2, :]).then_inc(s_rstd, 1)
                dve.wait_ge(s_rstd, u + 1)
                for n in range(u * G, (u + 1) * G):
                    k = n % KT
                    if n >= 2:
                        dve.wait_ge(s_hi, n - 1)
                        dve.wait_ge(s_lo, n - 1)
                    nc.vector.tensor_tensor(xn[:, n % 2, :], x[:, b % 2, k, :], rstd[:, u % 2, :],
                                            ALU.mult).then_inc(s_xn, 1)
                    dve.wait_ge(s_xn, n + 1)
                    nc.vector.tensor_scalar(val[:, n % 2, :], xn[:, n % 2, :], scale[:, k:k + 1],
                                            shift[:, k:k + 1], ALU.mult, ALU.add).then_inc(s_val, 1)
                    dve.wait_ge(s_val, n + 1)
                    dve.wait_ge(s_hi, n + 1)
                    nc.vector.tensor_tensor(h_lo[:, k, b * BW:(b + 1) * BW], val[:, n % 2, :],
                                            h_hi[:, k, b * BW:(b + 1) * BW].bitcast(F32),
                                            ALU.subtract).then_inc(s_lo, 1)


def phase_in_projection(nc, tag, w_rec, groups, T, h_hi, h_lo):
    BW = min(512, T)
    NB = T // BW
    FUNC = {"silu": ACT.Silu, "sigmoid": ACT.Sigmoid, "raw": ACT.Copy}
    with ExitStack() as ctx:
        ph = Phase(nc, tag, ctx)
        w = ph.sb("w", [P, 2, WREC])
        w_hi = ph.sb("w_hi", [P, 2, D], F32R)
        w_lo = ph.sb("w_lo", [P, 2, D], F32R)
        zero = ph.sb("zero", [P, 1])
        raw = ph.sb("raw", [P, 2, T + 2])
        acc = ph.sb("acc", [P, T])
        res = ph.sb("res", [P, 2, T])
        bank = [ph.ps(f"bank{b}", [P, 512]) for b in range(NB)]
        s_w, s_hi, s_lo, s_mm = ph.sems("w", 2), ph.sem("hi"), ph.sem("lo"), ph.sem("mm")
        s_ev, s_tap, s_conv = ph.sem("ev"), ph.sem("tap"), ph.sem("conv")
        s_res, s_st, s_pad, s_edge = ph.sem("res"), ph.sems("st", 2), ph.sem("pad"), ph.sem("edge")
        block = ctx.enter_context(nc.Block())

        def tiles(eng, body):
            done = convs = 0
            for g in groups:
                has_conv = g[2] in ("conv", "conv_silu")
                if g[1] > 1:
                    with eng.Fori(0, g[1] // 2) as i:
                        for j in range(2):
                            body(2 * i + (done + j), (done + j) % 2, i + (done + j) // 2, 2 * i + j,
                                 2 * i + (convs + j), g)
                else:
                    body(done, done % 2, done // 2, 0, convs, g)
                done += g[1]
                convs += g[1] * has_conv
            return done

        @block.sync
        def _(sp):
            def body(n, q, half, local, taps, g):
                sp.wait_ge(s_conv, n + 1)
                sp.dma_start(w[:, q], w_rec[bass.ds(local + g[0], 1)].rearrange("a p m -> p (a m)")
                             ).then_inc(s_w[q], 16)
            tiles(sp, body)

        @block.gpsimd
        def _(pool):
            nc.gpsimd.memset(zero[:], 0.0).then_inc(s_pad, 1)
            pool.wait_ge(s_pad, 1)

            def body(n, q, half, local, taps, g):
                pool.wait_ge(s_w[q], 16 * half + 16)
                pool.wait_ge(s_mm, NB * n + NB)
                nc.gpsimd.tensor_tensor(w_hi[:, q, :], w[:, q, 0:D], zero[:].to_broadcast([P, D]),
                                        ALU.add).then_inc(s_hi, 1)
                pool.wait_ge(s_hi, n + 1)
                nc.gpsimd.tensor_tensor(w_lo[:, q, :], w[:, q, 0:D], w_hi[:, q, :].bitcast(F32),
                                        ALU.subtract).then_inc(s_lo, 1)
            tiles(pool, body)

        @block.tensor
        def _(pe):
            pe.nop().then_inc(s_mm, 2 * NB)

            def body(n, q, half, local, taps, g):
                pe.wait_ge(s_lo, n + 1)
                for b in range(NB):
                    pe.wait_ge(s_ev, NB * n + (b + 1))
                    for k in range(KT):
                        m, r = slice(k * P, (k + 1) * P), slice(b * BW, (b + 1) * BW)
                        out = bank[b][:, 0:BW]
                        pe.matmul(out, w_hi[:, q, m], h_hi[:, k, r], start=(k == 0), stop=False)
                        pe.matmul(out, w_hi[:, q, m], h_lo[:, k, r], start=False, stop=False)
                        mm = pe.matmul(out, w_lo[:, q, m], h_hi[:, k, r], start=False, stop=(k == KT - 1))
                    mm.then_inc(s_mm, 1)
            tiles(pe, body)

        @block.scalar
        def _(act):
            for q in range(2):
                act.nop().then_inc(s_st[q], 16)
            act.nop().then_inc(s_ev, NB)

            def body(n, q, half, local, taps, g):
                conv = g[2] in ("conv", "conv_silu")
                if conv:
                    act.wait_ge(s_conv, n + 1)
                else:
                    act.wait_ge(s_st[q], 16 * half + 16)
                for b in range(NB):
                    act.wait_ge(s_mm, NB * n + (2 * NB + b + 1))
                    if conv:
                        dst, func = raw[:, q, 1 + b * BW:1 + (b + 1) * BW], ACT.Copy
                    else:
                        dst, func = res[:, q, b * BW:(b + 1) * BW], FUNC[g[2]]
                    nc.scalar.activation(dst, bank[b][:, 0:BW], func).then_inc(s_ev, 1)
                if g[2] == "conv_silu":
                    act.wait_ge(s_conv, n + 3)
                    act.wait_ge(s_st[q], 16 * half + 16)
                    nc.scalar.activation(res[:, q, :], acc[:], ACT.Silu).then_inc(s_res, 1)
                    act.wait_ge(s_res, n + 2)
                elif conv:
                    act.wait_ge(s_res, n + 2)
                else:
                    act.wait_ge(s_ev, NB * n + 2 * NB)
                    act.nop().then_inc(s_res, 1)
                act.dma_start(g[3][bass.ds(local * P, P), :], res[:, q, :]).then_inc(s_st[q], 16)
            total = tiles(act, body)
            for q in range(2):
                act.wait_ge(s_st[q], 16 * ((total + 1 - q) // 2 + 1))

        @block.vector
        def _(dve):
            dve.nop().then_inc(s_conv, 2)
            dve.nop().then_inc(s_res, 1)
            for q in range(2):
                nc.vector.memset(raw[:, q, 0:1], 0.0).then_inc(s_edge, 1)
                nc.vector.memset(raw[:, q, T + 1:T + 2], 0.0).then_inc(s_edge, 1)
            dve.wait_ge(s_edge, 4)

            def body(n, q, half, local, taps, g):
                if g[2] not in ("conv", "conv_silu"):
                    dve.wait_ge(s_lo, n + 1)
                    dve.wait_ge(s_conv, n + 2)
                    dve.nop().then_inc(s_conv, 1)
                    return
                dve.wait_ge(s_lo, n + 1)
                dve.wait_ge(s_ev, NB * n + 2 * NB)
                dve.wait_ge(s_res, n + 1)
                w0, w1, w2, bias = (w[:, q, D + j:D + j + 1] for j in range(4))
                nc.vector.tensor_scalar(acc[:], raw[:, q, 1:T + 1], w1, bias, ALU.mult, ALU.add).then_inc(s_tap, 1)
                dve.wait_ge(s_tap, 2 * taps + 1)
                nc.vector.scalar_tensor_tensor(out=acc[:], in0=raw[:, q, 0:T], scalar=w0, in1=acc[:],
                                               op0=ALU.mult, op1=ALU.add).then_inc(s_tap, 1)
                dve.wait_ge(s_tap, 2 * taps + 2)
                if g[2] == "conv_silu":
                    nc.vector.scalar_tensor_tensor(out=acc[:], in0=raw[:, q, 2:T + 2], scalar=w2, in1=acc[:],
                                                   op0=ALU.mult, op1=ALU.add).then_inc(s_conv, 1)
                else:
                    dve.wait_ge(s_st[q], 16 * half + 16)
                    nc.vector.scalar_tensor_tensor(out=res[:, q, :], in0=raw[:, q, 2:T + 2], scalar=w2,
                                                   in1=acc[:], op0=ALU.mult, op1=ALU.add).then_inc(s_res, 1)
                    dve.wait_ge(s_res, n + 2)
                    dve.nop().then_inc(s_conv, 1)
            tiles(dve, body)


def phase_filter_taps(nc, t, keep, taps_s):
    NB = SEQ // 512
    MAGIC = 12582912.0
    TURN = (6.28125, 0.00193500518798828125, 2 * np.pi - 6.28125 - 0.00193500518798828125)
    with ExitStack() as ctx:
        ph = Phase(nc, "taps", ctx)
        feats = ph.sb("feats", [H_EMB, SEQ])
        w1, w2, w3 = ph.sb("w1", [H_EMB, FH]), ph.sb("w2", [FH, FH]), ph.sb("w3", [FH, FH])
        pm = ph.sb("pm", [FH, 4])
        arg, turn, hid = ph.sb("arg", [FH, SEQ]), ph.sb("turn", [FH, SEQ]), ph.sb("hid", [FH, SEQ])
        trow = ph.sb("trow", [P, SEQ])
        window = ph.sb("window", [P, 2, SEQ])
        wo = ph.sb("wo", [FH, 2, 4, P])
        wc = ph.sb("wc", [FH, 2, 4, P])
        res = ph.sb("res", [P, 2, SEQ])
        ps = [ph.ps(f"ps{i}", [P, 4, 512]) for i in range(2)]
        s_in, s_mm, s_arg, s_hid = ph.sem("in"), ph.sem("mm"), ph.sem("arg"), ph.sem("hid")
        s_wo, s_wc, s_win = ph.sems("wo", 2), ph.sem("wc"), ph.sem("win")
        s_tm, s_res, s_fix, s_st = ph.sem("tm"), ph.sem("res"), ph.sem("fix"), ph.sems("st", 2)
        wo_v = t["h_w_out"].rearrange("h (q c) -> h q c", q=4)
        out_v = taps_s.rearrange("(o w s c) n -> o w s c n", o=2, w=NBK, s=2)
        block = ctx.enter_context(nc.Block())

        def tiles(eng):
            for blk in range(NBK):
                with eng.Fori(0, KT // NBK // 2) as i:
                    for j in range(2):
                        yield i, j, 2 * i + (KT // NBK * blk + j), i + KT // NBK // 2 * blk, blk

        @block.sync
        def _(sp):
            for dst, name in ((feats, "feats"), (w1, "h_w1"), (w2, "h_w2"), (w3, "h_w3"), (pm, "h_pm")):
                sp.dma_start(dst[:], t[name]).then_inc(s_in, 16)
            sp.dma_start(trow[:], t["trow"].to_broadcast([P, SEQ])).then_inc(s_in, 16)
            for i, j, m, half, blk in tiles(sp):
                sp.wait_ge(s_wc, 4 * m + 1)
                sp.dma_start(wo[:, j], wo_v[:, :, bass.ds(m * P, P)]).then_inc(s_wo[j], 16)

        @block.scalar
        def _(act):
            for layer in range(3):
                act.wait_ge(s_arg, 7 * layer + 7)
                nc.scalar.activation(hid[:], arg[:], ACT.Sin).then_inc(s_hid, 1)
            act.wait_ge(s_hid, 3)
            for j in range(2):
                act.nop().then_inc(s_st[j], 16)
            act.wait_ge(s_in, 96)
            for i, j, m, half, blk in tiles(act):
                act.wait_ge(s_res, 4 * m + 5)
                nc.scalar.activation(window[:, j, :], trow[:], ACT.Exp,
                                     scale=keep["par"][:, bass.ds(m + PAR["delta"], 1)]).then_inc(s_win, 1)
                for q in range(4):
                    act.wait_ge(s_res, 4 * m + q + 10)
                    if q % 2 == 0:
                        act.wait_ge(s_fix, 2 * m + q // 2 + 1)
                    act.dma_start(out_v[q // 2, blk, q % 2, bass.ds((2 * i + j) * P, P), :], res[:, q % 2, :]
                                  ).then_inc(s_st[q % 2], 16)
            for j in range(2):
                act.wait_ge(s_st[j], 16 * (2 * KT + 1))

        @block.tensor
        def _(pe):
            pe.wait_ge(s_in, 96)
            for layer, (w, src) in enumerate(((w1, feats), (w2, hid), (w3, hid))):
                if layer:
                    pe.wait_ge(s_hid, layer)
                for b in range(NB):
                    mm = pe.matmul(ps[0][0:FH, b, :], w[:], src[:, b * 512:(b + 1) * 512], start=True, stop=True)
                mm.then_inc(s_mm, 1)
            pe.wait_ge(s_hid, 3)
            for i, j, m, half, blk in tiles(pe):
                for q in range(4):
                    pe.wait_ge(s_wc, 4 * m + q + 6)
                    pe.wait_ge(s_res, 4 * m + q + 8)
                    for b in range(NB):
                        mm = pe.matmul(ps[q % 2][:, b, :], wc[:, j, q, :], hid[:, b * 512:(b + 1) * 512],
                                       start=True, stop=True)
                    mm.then_inc(s_tm, 1)

        @block.vector
        def _(dve):
            n = [0]

            def step(ins):
                n[0] += 1
                ins.then_inc(s_arg, 1)
                dve.wait_ge(s_arg, n[0])

            dve.wait_ge(s_in, 96)
            for layer in range(3):
                dve.wait_ge(s_mm, layer + 1)
                step(nc.vector.tensor_scalar(arg[:], ps[0][0:FH].rearrange("p a n -> p (a n)"), pm[:, layer:layer + 1],
                                             pm[:, 3:4], ALU.add, ALU.mult))
                step(nc.vector.tensor_scalar(turn[:], arg[:], float(1 / (2 * np.pi)), MAGIC, ALU.mult, ALU.add))
                step(nc.vector.tensor_scalar(turn[:], turn[:], MAGIC, None, ALU.subtract))
                for c in TURN:
                    step(nc.vector.scalar_tensor_tensor(out=arg[:], in0=turn[:], scalar=float(-c), in1=arg[:],
                                                        op0=ALU.mult, op1=ALU.add))
                step(nc.vector.tensor_scalar(arg[:], arg[:], 3.1415925, -3.1415925, ALU.min, ALU.max))
            dve.nop().then_inc(s_wc, 5)
            dve.nop().then_inc(s_res, 9)
            for i, j, m, half, blk in tiles(dve):
                dve.wait_ge(s_wo[j], 16 * half + 16)
                for o in range(2):
                    for s, op in enumerate((ALU.add, ALU.subtract)):
                        nc.vector.tensor_tensor(wc[:, j, 2 * o + s, :], wo[:, j, o, :], wo[:, j, 2 + o, :],
                                                op).then_inc(s_wc, 1)
                dve.wait_ge(s_win, m + 1)
                for q in range(4):
                    dve.wait_ge(s_tm, 4 * m + q + 1)
                    dve.wait_ge(s_st[q % 2], 32 * m + 16 * (q // 2) + 16)
                    nc.vector.tensor_tensor(res[:, q % 2, :], ps[q % 2][:].rearrange("p a n -> p (a n)"),
                                            window[:, j, :], ALU.mult).then_inc(s_res, 1)
                    if q % 2 == 0:
                        dve.wait_ge(s_res, 4 * m + q + 10)
                        nc.vector.tensor_tensor(res[:, 0, 0:1], res[:, 0, 0:1],
                                                keep["par"][:, bass.ds(m + (PAR["h_bias"] + KT * (q // 2)), 1)],
                                                ALU.add).then_inc(s_fix, 1)


def phase_filter_spectra(nc, t, taps_s, spec_s):
    NP = NG // 2
    with ExitStack() as ctx:
        ph = Phase(nc, "spec", ctx)
        f1 = ph.sb("f1", [P, NR * CG])
        tw = ph.sb("tw", [P, NK1, 3, P])
        xin = ph.sb("xin", [P, 2, 16, N2])
        y = ph.sb("y", [P, NR, CB])
        res = ph.sb("res", [P, 4, CB])
        bank = banks(ph, 8)
        s_c, s_ld, s_first, s_ev = ph.sem("c"), ph.sems("ld", 2), ph.sem("first"), ph.sems("ev", 2)
        s_second, s_res, s_st = ph.sem("second"), ph.sem("res"), ph.sems("st", 4)
        src = taps_s.rearrange("r (a n) -> (r a) n", n=N2).rearrange("(w g p) n -> w p g n", g=NG, p=P)
        dst = spec_s.rearrange("(w k p) (a n) -> w k p a n", k=NK1, p=P, a=2)
        stores = [len(range(r, NK1, 4)) for r in range(4)]
        block = ctx.enter_context(nc.Block())

        @block.sync
        def _(sp):
            sp.dma_start(f1[:], t["f1"]).then_inc(s_c, 16)
            sp.dma_start(tw[:], t["tw_fwd"]).then_inc(s_c, 16)
            with sp.Fori(0, 2 * NBK) as i:
                for part in range(2):
                    for c in range(NC):
                        sp.wait_ge(s_first, 2 * NP * i + (NP * part + 8 * c + 8))
                        for e in range(2):
                            sp.dma_start(xin[:, c % 2, 8 * e:8 * e + 8], src[bass.ds(2 * i + part, 1), :,
                                         16 * c + 8 * e:16 * c + 8 * e + 8, :].rearrange("w p g n -> p (w g) n")
                                         ).then_inc(s_ld[c % 2], 16)

        @block.tensor
        def _(pe):
            pe.nop().then_inc(s_first, 16)
            pe.wait_ge(s_c, 32)
            with pe.Fori(0, 2 * NBK) as i:
                for part in range(2):
                    for p in range(NP):
                        c = p // 8
                        if p % 8 == 0:
                            pe.wait_ge(s_ld[c % 2], 32 * NC * i + 32 * (NC // 2 * part + c // 2 + 1))
                        pe.wait_ge(s_ev[p % 2], NP * i + (NP // 2 * part + p // 2 + 1))
                        for g in range(2):
                            mm = pe.matmul(bank[p % 4][:, g * 256:(g + 1) * 256], xin[:, c % 2, (2 * p + g) % 16, :],
                                           f1[:], start=True, stop=True)
                        mm.then_inc(s_first, 1)
                    for e in range(2):
                        pe.wait_ge(s_ev[e], NP * i + (NP // 2 * (part + 1) + 2))
                    for k in range(NK1):
                        n = NK1 * part + k
                        pe.wait_ge(s_res, 2 * NK1 * i + (n + (1 if k >= 4 else 4)))
                        pairs = [((0, 2)[part], plane(k, 0))]
                        if 0 < k < NK1 - 1:
                            pairs.append(((1, 0)[part], plane(k, 1)))
                        for a, (m, pl) in enumerate(pairs):
                            mm = pe.matmul(bank[4 + k % 4][:, 0:CB], tw[:, k, m, :], y[:, pl, :], start=(a == 0),
                                           stop=(a == len(pairs) - 1))
                        mm.then_inc(s_second, 1)

        def take(eng_op, p):
            return eng_op(y[:, :, 16 * p:16 * (p + 1)].rearrange("p r (g c) -> p r g c", g=2),
                          bank[p % 4][:].rearrange("p (g r c) -> p r g c", g=2, c=CG))

        @block.scalar
        def _(act):
            act.nop().then_inc(s_ev[0], 2)
            act.nop().then_inc(s_res, 4)
            for r in range(4):
                act.nop().then_inc(s_st[r], 16)
            with act.Fori(0, 2 * NBK) as i:
                for part in range(2):
                    for p in range(0, NP, 2):
                        act.wait_ge(s_first, 2 * NP * i + (NP * part + p + 17))
                        take(nc.scalar.copy, p).then_inc(s_ev[0], 1)
                    for k in range(NK1):
                        n = NK1 * part + k
                        r = k % 4
                        act.wait_ge(s_second, 2 * NK1 * i + (n + 1))
                        act.wait_ge(s_st[r], 32 * stores[r] * i + 16 * (stores[r] * part + k // 4 + 1))
                        nc.scalar.copy(res[:, r, :], bank[4 + r][:, 0:CB]).then_inc(s_res, 1)
                        act.wait_ge(s_res, 2 * NK1 * i + (n + 5))
                        act.dma_start(dst[bass.ds(i, 1), k, :, part, :].rearrange("w p n -> p (w n)"),
                                      res[:, r, :]).then_inc(s_st[r], 16)
            for r in range(4):
                act.wait_ge(s_st[r], 16 * (2 * 2 * NBK * stores[r] + 1))

        @block.vector
        def _(dve):
            dve.nop().then_inc(s_ev[1], 2)
            with dve.Fori(0, 2 * NBK) as i:
                for part in range(2):
                    for p in range(1, NP, 2):
                        dve.wait_ge(s_first, 2 * NP * i + (NP * part + p + 17))
                        take(nc.vector.tensor_copy, p).then_inc(s_ev[1], 1)


def phase_long_conv(nc, tag, t, src_s, gate_s, dst_s, spec_s, order):
    NP, TP = NG // 2, NK1 * 2
    with ExitStack() as ctx:
        ph = Phase(nc, tag, ctx)
        f1 = ph.sb("f1", [P, NR * CG])
        tw = ph.sb("tw", [P, 2, NK1, 3, P])
        back = ph.sb("back", [P, 2, P])
        ident = ph.sb("ident", [P, P])
        xin = ph.sb("xin", [P, 2, 16, N2])
        gin = ph.sb("gin", [P, 2, 16, N2])
        res = ph.sb("res", [P, 2, 16, N2])
        y = ph.sb("y", [P, NPL, CB])
        spec = ph.sb("spec", [P, 2, 2, CB])
        prod = ph.sb("prod", [P, 2, 4, CB])
        w = ph.sb("w", [P, CB, NR])
        turned = ph.sb("turned", [P, 2, 2, 4 * N2])
        bank = banks(ph, 8)
        s_c, s_ld, s_gl, s_k = ph.sem("c"), ph.sems("ld", 2), ph.sems("gl", 2), ph.sems("k", 2)
        s_first, s_ev, s_u, s_prod, s_z = ph.sem("first"), ph.sems("ev", 2), ph.sem("u"), ph.sem("prod"), ph.sem("z")
        s_w, s_we, s_turn, s_te = ph.sem("w"), ph.sem("we"), ph.sem("turn"), ph.sems("te", 2)
        s_back, s_gate, s_st = ph.sem("back"), ph.sem("gate"), ph.sems("st", 2)

        def samples(s):
            return s.rearrange("r (a n) -> (r a) n", n=N2).rearrange("(w g p) n -> w p g n", g=NG, p=P)

        src, gate, dst = samples(src_s), samples(gate_s), samples(dst_s)
        spec_v = spec_s.rearrange("(w k p) n -> w k p n", k=NK1, p=P)
        NKQ = (len(range(0, NK1, 2)), len(range(1, NK1, 2)))
        block = ctx.enter_context(nc.Block())

        @block.sync
        def _(sp):
            for dst_sb, name in ((f1[:], "f1"), (tw[:, 0], "tw_fwd"), (tw[:, 1], "tw_inv"), (back[:], "back"),
                                 (ident[:], "ident")):
                sp.dma_start(dst_sb, t[name]).then_inc(s_c, 16)
            with sp.Fori(0, NBK) as i:
                def chunk(buf, view, c, sem):
                    for e in range(2):
                        sp.dma_start(buf[:, c % 2, 8 * e:8 * e + 8], view[bass.ds(i, 1), :,
                                     16 * c + 8 * e:16 * c + 8 * e + 8, :].rearrange("w p g n -> p (w g) n")
                                     ).then_inc(sem[c % 2], 16)

                for c in range(NC):
                    sp.wait_ge(s_first, NP * i + (8 * c + 8))
                    chunk(xin, src, c, s_ld)
                for k in range(NK1):
                    sp.wait_ge(s_prod, TP * i + (2 * k if k >= 2 else 2))
                    sp.dma_start(spec[:, k % 2], spec_v[bass.ds(i + order * NBK, 1), k]
                                 .rearrange("w p (a n) -> p (w a) n", a=2)).then_inc(s_k[k % 2], 16)
                    if k in (2, 3):
                        sp.wait_ge(s_gate, NQ * i + (4 * (k - 2) + 4))
                        chunk(gin, gate, k - 2, s_gl)
                for c in range(2, NC):
                    sp.wait_ge(s_gate, NQ * i + (4 * c + 4))
                    chunk(gin, gate, c, s_gl)

        @block.tensor
        def _(pe):
            pe.nop().then_inc(s_first, 16)
            pe.wait_ge(s_c, 80)
            with pe.Fori(0, NBK) as i:
                def forward(k):
                    if k >= 2:
                        pe.wait_ge(s_prod, TP * i + 2 * k)
                    ends = k in (0, NK1 - 1)
                    for part, mats in enumerate(((0, 1), (2, 0))):
                        out = bank[k % 2][:, part * CB:(part + 1) * CB]
                        mm = pe.matmul(out, tw[:, 0, k, mats[0], :], y[:, plane(k, 0), :], start=True, stop=ends)
                        if not ends:
                            mm = pe.matmul(out, tw[:, 0, k, mats[1], :], y[:, plane(k, 1), :], start=False, stop=True)
                    mm.then_inc(s_u, 1)

                def inverse(k):
                    pe.wait_ge(s_z, 2 * NK1 * i + (2 * k + 4))
                    if k == 0:
                        pe.wait_ge(s_gate, NQ * i + 8)
                    if k >= 2:
                        pe.wait_ge(s_we, NK1 * i + (k - 1))
                    for part, mats in enumerate(((0, 2), (1, 0))):
                        if part and k in (0, NK1 - 1):
                            continue
                        out = bank[4 + k % 2][:, part * CB:(part + 1) * CB]
                        pe.matmul(out, tw[:, 1, k, mats[0], :], y[:, plane(k, 0), :], start=True, stop=False)
                        mm = pe.matmul(out, tw[:, 1, k, mats[1], :], y[:, plane(k, 1), :], start=False, stop=True)
                    mm.then_inc(s_w, 1)

                def turn(q):
                    if q >= 2:
                        for h in range(2):
                            pe.wait_ge(s_te[h], NQ * i + (q - 1))
                    for h in range(2):
                        for g in range(4):
                            ch = 32 * q + CG * g + 4 * h
                            mm = pe.transpose(bank[2 * (q % 2) + h][:, g * P:(g + 1) * P],
                                              w[:, ch:ch + 4, :].rearrange("p c r -> p (c r)"), ident[:])
                    mm.then_inc(s_turn, 1)

                def last(q):
                    for h in range(2):
                        pe.wait_ge(s_te[h], NQ * i + (q + 1))
                    if q >= 2:
                        pe.wait_ge(s_gate, NQ * i + (q - 1 + 8))
                    out = bank[4 + q % 2][:]
                    pe.matmul(out, back[:, 0, :], turned[:, q % 2, 0, :], start=True, stop=False)
                    pe.matmul(out, back[:, 1, :], turned[:, q % 2, 1, :], start=False, stop=True).then_inc(s_back, 1)

                for p in range(NP):
                    c = p // 8
                    if p % 8 == 0:
                        pe.wait_ge(s_ld[c % 2], 16 * NC * i + (32 * (c // 2) + 32))
                    pe.wait_ge(s_ev[p % 2], NP // 2 * i + (p // 2 + 1))
                    for g in range(2):
                        mm = pe.matmul(bank[p % 4][:, g * 256:(g + 1) * 256], xin[:, c % 2, (2 * p + g) % 16, :],
                                       f1[:], start=True, stop=True)
                    mm.then_inc(s_first, 1)
                for e in range(2):
                    pe.wait_ge(s_ev[e], NP // 2 * i + (NP // 2 + 2))
                for k in range(NK1 + 1):
                    if k < NK1:
                        forward(k)
                    if k >= 1:
                        inverse(k - 1)
                pe.wait_ge(s_we, NK1 * i + NK1)
                turn(0)
                for q in range(NQ):
                    if q + 1 < NQ:
                        turn(q + 1)
                    last(q)

        def take(eng_op, p):
            return eng_op(y[:, 0:NR, 16 * p:16 * (p + 1)].rearrange("p r (g c) -> p r g c", g=2),
                          bank[p % 4][:].rearrange("p (g r c) -> p r g c", g=2, c=CG))

        @block.scalar
        def _(act):
            act.nop().then_inc(s_ev[0], 2)
            for r in range(2):
                act.nop().then_inc(s_st[r], 16)
            with act.Fori(0, NBK) as i:
                for p in range(0, NP, 2):
                    act.wait_ge(s_first, NP * i + (p + 17))
                    take(nc.scalar.copy, p).then_inc(s_ev[0], 1)
                for k in range(NK1):
                    act.wait_ge(s_w, NK1 * i + (k + 1))
                    np_ = 1 if k in (0, NK1 - 1) else 2
                    nc.scalar.copy(w[:, :, k:k + 16 * (np_ - 1) + 1:16].rearrange("p c a -> p a c"),
                                   bank[4 + k % 2][:, 0:np_ * CB].rearrange("p (a c) -> p a c", a=np_)
                                   ).then_inc(s_we, 1)

                def store(c):
                    act.wait_ge(s_gate, NQ * i + (4 * c + 4 + 8))
                    act.dma_start(dst[bass.ds(i, 1), :, 16 * c:16 * (c + 1), :].rearrange("w p g n -> p (w g) n"),
                                  res[:, c % 2]).then_inc(s_st[c % 2], 16)

                for q in range(NQ):
                    act.wait_ge(s_turn, NQ * i + (q + 1))
                    nc.scalar.copy(turned[:, q % 2, 0, :], bank[2 * (q % 2)][:]).then_inc(s_te[0], 1)
                    if q >= 5 and q % 4 == 1:
                        store(q // 4 - 1)
                store(NC - 1)
            for r in range(2):
                act.wait_ge(s_st[r], 16 * (NBK * NC // 2 + 1))

        @block.gpsimd
        def _(pool):
            pool.nop().then_inc(s_z, 2)
            with pool.Fori(0, NBK) as i:
                for k in range(NK1):
                    for part, op in enumerate((ALU.subtract, ALU.add)):
                        pool.wait_ge(s_prod, TP * i + (2 * k + 4))
                        nc.gpsimd.tensor_tensor(y[:, plane(k, part), :], prod[:, k % 2, part, :],
                                                prod[:, k % 2, 3 - part, :], op).then_inc(s_z, 1)

        @block.vector
        def _(dve):
            dve.nop().then_inc(s_ev[1], 2)
            dve.nop().then_inc(s_prod, 2)
            dve.nop().then_inc(s_gate, 8)
            with dve.Fori(0, NBK) as i:
                for p in range(1, NP, 2):
                    dve.wait_ge(s_first, NP * i + (p + 17))
                    take(nc.vector.tensor_copy, p).then_inc(s_ev[1], 1)
                for k in range(NK1):
                    dve.wait_ge(s_k[k % 2], 16 * NKQ[k % 2] * i + (16 * (k // 2) + 16))
                    dve.wait_ge(s_z, 2 * NK1 * i + (2 * (k - 1) + 2 if k >= 2 else 2))
                    dve.wait_ge(s_u, NK1 * i + (k + 1))
                    for a in range(2):
                        col = bank[k % 2][:, None, a * CB:(a + 1) * CB].to_broadcast([P, 2, CB])
                        nc.vector.tensor_tensor(prod[:, k % 2, 2 * a:2 * a + 2, :], col, spec[:, k % 2, :, :],
                                                ALU.mult).then_inc(s_prod, 1)
                for q in range(NQ + 1):
                    if q < NQ:
                        dve.wait_ge(s_turn, NQ * i + (q + 1))
                        nc.vector.tensor_copy(turned[:, q % 2, 1, :], bank[2 * (q % 2) + 1][:]).then_inc(s_te[1], 1)
                    if q >= 1:
                        r = q - 1
                        c = r // 4
                        if r % 4 == 0:
                            dve.wait_ge(s_gl[c % 2], 16 * NC * i + (32 * (c // 2) + 32))
                            dve.wait_ge(s_st[c % 2], 8 * NC * i + (16 * (c // 2) + 16))
                        dve.wait_ge(s_back, NQ * i + (r + 1))
                        at = (r % 4) * 4
                        nc.vector.tensor_tensor(res[:, c % 2, at:at + 4, :].rearrange("p g n -> p (g n)"),
                                                bank[4 + r % 2][:],
                                                gin[:, c % 2, at:at + 4, :].rearrange("p g n -> p (g n)"),
                                                ALU.mult).then_inc(s_gate, 1)


def phase_step_sizes(nc, t, dt_c, dt_s, ssd):
    NT = NCC + NCH
    H2 = 2 * HEADS
    with ExitStack() as ctx:
        ph = Phase(nc, "dt", ctx)
        raw = ph.sb("raw", [H2, NT * P])
        bias, a_neg = ph.sb("bias", [P, H2]), ph.sb("a", [P, H2])
        x, e, w, m = (ph.sb(n, [P, NT, H2]) for n in ("x", "e", "w", "m"))
        ps = ph.ps("turned", [P, 2, 512])
        sums = [ph.ps(f"sum{i}", [P, 512]) for i in range(6)]
        s_in, s_t, s_v, s_a, s_mm = ph.sem("in"), ph.sem("t"), ph.sem("v"), ph.sem("a"), ph.sem("mm")
        dt, a = ssd["dt"], ssd["a"]
        block = ctx.enter_context(nc.Block())

        @block.sync
        def _(sp):
            sp.dma_start(raw[:, 0:NCC * P], dt_c[0:H2, :]).then_inc(s_in, 16)
            sp.dma_start(raw[:, NCC * P:], dt_s[0:H2, :]).then_inc(s_in, 16)
            sp.dma_start(bias[:], t["m_dt_bias"].to_broadcast([P, H2])).then_inc(s_in, 16)
            sp.dma_start(a_neg[:], t["m_a_log"].to_broadcast([P, H2])).then_inc(s_in, 16)
            for name in ("ident", "masks", "d_row"):
                src = t[name].to_broadcast([P, HEADS]) if name == "d_row" else t[name]
                sp.dma_start(ssd[name][:], src).then_inc(s_in, 16)

        @block.tensor
        def _(pe):
            pe.wait_ge(s_in, 112)
            for c in range(NT):
                mm = pe.transpose(ps[:, c // 16, (c % 16) * H2:(c % 16 + 1) * H2], raw[:, c * P:(c + 1) * P],
                                  ssd["ident"][0:H2, 0:H2])
            mm.then_inc(s_t, 1)
            pe.wait_ge(s_v, LAST_DT)
            for i, (mask, d) in enumerate(((0, 0), (1, 0), (2, 1), (3, 1))):
                mm = pe.matmul(sums[i][:, 0:NT * HEADS], ssd["masks"][:, mask, :],
                               a[:, :, d * HEADS:(d + 1) * HEADS], start=True, stop=True)
            for d in range(2):
                mm = pe.matmul(sums[4 + d][:, 0:NT * HEADS], ssd["masks"][:, 4, :],
                               a[:, :, d * HEADS:(d + 1) * HEADS], start=True, stop=True)
            mm.then_inc(s_mm, 1)

        n_v = [0]

        @block.vector
        def _(dve):
            def step(ins):
                n_v[0] += 1
                ins.then_inc(s_v, 1)
                dve.wait_ge(s_v, n_v[0])

            dve.wait_ge(s_in, 112)
            dve.wait_ge(s_t, 1)
            bc = bias[:, None, :]
            step(nc.vector.tensor_tensor(x[:, 0:16, :], ps[:, 0, :].rearrange("p (c h) -> p c h", h=H2),
                                         bc.to_broadcast([P, 16, H2]), ALU.add))
            step(nc.vector.tensor_tensor(x[:, 16:NT, :], ps[:, 1, 0:(NT - 16) * H2].rearrange("p (c h) -> p c h", h=H2),
                                         bc.to_broadcast([P, NT - 16, H2]), ALU.add))
            step(nc.vector.tensor_scalar(w[:], x[:], -1.0, None, ALU.mult))
            step(nc.vector.tensor_tensor(w[:], w[:], x[:], ALU.min))
            dve.wait_ge(s_a, 3)
            step(nc.vector.tensor_scalar(a[:], e[:], -0.25, 1.0 / 3, ALU.mult, ALU.add))
            step(nc.vector.tensor_tensor(a[:], a[:], e[:], ALU.mult))
            step(nc.vector.tensor_scalar(a[:], a[:], -0.5, None, ALU.add))
            step(nc.vector.tensor_tensor(a[:], a[:], e[:], ALU.mult))
            step(nc.vector.scalar_tensor_tensor(out=a[:], in0=a[:], scalar=1.0, in1=e[:], op0=ALU.add, op1=ALU.mult))
            step(nc.vector.tensor_scalar(m[:], e[:], 1.0 / 128, None, ALU.is_lt))
            step(nc.vector.tensor_tensor(a[:], a[:], w[:], ALU.subtract))
            step(nc.vector.tensor_tensor(a[:], a[:], m[:], ALU.mult))
            step(nc.vector.tensor_tensor(a[:], a[:], w[:], ALU.add))
            step(nc.vector.scalar_tensor_tensor(out=dt[:], in0=x[:], scalar=0.0, in1=a[:], op0=ALU.max, op1=ALU.add))
            step(nc.vector.scalar_tensor_tensor(out=a[:], in0=dt[:], scalar=-1.0,
                                                in1=a_neg[:, None, :].to_broadcast([P, NT, H2]),
                                                op0=ALU.mult, op1=ALU.mult))
            assert n_v[0] == LAST_DT
            dve.wait_ge(s_a, 9)
            for d in range(2):
                step(nc.vector.tensor_tensor(ssd["tail"][:, :, d, :], ssd["tail"][:, :, d, :],
                                             dt[:, :, d * HEADS:(d + 1) * HEADS], ALU.mult))

        @block.scalar
        def _(act):
            act.wait_ge(s_in, 112)
            nc.scalar.activation(a_neg[:], a_neg[:], ACT.Exp).then_inc(s_a, 1)
            act.wait_ge(s_v, 4)
            nc.scalar.activation(e[:], w[:], ACT.Exp).then_inc(s_a, 1)
            act.wait_ge(s_a, 2)
            nc.scalar.activation(w[:], e[:], ACT.Ln, bias=1.0).then_inc(s_a, 1)
            act.wait_ge(s_mm, 1)
            for i, (name, d) in enumerate((("edge", 0), ("tail", 0), ("edge", 1), ("tail", 1), ("whole", 0),
                                           ("whole", 1))):
                nc.scalar.activation(ssd[name][:, :, d, :], sums[i][:, 0:NT * HEADS].rearrange("p (c h) -> p c h", h=HEADS),
                                     ACT.Exp).then_inc(s_a, 1)


LAST_DT = 15


def phase_token_major(nc, t, xbc_c, xbc_s, tok_s, ssd):
    NM = KT + GROUPS
    with ExitStack() as ctx:
        ph = Phase(nc, "tok", ctx)
        xin = ph.sb("in", [P, 2, NM, P])
        res = ph.sb("res", [P, 2, NM * P])
        bank = [ph.ps(f"b{i}", [P, 512]) for i in range(6)]
        s_ld, s_t, s_ev, s_st = ph.sems("ld", 2), ph.sem("t"), ph.sems("ev", 2), ph.sems("st", 2)
        dst = tok_s.rearrange("(c p) n -> c p n", p=P)
        block = ctx.enter_context(nc.Block())

        def chunks(eng, body):
            for src, n, done in ((xbc_c, NCC, 0), (xbc_s, NCH, NCC)):
                view = src[0:NM * P, :].rearrange("(m p) t -> p m t", p=P)
                with eng.Fori(0, n // 2) as i:
                    for q in range(2):
                        body(view, 2 * i + q, 2 * i + (done + q), i + done // 2, q)

        @block.sync
        def _(sp):
            def body(view, c, n, half, q):
                sp.wait_ge(s_t, n + 1)
                sp.dma_start(xin[:, q], view[:, :, bass.ds(c * P, P)]).then_inc(s_ld[q], 16)
            chunks(sp, body)

        @block.tensor
        def _(pe):
            pe.nop().then_inc(s_t, 2)

            def body(view, c, n, half, q):
                pe.wait_ge(s_ld[q], 16 * half + 16)
                pe.wait_ge(s_ev[0], 2 * n + 2)
                pe.wait_ge(s_ev[1], n + 1)
                for m in range(NM):
                    mm = pe.transpose(bank[3 * q + m // 4][:, (m % 4) * P:(m % 4 + 1) * P], xin[:, q, m, :],
                                      ssd["ident"][:])
                mm.then_inc(s_t, 1)
            chunks(pe, body)

        @block.scalar
        def _(act):
            act.nop().then_inc(s_ev[0], 4)
            for q in range(2):
                act.nop().then_inc(s_st[q], 16)

            def body(view, c, n, half, q):
                act.wait_ge(s_t, n + 3)
                act.wait_ge(s_st[q], 16 * half + 16)
                for b in (0, 2):
                    nc.scalar.copy(res[:, q, b * 512:(b + 1) * 512], bank[3 * q + b][:]).then_inc(s_ev[0], 1)
                act.wait_ge(s_ev[0], 2 * n + 6)
                act.wait_ge(s_ev[1], n + 3)
                act.dma_start(dst[bass.ds(n, 1)].rearrange("a p n -> p (a n)"), res[:, q, :]).then_inc(s_st[q], 16)
            chunks(act, body)
            for q in range(2):
                act.wait_ge(s_st[q], 16 * ((NCC + NCH) // 2 + 1))

        @block.vector
        def _(dve):
            dve.nop().then_inc(s_ev[1], 2)

            def body(view, c, n, half, q):
                dve.wait_ge(s_t, n + 3)
                dve.wait_ge(s_st[q], 16 * half + 16)
                nc.vector.tensor_copy(res[:, q, 512:1024], bank[3 * q + 1][:]).then_inc(s_ev[1], 1)
            chunks(dve, body)


def phase_states(nc, tok_s, st_s, ssd):
    XB = D + GROUPS * P
    with ExitStack() as ctx:
        ph = Phase(nc, "st", ctx)
        xb = ph.sb("xb", [P, 2, 2, XB])
        wx = ph.sb("wx", [P, 2, D])
        state = ph.sb("state", [P, 2, 2, D])
        faded = ph.sb("faded", [P, 2, D])
        ps = [ph.ps(f"s{d}", [P, 2, 512]) for d in range(2)]
        s_ld, s_wx, s_mm = [ph.sems(f"ld{d}", 2) for d in range(2)], ph.sems("wx", 2), ph.sems("mm", 2)
        s_fade, s_new = ph.sems("fade", 2), ph.sems("new", 2)
        s_st = [ph.sems(f"st{d}", 2) for d in range(2)]
        src = tok_s.rearrange("(c p) n -> c p n", p=P)
        dst = st_s.rearrange("(d c p) n -> d c p n", d=2, p=P)
        block = ctx.enter_context(nc.Block())

        def steps(eng, body):
            for s in range(NCC):
                body(s, 0, s, (s, NCC - 1 - s), None)
            with eng.Fori(0, NCH // 2) as i:
                for q in range(2):
                    f = 2 * i + q
                    b = i * (-2) + (NCH - 1 - q)
                    body(2 * i + (NCC + q), i + 1, q, (f + NCC, b + NCC), (f, b))

        @block.sync
        def _(sp):
            def body(s, half, q, chunk, latent):
                for d in range(2):
                    sp.wait_ge(s_mm[d], s + 1)
                    sp.dma_start(xb[:, q, d, :], src[bass.ds(chunk[d], 1)].rearrange("a p n -> p (a n)")
                                 ).then_inc(s_ld[d][q], 16)
            steps(sp, body)

        @block.tensor
        def _(pe):
            for d in range(2):
                pe.nop().then_inc(s_mm[d], 2)

            def body(s, half, q, chunk, latent):
                for d in range(2):
                    pe.wait_ge(s_wx[d], s + 1)
                    pe.wait_ge(s_new[d], s + 1)
                    for g in range(GROUPS):
                        mm = pe.matmul(ps[d][:, g // 2, (g % 2) * 256:(g % 2 + 1) * 256],
                                       xb[:, q, d, D + g * P:D + (g + 1) * P], wx[:, d, g * 256:(g + 1) * 256],
                                       start=True, stop=True)
                    mm.then_inc(s_mm[d], 1)
            steps(pe, body)

        @block.gpsimd
        def _(pool):
            def body(s, half, q, chunk, latent):
                for d in range(2):
                    pool.wait_ge(s_new[d], s + 1)
                    nc.gpsimd.tensor_tensor(faded[:, d, :].rearrange("p (h n) -> p h n", h=HEADS),
                                            state[:, d, q, :].rearrange("p (h n) -> p h n", h=HEADS),
                                            ssd["whole"][:, bass.ds(chunk[d], 1), d, :].rearrange("p a h -> p (a h)")
                                            [:, :, None].to_broadcast([P, HEADS, HD]), ALU.mult).then_inc(s_fade[d], 1)
            steps(pool, body)

        @block.scalar
        def _(act):
            for d in range(2):
                for q in range(2):
                    act.nop().then_inc(s_st[d][q], 16)

            def body(s, half, q, chunk, latent):
                if latent is None:
                    return
                for d in range(2):
                    act.wait_ge(s_new[d], s + 1)
                    act.dma_start(dst[d, bass.ds(latent[d], 1)].rearrange("a p n -> p (a n)"),
                                  state[:, d, q, :]).then_inc(s_st[d][q], 16)
            steps(act, body)
            for d in range(2):
                for q in range(2):
                    act.wait_ge(s_st[d][q], 16 * (NCH // 2 + 1))

        @block.vector
        def _(dve):
            for d in range(2):
                nc.vector.memset(state[:, d, 0, :], 0.0).then_inc(s_new[d], 1)

            def body(s, half, q, chunk, latent):
                for d in range(2):
                    dve.wait_ge(s_ld[d][q], 16 * half + 16)
                    dve.wait_ge(s_mm[d], s + 2)
                    nc.vector.tensor_tensor(wx[:, d, :].rearrange("p (h n) -> p h n", h=HEADS),
                                            xb[:, q, d, 0:D].rearrange("p (h n) -> p h n", h=HEADS),
                                            ssd["tail"][:, bass.ds(chunk[d], 1), d, :].rearrange("p a h -> p (a h)")
                                            [:, :, None].to_broadcast([P, HEADS, HD]), ALU.mult).then_inc(s_wx[d], 1)
                for d in range(2):
                    dve.wait_ge(s_mm[d], s + 3)
                    dve.wait_ge(s_fade[d], s + 1)
                    if latent is not None:
                        dve.wait_ge(s_st[d][1 - q], 16 * (half + q - 1) + 16)
                    nc.vector.tensor_tensor(state[:, d, 1 - q, :], faded[:, d, :], ps[d][:].rearrange("p a n -> p (a n)"),
                                            ALU.add).then_inc(s_new[d], 1)
            steps(dve, body)


def phase_ssd_outputs(nc, t, xbc_s, tok_s, st_s, z_s, g_s, ssd):
    with ExitStack() as ctx:
        ph = Phase(nc, "y", ctx)
        bc = ph.sb("bc", [P, 2, 2 * GROUPS, P])
        x = ph.sb("x", [P, 2, D])
        st = ph.sb("st", [P, 2, 2, D])
        z = ph.sb("z", [P, 2, KT, P])
        spread = ph.sb("spread", [P, 2, HEADS, P])
        decay = ph.sb("decay", [P, 2, HEADS, P])
        sc = ph.sb("sc", [P, 2, GROUPS, P])
        xdt = ph.sb("xdt", [P, 3, D])
        off = ph.sb("off", [P, 2, D])
        offs = ph.sb("offs", [P, D])
        y = ph.sb("y", [P, D])
        res = ph.sb("res", [P, 2, KT, P])
        p_sc = ph.ps("p_sc", [P, 512])
        p_seg = [ph.ps(f"p_seg{i}", [P, 512]) for i in range(2)]
        p_y = ph.ps("p_y", [P, 2, 512])
        p_off = ph.ps("p_off", [P, 2, 512])
        p_t = ph.ps("p_t", [P, 512])
        s_ld, s_stl, s_zl, s_gst = ph.sems("ld", 2), ph.sems("stl", 2), ph.sems("zl", 2), ph.sems("gst", 2)
        s_spread, s_xdt, s_scm, s_scs = ph.sem("spread"), ph.sem("xdt"), ph.sem("scm"), ph.sem("scs")
        s_seg, s_exp, s_dec = ph.sem("seg"), ph.sem("exp"), ph.sem("dec")
        s_diag, s_offm, s_off, s_offs = ph.sem("diag"), ph.sem("offm"), ph.sem("off"), ph.sem("offs")
        s_y, s_turn, s_res = ph.sem("ysum"), ph.sem("turn"), ph.sem("res")
        bc_v = xbc_s[D:, :].rearrange("(m p) t -> p m t", p=P)
        z_v, g_v = (v.rearrange("(m p) t -> p m t", p=P) for v in (z_s, g_s))
        x_v = tok_s.rearrange("(c p) n -> c p n", p=P)
        st_v = st_s.rearrange("(d c p) n -> c p d n", d=2, p=P)
        heads = lambda ap: ap.rearrange("p (h n) -> p h n", h=HEADS)
        per_head = lambda name, c, d: (ssd[name][:, bass.ds(c + NCC, 1), d, :].rearrange("p a h -> p (a h)"))
        block = ctx.enter_context(nc.Block())

        def chunks(eng, body):
            with eng.Fori(0, NCH // 2) as i:
                for q in range(2):
                    body(2 * i + q, i, q)

        @block.sync
        def _(sp):
            def body(c, half, q):
                sp.wait_ge(s_offm, 2 * c + 2)
                sp.wait_ge(s_xdt, 3 * c + 3)
                sp.dma_start(bc[:, q], bc_v[:, :, bass.ds(c * P, P)]).then_inc(s_ld[q], 16)
                sp.dma_start(x[:, q, :], x_v[bass.ds(c + NCC, 1), :, 0:D].rearrange("a p n -> p (a n)")
                             ).then_inc(s_ld[q], 16)
                sp.dma_start(st[:, q], st_v[bass.ds(c, 1)].rearrange("a p d n -> p (a d) n")).then_inc(s_stl[q], 16)
                sp.wait_ge(s_res, 2 * c + 2)
                sp.dma_start(z[:, q], z_v[:, :, bass.ds(half * (2 * P) + q * P, P)]).then_inc(s_zl[q], 16)
            chunks(sp, body)

        @block.gpsimd
        def _(pool):
            pool.nop().then_inc(s_xdt, 6)

            def body(c, half, q):
                for d in range(2):
                    pool.wait_ge(s_seg, 8 * c + 4 * d + 4)
                    nc.gpsimd.tensor_tensor(spread[:, d], ssd["masks"][:, 2 * d + 0, None, :].to_broadcast([P, HEADS, P]),
                                            ssd["a"][:, bass.ds(c + NCC, 1), d * HEADS:(d + 1) * HEADS]
                                            .rearrange("p a h -> p (a h)")[:, :, None].to_broadcast([P, HEADS, P]),
                                            ALU.mult).then_inc(s_spread, 1)
                pool.wait_ge(s_ld[q], 32 * half + 32)
                pool.wait_ge(s_diag, c + 1)
                for n in range(3):
                    f = (ssd["dt"][:, bass.ds(c + NCC, 1), n * HEADS:(n + 1) * HEADS].rearrange("p a h -> p (a h)")
                         if n < 2 else ssd["d_row"][:])
                    nc.gpsimd.tensor_tensor(heads(xdt[:, n, :]), heads(x[:, q, :]),
                                            f[:, :, None].to_broadcast([P, HEADS, HD]), ALU.mult).then_inc(s_xdt, 1)
                pool.wait_ge(s_off, 2 * c + 4)
                pool.wait_ge(s_y, c + 1)
                nc.gpsimd.tensor_tensor(offs[:], off[:, 0, :], off[:, 1, :], ALU.add).then_inc(s_offs, 1)
            chunks(pool, body)

        @block.tensor
        def _(pe):
            pe.nop().then_inc(s_seg, 8)
            pe.nop().then_inc(s_diag, 1)
            pe.nop().then_inc(s_offm, 4)

            def body(c, half, q):
                pe.wait_ge(s_ld[q], 32 * half + 32)
                pe.wait_ge(s_scs, 2 * c + 2)
                for g in range(GROUPS):
                    mm = pe.matmul(p_sc[:, g * P:(g + 1) * P], bc[:, q, g, :], bc[:, q, GROUPS + g, :], start=True,
                                   stop=True)
                mm.then_inc(s_scm, 1)
                for d in range(2):
                    pe.wait_ge(s_spread, 2 * c + d + 1)
                    for b in range(4):
                        n = 4 * d + b
                        pe.wait_ge(s_exp, 8 * c + n + 1)
                        pe.matmul(p_seg[n % 2][:], ssd["masks"][:, (1, 3)[d], :],
                                  spread[:, d, 4 * b:4 * b + 4, :].rearrange("p h q -> p (h q)"), start=True,
                                  stop=True).then_inc(s_seg, 1)
                pe.wait_ge(s_stl[q], 16 * half + 16)
                for d in range(2):
                    pe.wait_ge(s_off, 2 * c + d + 2)
                    for g in range(GROUPS):
                        mm = pe.matmul(p_off[:, g // 2, (g % 2) * 256:(g % 2 + 1) * 256], bc[:, q, GROUPS + g, :],
                                       st[:, q, d, g * 256:(g + 1) * 256], start=True, stop=True)
                    mm.then_inc(s_offm, 1)
                pe.wait_ge(s_dec, 8 * c + 9)
                pe.wait_ge(s_xdt, 3 * c + 9)
                pe.wait_ge(s_y, c + 1)
                for b in range(2):
                    pe.matmul(p_y[:, b, :], ssd["ident"][:], xdt[:, 2, b * 512:(b + 1) * 512], start=True,
                              stop=False, skip_group_check=True)
                    for h in range(8 * b, 8 * b + 8):
                        for d in range(2):
                            mm = pe.matmul(p_y[:, b, (h % 8) * HD:(h % 8 + 1) * HD], decay[:, d, h, :],
                                           xdt[:, d, h * HD:(h + 1) * HD], start=False,
                                           stop=(h % 8 == 7 and d == 1), skip_group_check=True)
                mm.then_inc(s_diag, 1)
                pe.wait_ge(s_y, c + 2)
                for b in range(2):
                    pe.wait_ge(s_res, 2 * c + b + 4)
                    for m in range(4):
                        mm = pe.transpose(p_t[:, m * P:(m + 1) * P], y[:, (4 * b + m) * P:(4 * b + m + 1) * P],
                                          ssd["ident"][:])
                    mm.then_inc(s_turn, 1)
            chunks(pe, body)

        @block.scalar
        def _(act):
            act.nop().then_inc(s_exp, 2)
            for q in range(2):
                act.nop().then_inc(s_gst[q], 16)

            def body(c, half, q):
                for n in range(8):
                    act.wait_ge(s_seg, 8 * c + n + 9)
                    act.wait_ge(s_diag, c + 1)
                    nc.scalar.activation(decay[:, n // 4, 4 * (n % 4):4 * (n % 4) + 4, :].rearrange("p h q -> p (h q)"),
                                         p_seg[n % 2][:], ACT.Exp).then_inc(s_exp, 1)
                act.wait_ge(s_res, 2 * c + 6)
                act.dma_start(g_v[:, :, bass.ds(c * P, P)], res[:, q]).then_inc(s_gst[q], 16)
            chunks(act, body)
            for q in range(2):
                act.wait_ge(s_gst[q], 16 * (NCH // 2 + 1))

        @block.vector
        def _(dve):
            for s, n in ((s_scs, 2), (s_off, 2), (s_y, 1), (s_res, 4), (s_dec, 1)):
                dve.nop().then_inc(s, n)

            def body(c, half, q):
                dve.wait_ge(s_scm, c + 1)
                for d in range(2):
                    dve.wait_ge(s_dec, 8 * c + 1)
                    nc.vector.tensor_tensor(sc[:, d], p_sc[:].rearrange("p (g q) -> p g q", g=GROUPS),
                                            ssd["masks"][:, 2 * d, None, :].to_broadcast([P, GROUPS, P]),
                                            ALU.mult).then_inc(s_scs, 1)
                dve.wait_ge(s_scs, 2 * c + 4)
                for n in range(8):
                    d, g = n // 4, n % 4
                    dve.wait_ge(s_exp, 8 * c + n + 3)
                    nc.vector.tensor_tensor(decay[:, d, 4 * g:4 * g + 4, :], decay[:, d, 4 * g:4 * g + 4, :],
                                            sc[:, d, g, None, :].to_broadcast([P, HPG, P]), ALU.mult).then_inc(s_dec, 1)
                for d in range(2):
                    dve.wait_ge(s_offm, 2 * c + d + 5)
                    nc.vector.tensor_tensor(heads(off[:, d, :]), heads(p_off[:].rearrange("p a n -> p (a n)")),
                                            per_head("edge", c, d)[:, :, None].to_broadcast([P, HEADS, HD]),
                                            ALU.mult).then_inc(s_off, 1)
                dve.wait_ge(s_offs, c + 1)
                dve.wait_ge(s_diag, c + 2)
                nc.vector.tensor_tensor(y[:], p_y[:].rearrange("p a n -> p (a n)"), offs[:], ALU.add).then_inc(s_y, 1)
                dve.wait_ge(s_zl[q], 16 * half + 16)
                dve.wait_ge(s_gst[q], 16 * half + 16)
                for b in range(2):
                    dve.wait_ge(s_turn, 2 * c + b + 1)
                    nc.vector.tensor_tensor(res[:, q, 4 * b:4 * b + 4, :].rearrange("p m n -> p (m n)"), p_t[:],
                                            z[:, q, 4 * b:4 * b + 4, :].rearrange("p m n -> p (m n)"),
                                            ALU.mult).then_inc(s_res, 1)
            chunks(dve, body)


def phase_gate_split(nc, a_s, b_s, h_hi, h_lo):
    HW = SEQ // 2
    NPC = KT * 2
    with ExitStack() as ctx:
        ph = Phase(nc, "gs", ctx)
        a, b, v = (ph.sb(n, [P, 2, HW]) for n in ("a", "b", "v"))
        s_ld, s_v, s_hi, s_lo = ph.sems("ld", 2), ph.sem("v"), ph.sem("hi"), ph.sem("lo")
        views = [(s.rearrange("(k p) t -> k p t", p=P)) for s in (a_s, b_s)]
        block = ctx.enter_context(nc.Block())

        @block.sync
        def _(sp):
            for n in range(NPC):
                if n >= 2:
                    sp.wait_ge(s_v, n - 1)
                for buf, view in zip((a, b), views):
                    sp.dma_start(buf[:, n % 2, :], view[n // 2, :, (n % 2) * HW:(n % 2 + 1) * HW]
                                 ).then_inc(s_ld[n % 2], 16)

        @block.vector
        def _(dve):
            for n in range(NPC):
                q, at = n % 2, slice((n % 2) * HW, (n % 2 + 1) * HW)
                dve.wait_ge(s_ld[q], 32 * (n // 2 + 1))
                if n >= 2:
                    dve.wait_ge(s_hi, n - 1)
                    dve.wait_ge(s_lo, n - 1)
                nc.vector.tensor_tensor(v[:, q, :], a[:, q, :], b[:, q, :], ALU.mult).then_inc(s_v, 1)
                dve.wait_ge(s_hi, n + 1)
                nc.vector.tensor_tensor(h_lo[:, n // 2, at], v[:, q, :], h_hi[:, n // 2, at].bitcast(F32),
                                        ALU.subtract).then_inc(s_lo, 1)

        @block.scalar
        def _(act):
            for n in range(NPC):
                act.wait_ge(s_v, n + 1)
                nc.scalar.activation(h_hi[:, n // 2, (n % 2) * HW:(n % 2 + 1) * HW], v[:, n % 2, :],
                                     ACT.Copy).then_inc(s_hi, 1)


def phase_branch(nc, tag, w_rec, first, h_hi, h_lo, gate_s, add_s, dst_s):
    NB, BW = SEQ // 512, 512
    with ExitStack() as ctx:
        ph = Phase(nc, tag, ctx)
        w = ph.sb("w", [P, 2, D])
        w_hi, w_lo = ph.sb("w_hi", [P, 2, D], F32R), ph.sb("w_lo", [P, 2, D], F32R)
        zero = ph.sb("zero", [P, 1])
        gate = ph.sb("gate", [P, 2, SEQ])
        add = ph.sb("add", [P, 2, SEQ]) if add_s is not None else None
        res = ph.sb("res", [P, SEQ])
        bank = [ph.ps(f"bank{b}", [P, 512]) for b in range(NB)]
        s_w, s_hi, s_lo, s_mm, s_side = ph.sems("w", 2), ph.sem("hi"), ph.sem("lo"), ph.sem("mm"), ph.sems("side", 2)
        s_g, s_sum, s_st, s_zero = ph.sem("gated"), ph.sem("sum"), ph.sem("st"), ph.sem("zero")
        sides = 1 if add is None else 2
        done = s_g if add is None else s_sum
        block = ctx.enter_context(nc.Block())

        def tiles(eng, body):
            with eng.Fori(0, KT // 2) as i:
                for q in range(2):
                    body(2 * i + q, i, q)

        @block.sync
        def _(sp):
            def body(n, half, q):
                sp.wait_ge(s_lo, n + 1)
                sp.dma_start(w[:, q], w_rec[bass.ds(n + first, 1), :, 0:D].rearrange("a p m -> p (a m)")
                             ).then_inc(s_w[q], 16)
                sp.wait_ge(done, NB * n + NB)
                sp.dma_start(gate[:, q, :], gate_s[bass.ds(n * P, P), :]).then_inc(s_side[q], 16)
                if add is not None:
                    sp.dma_start(add[:, q, :], add_s[bass.ds(n * P, P), :]).then_inc(s_side[q], 16)
            tiles(sp, body)

        @block.gpsimd
        def _(pool):
            nc.gpsimd.memset(zero[:], 0.0).then_inc(s_zero, 1)
            pool.wait_ge(s_zero, 1)
            pool.nop().then_inc(s_lo, 2)

            def body(n, half, q):
                pool.wait_ge(s_w[q], 16 * half + 16)
                pool.wait_ge(s_mm, NB * n + NB)
                nc.gpsimd.tensor_tensor(w_hi[:, q, :], w[:, q, :], zero[:].to_broadcast([P, D]),
                                        ALU.add).then_inc(s_hi, 1)
                pool.wait_ge(s_hi, n + 1)
                nc.gpsimd.tensor_tensor(w_lo[:, q, :], w[:, q, :], w_hi[:, q, :].bitcast(F32),
                                        ALU.subtract).then_inc(s_lo, 1)
            tiles(pool, body)

        @block.tensor
        def _(pe):
            pe.nop().then_inc(s_mm, 2 * NB)

            def body(n, half, q):
                pe.wait_ge(s_lo, n + 3)
                for b in range(NB):
                    pe.wait_ge(s_g, NB * n + (NB + b + 1))
                    for k in range(KT):
                        m, r = slice(k * P, (k + 1) * P), slice(b * BW, (b + 1) * BW)
                        pe.matmul(bank[b][:], w_hi[:, q, m], h_hi[:, k, r], start=(k == 0), stop=False)
                        pe.matmul(bank[b][:], w_hi[:, q, m], h_lo[:, k, r], start=False, stop=False)
                        mm = pe.matmul(bank[b][:], w_lo[:, q, m], h_hi[:, k, r], start=False, stop=(k == KT - 1))
                    mm.then_inc(s_mm, 1)
            tiles(pe, body)

        @block.vector
        def _(dve):
            dve.nop().then_inc(s_g, 2 * NB)
            if add is not None:
                dve.nop().then_inc(s_sum, 2 * NB)

            def body(n, half, q):
                dve.wait_ge(s_side[q], 16 * sides * half + 16 * sides)
                dve.wait_ge(s_st, 16 * n + 16)
                for b in range(NB):
                    r = slice(b * BW, (b + 1) * BW)
                    dve.wait_ge(s_mm, NB * n + (2 * NB + b + 1))
                    nc.vector.tensor_tensor(res[:, r], bank[b][:], gate[:, q, r], ALU.mult).then_inc(s_g, 1)
                    if add is not None:
                        dve.wait_ge(s_g, NB * n + (2 * NB + b + 1))
                        nc.vector.tensor_tensor(res[:, r], res[:, r], add[:, q, r], ALU.add).then_inc(s_sum, 1)
            tiles(dve, body)

        @block.scalar
        def _(act):
            act.nop().then_inc(s_st, 16)

            def body(n, half, q):
                act.wait_ge(done, NB * n + 3 * NB)
                act.dma_start(dst_s[bass.ds(n * P, P), :], res[:]).then_inc(s_st, 16)
            tiles(act, body)
            act.wait_ge(s_st, 16 * (KT + 1))


def phase_output(nc, t, keep, mix_s, out):
    NT = SEQ // P
    with ExitStack() as ctx:
        ph = Phase(nc, "out", ctx)
        w = ph.sb("w", [P, 2, D])
        wg = ph.sb("wg", [P, 2, D])
        w_hi, w_lo = ph.sb("w_hi", [P, KT, D], F32R), ph.sb("w_lo", [P, KT, D], F32R)
        mix = ph.sb("mix", [P, 2, KT, P])
        m_hi, m_lo = ph.sb("m_hi", [P, 2, KT, P], F32R), ph.sb("m_lo", [P, 2, KT, P], F32R)
        x = ph.sb("x", [P, 2, D])
        y = ph.sb("y", [P, 2, D])
        sq = ph.sb("sq", [P, D])
        ss = ph.sb("ss", [P, 4])
        fw = ph.sb("fw", [P, D])
        res = ph.sb("res", [P, 2, D])
        bank = [ph.ps(f"bank{b}", [P, 2, 512]) for b in range(2)]
        s_w, s_wg, s_whi, s_wlo, s_in = ph.sems("w", 2), ph.sem("wg"), ph.sem("whi"), ph.sem("wlo"), ph.sem("in")
        s_mix, s_x, s_mhi, s_mlo, s_mm = ph.sems("mix", 2), ph.sems("x", 2), ph.sem("mhi"), ph.sem("mlo"), ph.sem("mm")
        s_y, s_sq, s_ms, s_root, s_rec, s_res = (ph.sem(n) for n in ("y", "sq", "ms", "root", "rec", "res"))
        s_st = ph.sems("st", 2)
        mix_v = mix_s.rearrange("(k p) t -> p k t", p=P)
        block = ctx.enter_context(nc.Block())

        def tiles(eng, body):
            with eng.Fori(0, NT // 2) as i:
                for q in range(2):
                    body(2 * i + q, i, q)

        @block.sync
        def _(sp):
            sp.dma_start(fw[:], t["final_norm_w"].to_broadcast([P, D])).then_inc(s_in, 16)
            for k in range(KT):
                if k >= 2:
                    sp.wait_ge(s_wg, k - 1)
                sp.dma_start(w[:, k % 2, :], t["w_out"][k * P:(k + 1) * P, :]).then_inc(s_w[k % 2], 16)

            def body(n, half, q):
                sp.wait_ge(s_mlo, n + 1)
                sp.dma_start(mix[:, q], mix_v[:, :, bass.ds(n * P, P)]).then_inc(s_mix[q], 16)
                sp.wait_ge(s_y, n + 1)
                sp.dma_start(x[:, q, :], t["x"][bass.ds(n * P, P), :]).then_inc(s_x[q], 16)
            tiles(sp, body)

        @block.gpsimd
        def _(pool):
            pool.nop().then_inc(s_mlo, 2)

            def body(n, half, q):
                pool.wait_ge(s_mhi, n + 1)
                pool.wait_ge(s_mm, n + 1)
                nc.gpsimd.tensor_tensor(m_lo[:, q], mix[:, q], m_hi[:, q].bitcast(F32),
                                        ALU.subtract).then_inc(s_mlo, 1)
            tiles(pool, body)

        @block.tensor
        def _(pe):
            pe.nop().then_inc(s_mm, 2)
            pe.wait_ge(s_wlo, KT)

            def body(n, half, q):
                pe.wait_ge(s_mlo, n + 3)
                pe.wait_ge(s_y, n + 1)
                for b in range(2):
                    r = slice(b * 512, (b + 1) * 512)
                    for k in range(KT):
                        o = bank[q][:, b, :]
                        pe.matmul(o, m_hi[:, q, k, :], w_hi[:, k, r], start=(k == 0), stop=False)
                        pe.matmul(o, m_hi[:, q, k, :], w_lo[:, k, r], start=False, stop=False)
                        mm = pe.matmul(o, m_lo[:, q, k, :], w_hi[:, k, r], start=False, stop=(k == KT - 1))
                mm.then_inc(s_mm, 1)
            tiles(pe, body)

        @block.scalar
        def _(act):
            for k in range(KT):
                act.wait_ge(s_wg, k + 1)
                nc.scalar.activation(w_hi[:, k, :], wg[:, k % 2, :], ACT.Copy).then_inc(s_whi, 1)
            for q in range(2):
                act.nop().then_inc(s_st[q], 16)
            act.wait_ge(s_mix[0], 16)
            nc.scalar.activation(m_hi[:, 0], mix[:, 0], ACT.Copy).then_inc(s_mhi, 1)

            def body(n, half, q, last=False):
                if not last:
                    act.wait_ge(s_mix[1 - q], 16 * (half + q) + 16)
                    act.wait_ge(s_mm, n + 2)
                    nc.scalar.activation(m_hi[:, 1 - q], mix[:, 1 - q], ACT.Copy).then_inc(s_mhi, 1)
                act.wait_ge(s_y, n + 3)
                nc.scalar.activation(sq[:], y[:, q, :], ACT.Square, accum_out=ss[:, 0:1]).then_inc(s_sq, 1)
                act.wait_ge(s_ms, n + 1)
                nc.scalar.activation(ss[:, 2:3], ss[:, 1:2], ACT.Sqrt).then_inc(s_root, 1)
                act.wait_ge(s_res, n + 1)
                act.dma_start(out[bass.ds(n * P, P), :], res[:, q, :]).then_inc(s_st[q], 16)
            with act.Fori(0, NT // 2 - 1) as i:
                for q in range(2):
                    body(2 * i + q, i, q)
            body(NT - 2, NT // 2 - 1, 0)
            body(NT - 1, NT // 2 - 1, 1, last=True)
            for q in range(2):
                act.wait_ge(s_st[q], 16 * (NT // 2 + 1))

        @block.vector
        def _(dve):
            dve.wait_ge(s_in, 16)
            dve.nop().then_inc(s_y, 2)
            for k in range(KT):
                dve.wait_ge(s_w[k % 2], 16 * (k // 2 + 1))
                if k >= 2:
                    dve.wait_ge(s_wlo, k - 1)
                nc.vector.tensor_tensor(wg[:, k % 2, :], w[:, k % 2, :], keep["gate"][:], ALU.mult).then_inc(s_wg, 1)
                dve.wait_ge(s_whi, k + 1)
                nc.vector.tensor_tensor(w_lo[:, k, :], wg[:, k % 2, :], w_hi[:, k, :].bitcast(F32),
                                        ALU.subtract).then_inc(s_wlo, 1)

            def body(n, half, q):
                dve.wait_ge(s_x[q], 16 * half + 16)
                dve.wait_ge(s_mm, n + 3)
                nc.vector.tensor_tensor(y[:, q, :], x[:, q, :], bank[q][:].rearrange("p a n -> p (a n)"),
                                        ALU.add).then_inc(s_y, 1)
                dve.wait_ge(s_sq, n + 1)
                nc.vector.tensor_scalar(ss[:, 1:2], ss[:, 0:1], 1.0 / D, EPS, ALU.mult, ALU.add).then_inc(s_ms, 1)
                dve.wait_ge(s_root, n + 1)
                nc.vector.reciprocal(ss[:, 3:4], ss[:, 2:3]).then_inc(s_rec, 1)
                dve.wait_ge(s_rec, n + 1)
                dve.wait_ge(s_st[q], 16 * half + 16)
                nc.vector.scalar_tensor_tensor(out=res[:, q, :], in0=y[:, q, :], scalar=ss[:, 3:4], in1=fw[:],
                                               op0=ALU.mult, op1=ALU.mult).then_inc(s_res, 1)
            tiles(dve, body)


PAR_LAYOUT = (("shift_b", KT), ("scale_b", KT), ("norm_w", KT), ("m_norm_w", KT), ("h_bias", 2 * KT),
              ("delta", KT), ("zero", KT))
PAR, _at = {}, 0
for _name, _n in PAR_LAYOUT:
    PAR[_name] = _at
    _at += _n
NPAR = _at


def columns(v):
    return np.ascontiguousarray(np.reshape(v, (-1, P)).T)


def layout(inputs):
    a = {k: np.asarray(v) for k, v in inputs.items()}
    f = np.float32
    out = {}
    out["x"] = a["x"][0]
    out["xT"] = a["x"][0].T
    out["ctxT"] = a["ctx"][0].T
    out["c_cols"] = np.stack([a["c"][0].reshape(P, KT), a["c_ctx"].reshape(P, KT)], axis=2)
    out["ada_w"] = a["ada_w"][0]
    out["gate_bias"] = a["ada_b"][:, 2 * D:]
    w = a["w_in"][0]
    o_xbc = D
    o_dt = o_xbc + 2 * D
    o_rest = o_dt + 2 * HEADS
    dt = np.concatenate([w[:, o_dt:o_rest], np.zeros((D, P - 2 * HEADS), f)], axis=1)
    w = np.concatenate([w[:, :o_dt], dt, w[:, o_rest:]], axis=1)
    nt = w.shape[1] // P
    rec = np.zeros((nt, P, WREC), f)
    rec[:, :, :D] = w.reshape(KT, P, nt, P).transpose(2, 1, 0, 3).reshape(nt, P, D)
    for first, cw, cb in ((T_XBC, a["m_conv_w"][0], a["m_conv_b"][0]), (T_PROJ, a["h_conv_w"][0], a["h_conv_b"][0])):
        n = cb.shape[0] // P
        taps = np.concatenate([cw, cb[None]], axis=0)
        rec[first:first + n, :, D:] = taps.reshape(4, n, P).transpose(1, 2, 0)
    out["w_rec"] = rec
    lo, hi = np.log(f(1e-2)) / f(1.5), np.log(f(1e-2)) / f(0.3)
    ds = np.arange(D, dtype=f) / f(D - 1)
    delta = np.abs(f(lo) * (f(1) - ds) + f(hi) * ds).astype(f)
    out["par"] = np.concatenate([columns(v) for v in (
        a["ada_b"][0, :D], a["ada_b"][0, D:2 * D], a["norm_w"][0], a["m_norm_w"][0],
        a["h_bias"][0].reshape(-1), delta, np.zeros(D, f))], axis=1)
    out["w_br"] = np.concatenate([
        a[k][0].reshape(KT, P, KT, P).transpose(2, 1, 0, 3).reshape(KT, P, D) for k in ("w_branch_m", "w_branch_h")])
    out["w_out"] = a["w_out"][0]
    out["final_norm_w"] = a["final_norm_w"][None]
    out["m_dt_bias"] = a["m_dt_bias"][0].reshape(1, -1)
    out["m_a_log"] = a["m_a_log"][0].reshape(1, -1)
    out["d_row"] = a["m_d"]
    out["h_pm"] = np.stack([a[k][0] for k in ("h_b1", "h_b2", "h_b3", "h_freq")], axis=1)
    for k in ("h_w1", "h_w2", "h_w3", "h_w_out"):
        out[k] = a[k][0]
    out.update(constants())
    return {k: np.ascontiguousarray(v) for k, v in out.items()}


def constants():
    f = np.float32
    out = {}
    t = np.arange(SEQ, dtype=f) / f(SEQ - 1)
    bands = (H_EMB - 1) // 2
    bstep = np.arange(bands, dtype=f) / f(bands - 1)
    bf = f(1e-4) * (f(1) - bstep) + f(bands - 1) * bstep
    w = f(2.0 * np.pi / SEQ) * np.arange(SEQ, dtype=f)
    fw = (bf[:, None] * w[None, :]).astype(f).astype(np.float64)
    out["feats"] = np.concatenate([t[None], np.cos(fw), -np.sin(fw)], axis=0).astype(f)
    out["trow"] = -t[None]
    n1 = np.arange(N1D)[:, None]
    k1 = np.arange(NK1)[None, :]
    ang = 2 * np.pi * n1 * k1 / N1
    fwd = np.concatenate([np.cos(ang), -np.sin(ang)[:, 1:NK1 - 1]], axis=1)
    out["f1"] = np.einsum("ar,cd->card", fwd, np.eye(CG)).reshape(P, NR * CG).astype(f)
    al = np.where((np.arange(NK1) == 0) | (np.arange(NK1) == NK1 - 1), 1.0, 2.0) / NF
    inv = np.concatenate([np.cos(ang) * al, (-np.sin(ang) * al)[:, 1:NK1 - 1]], axis=1)
    eye = np.eye(CG).reshape(2, 4, CG)
    out["back"] = np.einsum("ar,hcd->crhda", inv, eye).reshape(P, 2, P).astype(f)
    n2 = np.arange(N2)[:, None, None]
    k2 = np.arange(N2)[None, None, :]
    kk = np.arange(NK1)[None, :, None] + N1 * k2
    th = 2 * np.pi * ((n2 * kk) % NF) / NF
    tw = np.stack([np.cos(th), np.sin(th), -np.sin(th)], axis=2)
    out["tw_fwd"] = tw.astype(f)
    out["tw_inv"] = tw.transpose(3, 1, 2, 0).astype(f)
    out["ident"] = np.eye(P, dtype=f)
    r, c = np.arange(P)[:, None], np.arange(P)[None, :]
    out["masks"] = np.stack([r <= c, r > c, r >= c, r < c, r >= 0 * c], axis=1).astype(f)
    return out


T_Z, T_XBC = 0, KT
T_DT = T_XBC + 2 * KT
T_HG = T_DT + 1
T_PROJ = T_HG + KT
T_G = T_PROJ + 3 * KT
N_TILES = T_G + 2 * KT


def program(nc, t, out):
    def scratch(name, rows, cols):
        return nc.dram_tensor(name, [rows, cols], F32).ap()

    z_s = scratch("z_s", D, SEQ)
    xbc_s = scratch("xbc_s", 2 * D, SEQ)
    xbc_c = scratch("xbc_c", 2 * D, CTX)
    dt_s = scratch("dt_s", P, SEQ)
    dt_c = scratch("dt_c", P, CTX)
    hg_s = scratch("hg_s", D, SEQ)
    u_s = scratch("u_s", 3 * D, SEQ)
    g_s = scratch("g_s", 2 * D, SEQ)
    taps_s = scratch("taps_s", 4 * D, SEQ)
    spec_s = scratch("spec_s", 2 * NBK * NK1 * P, 2 * CB)
    z1_s = scratch("z1_s", D, SEQ)
    z2_s = scratch("z2_s", D, SEQ)
    tok_s = scratch("tok_s", (NCC + NCH) * P, D + GROUPS * P)
    st_s = scratch("st_s", 2 * NCH * P, D)
    ym_s = scratch("ym_s", D, SEQ)
    part_s = scratch("part_s", D, SEQ)
    mix_s = scratch("mix_s", D, SEQ)
    with ExitStack() as ctx:
        ph = Phase(nc, "keep", ctx)
        keep = {"par": ph.sb("par", [P, NPAR]), "mod": ph.sb("mod", [P, 2, 2, KT]), "gate": ph.sb("gate", [P, D])}
        mod, par = keep["mod"], keep["par"]
        phase_modulation(nc, t, keep)
        with ExitStack() as hctx:
            h = Phase(nc, "hc", hctx)
            hi, lo = h.sb("hi", [P, KT, CTX], F32R), h.sb("lo", [P, KT, CTX], F32R)
            phase_norm(nc, "nc", t["ctxT"], CTX, KT, mod[:, 1, 0, :], mod[:, 1, 1, :], hi, lo)
            phase_in_projection(nc, "pc", t["w_rec"], [(T_XBC, 2 * KT, "conv_silu", xbc_c), (T_DT, 1, "raw", dt_c)],
                                CTX, hi, lo)
        with ExitStack() as hctx:
            h = Phase(nc, "hl", hctx)
            hi, lo = h.sb("hi", [P, KT, SEQ], F32R), h.sb("lo", [P, KT, SEQ], F32R)
            phase_norm(nc, "nl", t["xT"], SEQ, KT, mod[:, 0, 0, :], mod[:, 0, 1, :], hi, lo)
            phase_in_projection(nc, "pl", t["w_rec"], [
                (T_Z, KT, "silu", z_s), (T_XBC, 2 * KT, "conv_silu", xbc_s), (T_DT, 1, "raw", dt_s),
                (T_HG, KT, "silu", hg_s), (T_PROJ, 3 * KT, "conv", u_s), (T_G, 2 * KT, "sigmoid", g_s)],
                SEQ, hi, lo)
        phase_filter_taps(nc, t, keep, taps_s)
        phase_filter_spectra(nc, t, taps_s, spec_s)
        phase_long_conv(nc, "c0", t, u_s[0:D, :], u_s[D:2 * D, :], z1_s, spec_s, 0)
        phase_long_conv(nc, "c1", t, z1_s, u_s[2 * D:3 * D, :], z2_s, spec_s, 1)
        with ExitStack() as sctx:
            ssd = ssd_buffers(Phase(nc, "ssd", sctx))
            phase_step_sizes(nc, t, dt_c, dt_s, ssd)
            phase_token_major(nc, t, xbc_c, xbc_s, tok_s, ssd)
            phase_states(nc, tok_s, st_s, ssd)
            phase_ssd_outputs(nc, t, xbc_s, tok_s, st_s, z_s, ym_s, ssd)
        with ExitStack() as hctx:
            h = Phase(nc, "ho", hctx)
            hi, lo = h.sb("hi", [P, KT, SEQ], F32R), h.sb("lo", [P, KT, SEQ], F32R)
            phase_norm(nc, "ng", ym_s, SEQ, KT // GROUPS, par[:, PAR["m_norm_w"]:PAR["m_norm_w"] + KT],
                       par[:, PAR["zero"]:PAR["zero"] + KT], hi, lo)
            phase_branch(nc, "bm", t["w_br"], 0, hi, lo, g_s[0:D, :], None, part_s)
            phase_gate_split(nc, z2_s, hg_s, hi, lo)
            phase_branch(nc, "bh", t["w_br"], KT, hi, lo, g_s[D:2 * D, :], part_s, mix_s)
        phase_output(nc, t, keep, mix_s, out)


def ssd_buffers(ph):
    NT = NCC + NCH
    ssd = {n: ph.sb(n, [P, NT, 2 * HEADS]) for n in ("dt", "a")}
    ssd.update({n: ph.sb(n, [P, NT, 2, HEADS]) for n in ("edge", "tail", "whole")})
    ssd.update(ident=ph.sb("ident", [P, P]), masks=ph.sb("masks", [P, 5, P]), d_row=ph.sb("d_row", [P, HEADS]))
    return ssd


def kernel(**inputs):
    import concourse.bacc as bacc
    from concourse.bass_utils import run_bass_kernel_spmd

    nc = bacc.Bacc("TRN2", target_bir_lowering=False, num_devices=1)
    arrays = {f"in_{k}": v for k, v in layout(inputs).items()}
    t = {k[3:]: nc.dram_tensor(k, v.shape, mybir.dt.from_np(v.dtype), kind="ExternalInput").ap()
         for k, v in arrays.items()}
    out = nc.dram_tensor("out", [SEQ, D], F32, kind="ExternalOutput").ap()
    program(nc, t, out)
    r = run_bass_kernel_spmd(nc, [arrays], core_ids=[0])
    return np.reshape(r.results[0]["out"], (1, SEQ, D))
```

```python
from contextlib import ExitStack

import numpy as np
import concourse.bass as bass
from concourse import mybir

F32 = mybir.dt.float32
F32R = mybir.dt.float32r
ALU = mybir.AluOpType
ACT = mybir.ActivationFunctionType

P = 128
D = 1024
KT = D // P
SEQ = 2048
CTX = 256
EPS = 1e-6
CHUNK = 128
NCH = SEQ // CHUNK
NCC = CTX // CHUNK
HEADS = 16
GROUPS = 4
HPG = HEADS // GROUPS
HD = 64
NTAP = 4

NF = 2 * SEQ
N2 = 128
N1 = NF // N2
N1D = SEQ // N2
NK1 = N1 // 2 + 1
NR = N1
CB = 256
CG = 8
NG = CB // CG
FH = 64
H_EMB = 33
NBK = D // CB
NQ = NG // 4
NC = NG // 16
IM0, IM16 = NR, NR + 1
NPL = NR + 2


def plane(k1, part):
    if part == 0:
        return k1
    return {0: IM0, N1 // 2: IM16}.get(k1, N1 // 2 + k1)


def banks(ph, n):
    return [ph.ps(f"bank{i}", [P, 512]) for i in range(n)]


class Phase:

    def __init__(self, nc, tag, ctx):
        self.nc, self.tag, self.ctx, self.used = nc, tag, ctx, []
        ctx.callback(self.release)

    def release(self):
        if self.used:
            self.nc.clear_and_free_semaphores(self.used)
            self.nc.all_engine_barrier()

    def sb(self, name, shape, dt=F32):
        return self.ctx.enter_context(self.nc.sbuf_tensor(f"{self.tag}_{name}", shape, dt))

    def ps(self, name, shape, dt=F32):
        return self.ctx.enter_context(self.nc.psum_tensor(f"{self.tag}_{name}", shape, dt))

    def sem(self, name):
        self.used.append(self.nc.alloc_semaphore(f"{self.tag}_{name}"))
        return self.used[-1]

    def sems(self, name, n):
        return [self.sem(f"{name}{i}") for i in range(n)]


def phase_modulation(nc, t, keep, hid_s):
    with ExitStack() as ctx:
        ph = Phase(nc, "ada", ctx)
        c_sb = ph.sb("c", [P, KT, 2])
        sc = ph.sb("silu", [P, KT, 2])
        sc_rep = ph.sb("silu_rep", [P, KT, P])
        aw = ph.sb("w", [P, 3, KT, D])
        gate_b = ph.sb("gate_bias", [P, D])
        one = ph.sb("scale1", [P, KT, 2])
        cols = ph.ps("cols", [P, 16, 2])
        gps = ph.ps("gate", [P, 2, 512])
        s_in, s_aw, s_silu, s_rep = ph.sem("in"), ph.sems("w", 3), ph.sem("silu"), ph.sem("rep")
        s_mm, s_dve = ph.sem("mm"), ph.sem("dve")
        NB = SEQ // 512
        MAGIC = 12582912.0
        TURN = (6.28125, 0.00193500518798828125, 2 * np.pi - 6.28125 - 0.00193500518798828125)
        feats = ph.sb("feats", [H_EMB, SEQ])
        w1, w2, w3 = ph.sb("w1", [H_EMB, 2, FH]), ph.sb("w2", [FH, 2, FH]), ph.sb("w3", [FH, 2, FH])
        pm = ph.sb("pm", [P, 4])
        arg, turn, hid = ph.sb("arg", [P, SEQ]), ph.sb("turn", [P, SEQ]), ph.sb("hid", [P, SEQ])
        z = ph.ps("z", [P, NB, 512])
        s_mlp, s_z, s_arg = ph.sem("mlp"), ph.sem("z_done"), ph.sem("arg_done")
        s_hid, s_st = ph.sem("hid_done"), ph.sem("st")
        aw_v = t["ada_w"].rearrange("(p k) n -> p k n", k=KT)
        block = ctx.enter_context(nc.Block())

        @block.sync
        def _(sp):
            sp.dma_start(feats[:], t["feats"]).then_inc(s_mlp, 16)
            for r in range(2):
                for dst, name in ((w1, "h_w1"), (w2, "h_w2"), (w3, "h_w3")):
                    sp.dma_start(dst[:, r, :], t[name]).then_inc(s_mlp, 16)
                sp.dma_start(pm[r * FH:(r + 1) * FH, :], t["h_pm"]).then_inc(s_mlp, 16)
            sp.dma_start(c_sb[:], t["c_cols"]).then_inc(s_in, 16)
            sp.dma_start(keep["par"][:], t["par"]).then_inc(s_in, 16)
            sp.dma_start(gate_b[:], t["gate_bias"].to_broadcast([P, D])).then_inc(s_in, 16)
            for n in range(3):
                sp.dma_start(aw[:, n], aw_v[:, :, n * D:(n + 1) * D]).then_inc(s_aw[n], 16)

        @block.scalar
        def _(act):
            act.wait_ge(s_in, 48)
            nc.scalar.activation(sc[:], c_sb[:], ACT.Silu).then_inc(s_silu, 1)
            for layer in range(3):
                act.wait_ge(s_arg, 7 * layer + 7)
                nc.scalar.activation(hid[:], arg[:], ACT.Sin).then_inc(s_hid, 1)
            act.wait_ge(s_hid, 3)
            act.dma_start(hid_s, hid[:]).then_inc(s_st, 16)
            act.wait_ge(s_st, 16)

        @block.tensor
        def _(pe):
            def layer(n, w, src):
                if n:
                    pe.wait_ge(s_hid, n)
                for b in range(NB):
                    mm = pe.matmul(z[:, b, :], w[:].rearrange("p r h -> p (r h)"),
                                   src[0:w.shape[0], b * 512:(b + 1) * 512], start=True, stop=True)
                mm.then_inc(s_z, 1)

            pe.wait_ge(s_mlp, 144)
            layer(0, w1, feats)
            pe.wait_ge(s_silu, 1)
            for n in range(2):
                layer(n + 1, (w2, w3)[n], hid)
                pe.wait_ge(s_aw[n], 16)
                for m in range(KT):
                    for k in range(KT):
                        mm = pe.matmul(cols[:, n * KT + m, :], aw[:, n, k, m * P:(m + 1) * P],
                                       sc[:, k, :], start=(k == 0), stop=(k == KT - 1))
                mm.then_inc(s_mm, 1)
            pe.wait_ge(s_aw[2], 16)
            pe.wait_ge(s_rep, 1)
            for h in range(2):
                for k in range(KT):
                    mm = pe.matmul(gps[:, h, :], sc_rep[:, k, :], aw[:, 2, k, h * 512:(h + 1) * 512],
                                   start=(k == 0), stop=(k == KT - 1))
            mm.then_inc(s_mm, 1)

        @block.vector
        def _(dve):
            n = [0]

            def step(ins):
                n[0] += 1
                ins.then_inc(s_arg, 1)
                dve.wait_ge(s_arg, n[0])

            dve.wait_ge(s_mlp, 144)
            for layer in range(3):
                dve.wait_ge(s_z, layer + 1)
                step(nc.vector.tensor_scalar(arg[:], z[:].rearrange("p a n -> p (a n)"), pm[:, layer:layer + 1],
                                             pm[:, 3:4], ALU.add, ALU.mult))
                step(nc.vector.tensor_scalar(turn[:], arg[:], float(1 / (2 * np.pi)), MAGIC, ALU.mult, ALU.add))
                step(nc.vector.tensor_scalar(turn[:], turn[:], MAGIC, None, ALU.subtract))
                for c in TURN:
                    step(nc.vector.scalar_tensor_tensor(out=arg[:], in0=turn[:], scalar=float(-c), in1=arg[:],
                                                        op0=ALU.mult, op1=ALU.add))
                step(nc.vector.tensor_scalar(arg[:], arg[:], 3.1415925, -3.1415925, ALU.min, ALU.max))
            dve.wait_ge(s_silu, 1)
            nc.vector.tensor_copy(sc_rep[:], sc[:, :, 0:1].to_broadcast([P, KT, P])).then_inc(s_rep, 1)
            dve.wait_ge(s_mm, 2)
            par = keep["par"]
            for v in range(2):
                nc.vector.tensor_tensor(keep["mod"][:, v, 1, :], cols[:, 0:KT, v],
                                        par[:, PAR["shift_b"]:PAR["shift_b"] + KT], ALU.add).then_inc(s_dve, 1)
                nc.vector.tensor_tensor(one[:, :, v], cols[:, KT:2 * KT, v],
                                        par[:, PAR["scale_b"]:PAR["scale_b"] + KT], ALU.add).then_inc(s_dve, 1)
                dve.wait_ge(s_dve, 2 + 3 * v)
                nc.vector.scalar_tensor_tensor(out=keep["mod"][:, v, 0, :], in0=one[:, :, v], scalar=1.0,
                                               in1=par[:, PAR["norm_w"]:PAR["norm_w"] + KT],
                                               op0=ALU.add, op1=ALU.mult).then_inc(s_dve, 1)
            dve.wait_ge(s_mm, 3)
            nc.vector.tensor_tensor(keep["gate"][:], gps[:].rearrange("p a n -> p (a n)"), gate_b[:], ALU.add)


def phase_norm(nc, tag, xT, T, scale, shift, h_hi, h_lo):
    BW = min(512, T)
    NB = T // BW
    with ExitStack() as ctx:
        ph = Phase(nc, tag, ctx)
        x = ph.sb("x", [P, 2, KT, BW])
        sq = ph.sb("sq", [P, 2, BW])
        ms = ph.sb("ms", [P, 2, BW])
        rstd = ph.sb("rstd", [P, 2, BW])
        xn = ph.sb("xn", [P, 2, BW])
        ones = ph.sb("ones", [P, P])
        ssq = ph.ps("ssq", [P, 2, 512])
        s_one, s_x, s_sq, s_mm = ph.sem("one"), [ph.sems(f"x{b}", 2) for b in range(2)], ph.sem("sq"), ph.sem("mm")
        s_ms, s_root, s_rstd, s_xn = ph.sem("ms"), ph.sem("root"), ph.sem("rstd"), ph.sem("xn")
        s_hi, s_lo = ph.sem("hi"), ph.sem("lo")
        xv = xT.rearrange("(k p) t -> p k t", p=P)
        HK = KT // 2
        block = ctx.enter_context(nc.Block())

        @block.sync
        def _(sp):
            for b in range(NB):
                if b >= 2:
                    sp.wait_ge(s_xn, KT * (b - 1))
                for n in range(2):
                    sp.dma_start(x[:, b % 2, n * HK:(n + 1) * HK], xv[:, n * HK:(n + 1) * HK, b * BW:(b + 1) * BW]
                                 ).then_inc(s_x[b % 2][n], 16)

        @block.scalar
        def _(act):
            def square(n):
                b, k = n // KT, n % KT
                act.wait_ge(s_x[b % 2][k // HK], 16 * (b // 2 + 1))
                if n >= 2:
                    act.wait_ge(s_mm, n - 1)
                nc.scalar.activation(sq[:, n % 2, :], x[:, b % 2, k, :], ACT.Square).then_inc(s_sq, 1)

            def root(b):
                act.wait_ge(s_ms, b + 1)
                if b >= 2:
                    act.wait_ge(s_xn, KT * (b - 1))
                nc.scalar.activation(rstd[:, b % 2, :], ms[:, b % 2, :], ACT.Sqrt).then_inc(s_root, 1)

            for k in range(KT):
                square(k)
            root(0)
            for b in range(NB):
                for k in range(KT):
                    n = b * KT + k
                    if b + 1 < NB:
                        square(n + KT)
                    act.wait_ge(s_xn, n + 1)
                    nc.scalar.activation(h_hi[:, k, b * BW:(b + 1) * BW], xn[:, n % 2, :], ACT.Identity,
                                         bias=shift[:, k:k + 1]).then_inc(s_hi, 1)
                if b + 1 < NB:
                    root(b + 1)

        @block.tensor
        def _(pe):
            pe.wait_ge(s_one, 1)
            for b in range(NB):
                if b >= 2:
                    pe.wait_ge(s_ms, b - 1)
                for k in range(KT):
                    n = b * KT + k
                    pe.wait_ge(s_sq, n + 1)
                    pe.matmul(ssq[:, b % 2, 0:BW], ones[:], sq[:, n % 2, :], start=(k == 0),
                              stop=(k == KT - 1)).then_inc(s_mm, 1)

        @block.vector
        def _(dve):
            nc.vector.memset(ones[:], 1.0).then_inc(s_one, 1)

            def low(n):
                b, k = n // KT, n % KT
                dve.wait_ge(s_hi, n + 1)
                nc.vector.scalar_tensor_tensor(out=h_lo[:, k, b * BW:(b + 1) * BW], in0=xn[:, n % 2, :],
                                               scalar=shift[:, k:k + 1],
                                               in1=h_hi[:, k, b * BW:(b + 1) * BW].bitcast(F32), op0=ALU.add,
                                               op1=ALU.subtract).then_inc(s_lo, 1)

            for b in range(NB):
                dve.wait_ge(s_mm, KT * (b + 1))
                if b >= 2:
                    dve.wait_ge(s_root, b - 1)
                nc.vector.tensor_scalar(ms[:, b % 2, :], ssq[:, b % 2, 0:BW], 1.0 / D, EPS, ALU.mult,
                                        ALU.add).then_inc(s_ms, 1)
                dve.wait_ge(s_root, b + 1)
                nc.vector.reciprocal(rstd[:, b % 2, :], rstd[:, b % 2, :]).then_inc(s_rstd, 1)
                dve.wait_ge(s_rstd, b + 1)
                for k in range(KT):
                    n = b * KT + k
                    if n >= 2:
                        dve.wait_ge(s_lo, n - 1)
                    nc.vector.scalar_tensor_tensor(out=xn[:, n % 2, :], in0=x[:, b % 2, k, :],
                                                   scalar=scale[:, k:k + 1], in1=rstd[:, b % 2, :],
                                                   op0=ALU.mult, op1=ALU.mult).then_inc(s_xn, 1)
                    if k > 0:
                        low(n - 1)
                dve.wait_ge(s_xn, KT * (b + 1))
                low(b * KT + KT - 1)


def phase_in_projection(nc, tag, w_rec, taps_d, groups, T, h_hi, h_lo):
    BW = min(512, T)
    NB = T // BW
    FUNC = {"silu": ACT.Silu, "sigmoid": ACT.Sigmoid, "raw": ACT.Copy}
    with ExitStack() as ctx:
        ph = Phase(nc, tag, ctx)
        w = ph.sb("w", [P, 2, D])
        conv_taps = ph.sb("taps", [P, N_CONV * NTAP])
        w_hi = ph.sb("w_hi", [P, 2, D], F32R)
        w_lo = ph.sb("w_lo", [P, 2, D], F32R)
        zero = ph.sb("zero", [P, 1])
        raw = ph.sb("raw", [P, 2, T + 2])
        acc = ph.sb("acc", [P, T])
        res = ph.sb("res", [P, 2, T])
        bank = [ph.ps(f"bank{b}", [P, 512]) for b in range(NB)]
        s_w, s_hi, s_lo, s_mm = ph.sems("w", 2), ph.sem("hi"), ph.sem("lo"), ph.sem("mm")
        s_ev, s_tap, s_conv = ph.sem("ev"), ph.sem("tap"), ph.sem("conv")
        s_res, s_st, s_pad, s_edge = ph.sem("res"), ph.sems("st", 2), ph.sem("pad"), ph.sem("edge")
        s_taps = ph.sem("taps_in")
        block = ctx.enter_context(nc.Block())

        def tiles(eng, body):
            done = convs = 0
            for g in groups:
                has_conv = g[2] in ("conv", "conv_silu")
                if g[1] > 1:
                    with eng.Fori(0, g[1] // 2) as i:
                        for j in range(2):
                            body(2 * i + (done + j), (done + j) % 2, i + (done + j) // 2, 2 * i + j,
                                 2 * i + (convs + j), g)
                else:
                    body(done, done % 2, done // 2, 0, convs, g)
                done += g[1]
                convs += g[1] * has_conv
            return done

        @block.sync
        def _(sp):
            sp.dma_start(conv_taps[:], taps_d).then_inc(s_taps, 16)

            def body(n, q, half, local, taps, g):
                sp.wait_ge(s_lo, n + 1)
                sp.dma_start(w[:, q], w_rec[bass.ds(local + g[0], 1)].rearrange("a p m -> p (a m)")
                             ).then_inc(s_w[q], 16)
            tiles(sp, body)

        @block.gpsimd
        def _(pool):
            nc.gpsimd.memset(zero[:], 0.0).then_inc(s_pad, 1)
            pool.wait_ge(s_pad, 1)
            pool.nop().then_inc(s_lo, 2)

            def body(n, q, half, local, taps, g):
                pool.wait_ge(s_w[q], 16 * half + 16)
                pool.wait_ge(s_mm, NB * n + NB)
                nc.gpsimd.tensor_tensor(w_hi[:, q, :], w[:, q, 0:D], zero[:].to_broadcast([P, D]),
                                        ALU.add).then_inc(s_hi, 1)
                pool.wait_ge(s_hi, n + 1)
                nc.gpsimd.tensor_tensor(w_lo[:, q, :], w[:, q, 0:D], w_hi[:, q, :].bitcast(F32),
                                        ALU.subtract).then_inc(s_lo, 1)
            tiles(pool, body)

        @block.tensor
        def _(pe):
            pe.nop().then_inc(s_mm, 2 * NB)

            def body(n, q, half, local, taps, g):
                pe.wait_ge(s_lo, n + 3)
                for b in range(NB):
                    pe.wait_ge(s_ev, NB * n + (b + 1))
                    for k in range(KT):
                        m, r = slice(k * P, (k + 1) * P), slice(b * BW, (b + 1) * BW)
                        out = bank[b][:, 0:BW]
                        pe.matmul(out, w_hi[:, q, m], h_hi[:, k, r], start=(k == 0), stop=False)
                        pe.matmul(out, w_hi[:, q, m], h_lo[:, k, r], start=False, stop=False)
                        mm = pe.matmul(out, w_lo[:, q, m], h_hi[:, k, r], start=False, stop=(k == KT - 1))
                    mm.then_inc(s_mm, 1)
            tiles(pe, body)

        @block.scalar
        def _(act):
            for q in range(2):
                act.nop().then_inc(s_st[q], 16)
            act.nop().then_inc(s_ev, NB)

            def body(n, q, half, local, taps, g):
                conv = g[2] in ("conv", "conv_silu")
                if conv:
                    act.wait_ge(s_conv, n + 1)
                else:
                    act.wait_ge(s_st[q], 16 * half + 16)
                for b in range(NB):
                    act.wait_ge(s_mm, NB * n + (2 * NB + b + 1))
                    if conv:
                        dst, func = raw[:, q, 1 + b * BW:1 + (b + 1) * BW], ACT.Copy
                    else:
                        dst, func = res[:, q, b * BW:(b + 1) * BW], FUNC[g[2]]
                    nc.scalar.activation(dst, bank[b][:, 0:BW], func).then_inc(s_ev, 1)
                if g[2] == "conv_silu":
                    act.wait_ge(s_conv, n + 3)
                    act.wait_ge(s_st[q], 16 * half + 16)
                    nc.scalar.activation(res[:, q, :], acc[:], ACT.Silu).then_inc(s_res, 1)
                    act.wait_ge(s_res, n + 2)
                elif conv:
                    act.wait_ge(s_res, n + 2)
                else:
                    act.wait_ge(s_ev, NB * n + 2 * NB)
                    act.nop().then_inc(s_res, 1)
                act.dma_start(g[3][bass.ds(local * P, P), :], res[:, q, :]).then_inc(s_st[q], 16)
            total = tiles(act, body)
            for q in range(2):
                act.wait_ge(s_st[q], 16 * ((total + 1 - q) // 2 + 1))

        @block.vector
        def _(dve):
            dve.nop().then_inc(s_conv, 2)
            dve.nop().then_inc(s_res, 1)
            for q in range(2):
                nc.vector.memset(raw[:, q, 0:1], 0.0).then_inc(s_edge, 1)
                nc.vector.memset(raw[:, q, T + 1:T + 2], 0.0).then_inc(s_edge, 1)
            dve.wait_ge(s_edge, 4)
            dve.wait_ge(s_taps, 16)

            def body(n, q, half, local, taps, g):
                if g[2] not in ("conv", "conv_silu"):
                    dve.wait_ge(s_conv, n + 2)
                    dve.nop().then_inc(s_conv, 1)
                    return
                dve.wait_ge(s_ev, NB * n + 2 * NB)
                dve.wait_ge(s_res, n + 1)
                at = local * NTAP + g[4] * NTAP
                w0, w1, w2, bias = (conv_taps[:, bass.ds(at + j, 1)] for j in range(NTAP))
                nc.vector.tensor_scalar(acc[:], raw[:, q, 1:T + 1], w1, bias, ALU.mult, ALU.add).then_inc(s_tap, 1)
                dve.wait_ge(s_tap, 2 * taps + 1)
                nc.vector.scalar_tensor_tensor(out=acc[:], in0=raw[:, q, 0:T], scalar=w0, in1=acc[:],
                                               op0=ALU.mult, op1=ALU.add).then_inc(s_tap, 1)
                dve.wait_ge(s_tap, 2 * taps + 2)
                if g[2] == "conv_silu":
                    nc.vector.scalar_tensor_tensor(out=acc[:], in0=raw[:, q, 2:T + 2], scalar=w2, in1=acc[:],
                                                   op0=ALU.mult, op1=ALU.add).then_inc(s_conv, 1)
                else:
                    dve.wait_ge(s_st[q], 16 * half + 16)
                    nc.vector.scalar_tensor_tensor(out=res[:, q, :], in0=raw[:, q, 2:T + 2], scalar=w2,
                                                   in1=acc[:], op0=ALU.mult, op1=ALU.add).then_inc(s_res, 1)
                    dve.wait_ge(s_res, n + 2)
                    dve.nop().then_inc(s_conv, 1)
            tiles(dve, body)


def phase_filter_taps(nc, t, keep, tables, hid_s, taps_s):
    NB = SEQ // 512
    with ExitStack() as ctx:
        ph = Phase(nc, "taps", ctx)
        hid = ph.sb("hid", [P, SEQ])
        hid_hi, hid_lo = ph.sb("hid_hi", [P, SEQ], F32R), ph.sb("hid_lo", [FH, SEQ], F32R)
        trow = ph.sb("trow", [P, SEQ])
        window = ph.sb("window", [P, 2, SEQ])
        wo = ph.sb("wo", [P, 2, 4, P])
        wc = ph.sb("wc", [P, 4, P])
        ws = ph.sb("ws", [P, 2, 4, P], F32R)
        zero = ph.sb("zero", [P, 1])
        res = ph.sb("res", [P, 2, SEQ])
        ps = [ph.ps(f"ps{i}", [P, 4, 512]) for i in range(2)]
        s_in, s_hid = ph.sem("in"), ph.sem("hid_in")
        s_wo, s_wc, s_win = ph.sems("wo", 2), ph.sem("wc"), ph.sem("win")
        s_tab = ph.sem("tab")
        s_zero, s_whi, s_ws, s_split = ph.sem("zero"), ph.sem("whi"), ph.sem("ws"), ph.sem("split")
        s_tm, s_res, s_fix, s_st = ph.sem("tm"), ph.sem("res"), ph.sem("fix"), ph.sems("st", 2)
        wo_v = t["h_w_out"].rearrange("h (q c) -> h q c", q=4)
        out_v = taps_s.rearrange("(o w s c) n -> o w s c n", o=2, w=NBK, s=2)
        block = ctx.enter_context(nc.Block())

        def tiles(eng):
            for blk in range(NBK):
                with eng.Fori(0, KT // NBK // 2) as i:
                    for j in range(2):
                        yield i, j, 2 * i + (KT // NBK * blk + j), i + KT // NBK // 2 * blk, blk

        @block.sync
        def _(sp):
            sp.dma_start(hid[:], hid_s).then_inc(s_hid, 16)
            sp.dma_start(trow[:], t["trow"].to_broadcast([P, SEQ])).then_inc(s_in, 16)
            for i, j, m, half, blk in tiles(sp):
                sp.wait_ge(s_wc, 4 * m + 1)
                for r in range(2):
                    sp.dma_start(wo[r * FH:(r + 1) * FH, j], wo_v[:, :, bass.ds(m * P, P)]).then_inc(s_wo[j], 16)

        @block.gpsimd
        def _(pool):
            nc.gpsimd.memset(zero[:], 0.0).then_inc(s_zero, 1)
            pool.wait_ge(s_zero, 1)
            pool.nop().then_inc(s_wc, 5)
            for i, j, m, half, blk in tiles(pool):
                pool.wait_ge(s_wo[j], 32 * half + 32)
                for o in range(2):
                    for s, op in enumerate((ALU.add, ALU.subtract)):
                        nc.gpsimd.tensor_tensor(wc[:, 2 * o + s, :], wo[:, j, o, :], wo[:, j, 2 + o, :],
                                                op).then_inc(s_wc, 1)
                pool.wait_ge(s_wc, 4 * m + 9)
                pool.wait_ge(s_tm, 4 * m + 4)
                nc.gpsimd.tensor_tensor(ws[:, j], wc[:], zero[:, :, None].to_broadcast([P, 4, P]),
                                        ALU.add).then_inc(s_whi, 1)
                pool.wait_ge(s_whi, m + 1)
                nc.gpsimd.tensor_tensor(ws[FH:P, j], wc[FH:P], ws[FH:P, j].bitcast(F32), ALU.subtract).then_inc(s_ws, 1)
                pool.wait_ge(s_ws, m + 1)

        @block.scalar
        def _(act):
            act.wait_ge(s_hid, 16)
            nc.scalar.activation(hid_hi[:], hid[:], ACT.Copy).then_inc(s_split, 1)
            for name, dst in tables.items():
                act.dma_start(dst[:], t[name]).then_inc(s_tab, 16)
            for j in range(2):
                act.nop().then_inc(s_st[j], 16)
            act.wait_ge(s_in, 16)
            for i, j, m, half, blk in tiles(act):
                act.wait_ge(s_res, 4 * m + 5)
                nc.scalar.activation(window[:, j, :], trow[:], ACT.Exp,
                                     scale=keep["par"][:, bass.ds(m + PAR["delta"], 1)]).then_inc(s_win, 1)
                for q in range(4):
                    act.wait_ge(s_res, 4 * m + q + 10)
                    if q % 2 == 0:
                        act.wait_ge(s_fix, 2 * m + q // 2 + 1)
                    act.dma_start(out_v[q // 2, blk, q % 2, bass.ds((2 * i + j) * P, P), :], res[:, q % 2, :]
                                  ).then_inc(s_st[q % 2], 16)
            for j in range(2):
                act.wait_ge(s_st[j], 16 * (2 * KT + 1))
            act.wait_ge(s_tab, 16 * len(tables))

        @block.tensor
        def _(pe):
            pe.wait_ge(s_split, 2)
            pe.nop().then_inc(s_tm, 8)
            for i, j, m, half, blk in tiles(pe):
                pe.wait_ge(s_ws, m + 1)
                for q in range(4):
                    pe.wait_ge(s_res, 4 * m + q + 8)
                    for b in range(NB):
                        r = slice(b * 512, (b + 1) * 512)
                        pe.matmul(ps[q % 2][:, b, :], ws[:, j, q, :], hid_hi[:, r], start=True, stop=False)
                        mm = pe.matmul(ps[q % 2][:, b, :], ws[0:FH, j, q, :], hid_lo[:, r], start=False, stop=True)
                    mm.then_inc(s_tm, 1)

        @block.vector
        def _(dve):
            dve.wait_ge(s_hid, 16)
            dve.wait_ge(s_split, 1)
            nc.vector.tensor_tensor(hid_lo[:], hid[0:FH], hid_hi[0:FH].bitcast(F32), ALU.subtract).then_inc(s_split, 1)
            dve.nop().then_inc(s_res, 9)
            for i, j, m, half, blk in tiles(dve):
                dve.wait_ge(s_win, m + 1)
                for q in range(4):
                    dve.wait_ge(s_tm, 4 * m + q + 9)
                    dve.wait_ge(s_st[q % 2], 32 * m + 16 * (q // 2) + 16)
                    nc.vector.tensor_tensor(res[:, q % 2, :], ps[q % 2][:].rearrange("p a n -> p (a n)"),
                                            window[:, j, :], ALU.mult).then_inc(s_res, 1)
                    if q % 2 == 0:
                        dve.wait_ge(s_res, 4 * m + q + 10)
                        nc.vector.tensor_tensor(res[:, 0, 0:1], res[:, 0, 0:1],
                                                keep["par"][:, bass.ds(m + (PAR["h_bias"] + KT * (q // 2)), 1)],
                                                ALU.add).then_inc(s_fix, 1)


def phase_filter_spectra(nc, tables, taps_s, spec_s):
    NP = NG // 2
    with ExitStack() as ctx:
        ph = Phase(nc, "spec", ctx)
        f1, tw = tables["f1"], tables["tw_fwd"]
        xin = ph.sb("xin", [P, 2, 16, N2])
        y = ph.sb("y", [P, NR, CB])
        res = ph.sb("res", [P, 4, CB])
        bank = banks(ph, 8)
        s_ld, s_first, s_ev = ph.sems("ld", 2), ph.sem("first"), ph.sems("ev", 2)
        s_second, s_res, s_st = ph.sem("second"), ph.sem("res"), ph.sems("st", 4)
        src = taps_s.rearrange("r (a n) -> (r a) n", n=N2).rearrange("(w g p) n -> w p g n", g=NG, p=P)
        dst = spec_s.rearrange("(w k p) (a n) -> w k p a n", k=NK1, p=P, a=2)
        stores = [len(range(r, NK1, 4)) for r in range(4)]
        block = ctx.enter_context(nc.Block())

        @block.sync
        def _(sp):
            with sp.Fori(0, 2 * NBK) as i:
                for part in range(2):
                    for c in range(NC):
                        sp.wait_ge(s_first, 2 * NP * i + (NP * part + 8 * c + 8))
                        for e in range(2):
                            sp.dma_start(xin[:, c % 2, 8 * e:8 * e + 8], src[bass.ds(2 * i + part, 1), :,
                                         16 * c + 8 * e:16 * c + 8 * e + 8, :].rearrange("w p g n -> p (w g) n")
                                         ).then_inc(s_ld[c % 2], 16)

        @block.tensor
        def _(pe):
            pe.nop().then_inc(s_first, 16)
            with pe.Fori(0, 2 * NBK) as i:
                for part in range(2):
                    for p in range(NP):
                        c = p // 8
                        if p % 8 == 0:
                            pe.wait_ge(s_ld[c % 2], 32 * NC * i + 32 * (NC // 2 * part + c // 2 + 1))
                        pe.wait_ge(s_ev[p % 2], NP * i + (NP // 2 * part + p // 2 + 1))
                        for g in range(2):
                            mm = pe.matmul(bank[p % 4][:, g * 256:(g + 1) * 256], xin[:, c % 2, (2 * p + g) % 16, :],
                                           f1[:], start=True, stop=True)
                        mm.then_inc(s_first, 1)
                    for e in range(2):
                        pe.wait_ge(s_ev[e], NP * i + (NP // 2 * (part + 1) + 2))
                    for k in range(NK1):
                        n = NK1 * part + k
                        pe.wait_ge(s_res, 2 * NK1 * i + (n + (1 if k >= 4 else 4)))
                        pairs = [((0, 2)[part], plane(k, 0))]
                        if 0 < k < NK1 - 1:
                            pairs.append(((1, 0)[part], plane(k, 1)))
                        for a, (m, pl) in enumerate(pairs):
                            mm = pe.matmul(bank[4 + k % 4][:, 0:CB], tw[:, k, m, :], y[:, pl, :], start=(a == 0),
                                           stop=(a == len(pairs) - 1))
                        mm.then_inc(s_second, 1)

        def take(eng_op, p):
            return eng_op(y[:, :, 16 * p:16 * (p + 1)].rearrange("p r (g c) -> p r g c", g=2),
                          bank[p % 4][:].rearrange("p (g r c) -> p r g c", g=2, c=CG))

        @block.scalar
        def _(act):
            act.nop().then_inc(s_ev[0], 2)
            act.nop().then_inc(s_res, 4)
            for r in range(4):
                act.nop().then_inc(s_st[r], 16)
            with act.Fori(0, 2 * NBK) as i:
                for part in range(2):
                    for p in range(0, NP, 2):
                        act.wait_ge(s_first, 2 * NP * i + (NP * part + p + 17))
                        take(nc.scalar.copy, p).then_inc(s_ev[0], 1)
                    for k in range(NK1):
                        n = NK1 * part + k
                        r = k % 4
                        act.wait_ge(s_second, 2 * NK1 * i + (n + 1))
                        act.wait_ge(s_st[r], 32 * stores[r] * i + 16 * (stores[r] * part + k // 4 + 1))
                        nc.scalar.copy(res[:, r, :], bank[4 + r][:, 0:CB]).then_inc(s_res, 1)
                        act.wait_ge(s_res, 2 * NK1 * i + (n + 5))
                        act.dma_start(dst[bass.ds(i, 1), k, :, part, :].rearrange("w p n -> p (w n)"),
                                      res[:, r, :]).then_inc(s_st[r], 16)
            for r in range(4):
                act.wait_ge(s_st[r], 16 * (2 * 2 * NBK * stores[r] + 1))

        @block.vector
        def _(dve):
            dve.nop().then_inc(s_ev[1], 2)
            with dve.Fori(0, 2 * NBK) as i:
                for part in range(2):
                    for p in range(1, NP, 2):
                        dve.wait_ge(s_first, 2 * NP * i + (NP * part + p + 17))
                        take(nc.vector.tensor_copy, p).then_inc(s_ev[1], 1)


def phase_long_conv(nc, tag, tables, src_s, gate_s, dst_s, spec_s, order):
    NP, TP = NG // 2, NK1 * 2
    with ExitStack() as ctx:
        ph = Phase(nc, tag, ctx)
        f1, tw, tw_inv, back, ident = (tables[n] for n in ("f1", "tw_fwd", "tw_inv", "back", "ident"))
        xin = ph.sb("xin", [P, 2, 16, N2])
        gin = ph.sb("gin", [P, 2, 16, N2])
        res = ph.sb("res", [P, 2, 16, N2])
        y = ph.sb("y", [P, NPL, CB])
        spec = ph.sb("spec", [P, 2, 2, CB])
        prod = ph.sb("prod", [P, 2, 4, CB])
        w = ph.sb("w", [P, CB, NR])
        turned = ph.sb("turned", [P, 2, 2, 4 * N2])
        bank = banks(ph, 8)
        s_ld, s_gl, s_k = ph.sems("ld", 2), ph.sems("gl", 2), ph.sems("k", 2)
        s_first, s_ev, s_u, s_prod, s_z = ph.sem("first"), ph.sems("ev", 2), ph.sem("u"), ph.sem("prod"), ph.sem("z")
        s_w, s_we, s_turn, s_te = ph.sem("w"), ph.sem("we"), ph.sem("turn"), ph.sems("te", 2)
        s_back, s_gate, s_st = ph.sem("back"), ph.sem("gate"), ph.sems("st", 2)

        def samples(s):
            return s.rearrange("r (a n) -> (r a) n", n=N2).rearrange("(w g p) n -> w p g n", g=NG, p=P)

        src, gate, dst = samples(src_s), samples(gate_s), samples(dst_s)
        spec_v = spec_s.rearrange("(w k p) n -> w k p n", k=NK1, p=P)
        NKQ = (len(range(0, NK1, 2)), len(range(1, NK1, 2)))
        block = ctx.enter_context(nc.Block())

        @block.sync
        def _(sp):
            with sp.Fori(0, NBK) as i:
                def chunk(buf, view, c, sem):
                    for e in range(2):
                        sp.dma_start(buf[:, c % 2, 8 * e:8 * e + 8], view[bass.ds(i, 1), :,
                                     16 * c + 8 * e:16 * c + 8 * e + 8, :].rearrange("w p g n -> p (w g) n")
                                     ).then_inc(sem[c % 2], 16)

                for c in range(NC):
                    sp.wait_ge(s_first, NP * i + (8 * c + 8))
                    chunk(xin, src, c, s_ld)
                for k in range(NK1):
                    sp.wait_ge(s_prod, TP * i + (2 * k if k >= 2 else 2))
                    sp.dma_start(spec[:, k % 2], spec_v[bass.ds(i + order * NBK, 1), k]
                                 .rearrange("w p (a n) -> p (w a) n", a=2)).then_inc(s_k[k % 2], 16)
                    if k in (2, 3):
                        sp.wait_ge(s_gate, NQ * i + (4 * (k - 2) + 4))
                        chunk(gin, gate, k - 2, s_gl)
                for c in range(2, NC):
                    sp.wait_ge(s_gate, NQ * i + (4 * c + 4))
                    chunk(gin, gate, c, s_gl)

        @block.tensor
        def _(pe):
            pe.nop().then_inc(s_first, 16)
            with pe.Fori(0, NBK) as i:
                def forward(k):
                    if k >= 2:
                        pe.wait_ge(s_prod, TP * i + 2 * k)
                    ends = k in (0, NK1 - 1)
                    for part, mats in enumerate(((0, 1), (2, 0))):
                        out = bank[k % 2][:, part * CB:(part + 1) * CB]
                        mm = pe.matmul(out, tw[:, k, mats[0], :], y[:, plane(k, 0), :], start=True, stop=ends)
                        if not ends:
                            mm = pe.matmul(out, tw[:, k, mats[1], :], y[:, plane(k, 1), :], start=False, stop=True)
                    mm.then_inc(s_u, 1)

                def inverse(k):
                    pe.wait_ge(s_z, 2 * NK1 * i + (2 * k + 4))
                    if k == 0:
                        pe.wait_ge(s_gate, NQ * i + 8)
                    if k >= 2:
                        pe.wait_ge(s_we, NK1 * i + (k - 1))
                    for part, mats in enumerate(((0, 2), (1, 0))):
                        if part and k in (0, NK1 - 1):
                            continue
                        out = bank[4 + k % 2][:, part * CB:(part + 1) * CB]
                        pe.matmul(out, tw_inv[:, k, mats[0], :], y[:, plane(k, 0), :], start=True, stop=False)
                        mm = pe.matmul(out, tw_inv[:, k, mats[1], :], y[:, plane(k, 1), :], start=False, stop=True)
                    mm.then_inc(s_w, 1)

                def turn(q):
                    if q >= 2:
                        for h in range(2):
                            pe.wait_ge(s_te[h], NQ * i + (q - 1))
                    for h in range(2):
                        for g in range(4):
                            ch = 32 * q + CG * g + 4 * h
                            mm = pe.transpose(bank[2 * (q % 2) + h][:, g * P:(g + 1) * P],
                                              w[:, ch:ch + 4, :].rearrange("p c r -> p (c r)"), ident[:])
                    mm.then_inc(s_turn, 1)

                def last(q):
                    for h in range(2):
                        pe.wait_ge(s_te[h], NQ * i + (q + 1))
                    if q >= 2:
                        pe.wait_ge(s_gate, NQ * i + (q - 1 + 8))
                    out = bank[4 + q % 2][:]
                    pe.matmul(out, back[:, 0, :], turned[:, q % 2, 0, :], start=True, stop=False)
                    pe.matmul(out, back[:, 1, :], turned[:, q % 2, 1, :], start=False, stop=True).then_inc(s_back, 1)

                for p in range(NP):
                    c = p // 8
                    if p % 8 == 0:
                        pe.wait_ge(s_ld[c % 2], 16 * NC * i + (32 * (c // 2) + 32))
                    pe.wait_ge(s_ev[p % 2], NP // 2 * i + (p // 2 + 1))
                    for g in range(2):
                        mm = pe.matmul(bank[p % 4][:, g * 256:(g + 1) * 256], xin[:, c % 2, (2 * p + g) % 16, :],
                                       f1[:], start=True, stop=True)
                    mm.then_inc(s_first, 1)
                for e in range(2):
                    pe.wait_ge(s_ev[e], NP // 2 * i + (NP // 2 + 2))
                for k in range(NK1 + 1):
                    if k < NK1:
                        forward(k)
                    if k >= 1:
                        inverse(k - 1)
                pe.wait_ge(s_we, NK1 * i + NK1)
                turn(0)
                for q in range(NQ):
                    if q + 1 < NQ:
                        turn(q + 1)
                    last(q)

        def take(eng_op, p):
            return eng_op(y[:, 0:NR, 16 * p:16 * (p + 1)].rearrange("p r (g c) -> p r g c", g=2),
                          bank[p % 4][:].rearrange("p (g r c) -> p r g c", g=2, c=CG))

        @block.scalar
        def _(act):
            act.nop().then_inc(s_ev[0], 2)
            for r in range(2):
                act.nop().then_inc(s_st[r], 16)
            with act.Fori(0, NBK) as i:
                for p in range(0, NP, 2):
                    act.wait_ge(s_first, NP * i + (p + 17))
                    take(nc.scalar.copy, p).then_inc(s_ev[0], 1)
                for k in range(NK1):
                    act.wait_ge(s_w, NK1 * i + (k + 1))
                    np_ = 1 if k in (0, NK1 - 1) else 2
                    nc.scalar.copy(w[:, :, k:k + 16 * (np_ - 1) + 1:16].rearrange("p c a -> p a c"),
                                   bank[4 + k % 2][:, 0:np_ * CB].rearrange("p (a c) -> p a c", a=np_)
                                   ).then_inc(s_we, 1)

                def store(c):
                    act.wait_ge(s_gate, NQ * i + (4 * c + 4 + 8))
                    act.dma_start(dst[bass.ds(i, 1), :, 16 * c:16 * (c + 1), :].rearrange("w p g n -> p (w g) n"),
                                  res[:, c % 2]).then_inc(s_st[c % 2], 16)

                for q in range(NQ):
                    act.wait_ge(s_turn, NQ * i + (q + 1))
                    nc.scalar.copy(turned[:, q % 2, 0, :], bank[2 * (q % 2)][:]).then_inc(s_te[0], 1)
                    if q >= 5 and q % 4 == 1:
                        store(q // 4 - 1)
                store(NC - 1)
            for r in range(2):
                act.wait_ge(s_st[r], 16 * (NBK * NC // 2 + 1))

        @block.gpsimd
        def _(pool):
            pool.nop().then_inc(s_z, 2)
            with pool.Fori(0, NBK) as i:
                for k in range(NK1):
                    for part, op in enumerate((ALU.subtract, ALU.add)):
                        pool.wait_ge(s_prod, TP * i + (2 * k + 4))
                        nc.gpsimd.tensor_tensor(y[:, plane(k, part), :], prod[:, k % 2, part, :],
                                                prod[:, k % 2, 3 - part, :], op).then_inc(s_z, 1)

        @block.vector
        def _(dve):
            dve.nop().then_inc(s_ev[1], 2)
            dve.nop().then_inc(s_prod, 2)
            dve.nop().then_inc(s_gate, 8)
            with dve.Fori(0, NBK) as i:
                for p in range(1, NP, 2):
                    dve.wait_ge(s_first, NP * i + (p + 17))
                    take(nc.vector.tensor_copy, p).then_inc(s_ev[1], 1)
                for k in range(NK1):
                    dve.wait_ge(s_k[k % 2], 16 * NKQ[k % 2] * i + (16 * (k // 2) + 16))
                    dve.wait_ge(s_z, 2 * NK1 * i + (2 * (k - 1) + 2 if k >= 2 else 2))
                    dve.wait_ge(s_u, NK1 * i + (k + 1))
                    for a in range(2):
                        col = bank[k % 2][:, None, a * CB:(a + 1) * CB].to_broadcast([P, 2, CB])
                        nc.vector.tensor_tensor(prod[:, k % 2, 2 * a:2 * a + 2, :], col, spec[:, k % 2, :, :],
                                                ALU.mult).then_inc(s_prod, 1)
                for q in range(NQ + 1):
                    if q < NQ:
                        dve.wait_ge(s_turn, NQ * i + (q + 1))
                        nc.vector.tensor_copy(turned[:, q % 2, 1, :], bank[2 * (q % 2) + 1][:]).then_inc(s_te[1], 1)
                    if q >= 1:
                        r = q - 1
                        c = r // 4
                        if r % 4 == 0:
                            dve.wait_ge(s_gl[c % 2], 16 * NC * i + (32 * (c // 2) + 32))
                            dve.wait_ge(s_st[c % 2], 8 * NC * i + (16 * (c // 2) + 16))
                        dve.wait_ge(s_back, NQ * i + (r + 1))
                        at = (r % 4) * 4
                        nc.vector.tensor_tensor(res[:, c % 2, at:at + 4, :].rearrange("p g n -> p (g n)"),
                                                bank[4 + r % 2][:],
                                                gin[:, c % 2, at:at + 4, :].rearrange("p g n -> p (g n)"),
                                                ALU.mult).then_inc(s_gate, 1)


def phase_step_sizes(nc, t, dt_c, dt_s, ssd):
    NT = NCC + NCH
    H2 = 2 * HEADS
    with ExitStack() as ctx:
        ph = Phase(nc, "dt", ctx)
        raw = ph.sb("raw", [H2, NT * P])
        bias, a_neg = ph.sb("bias", [P, H2]), ph.sb("a", [P, H2])
        x, e, w, m = (ph.sb(n, [P, NT, H2]) for n in ("x", "e", "w", "m"))
        ps = ph.ps("turned", [P, 2, 512])
        sums = [ph.ps(f"sum{i}", [P, 512]) for i in range(6)]
        s_in, s_t, s_v, s_a, s_mm = ph.sem("in"), ph.sem("t"), ph.sem("v"), ph.sem("a"), ph.sem("mm")
        dt, a = ssd["dt"], ssd["a"]
        block = ctx.enter_context(nc.Block())

        @block.sync
        def _(sp):
            sp.dma_start(raw[:, 0:NCC * P], dt_c[0:H2, :]).then_inc(s_in, 16)
            sp.dma_start(raw[:, NCC * P:], dt_s[0:H2, :]).then_inc(s_in, 16)
            sp.dma_start(bias[:], t["m_dt_bias"].to_broadcast([P, H2])).then_inc(s_in, 16)
            sp.dma_start(a_neg[:], t["m_a_log"].to_broadcast([P, H2])).then_inc(s_in, 16)
            for name in ("ident", "masks", "d_row"):
                src = t[name].to_broadcast([P, HEADS]) if name == "d_row" else t[name]
                sp.dma_start(ssd[name][:], src).then_inc(s_in, 16)

        @block.tensor
        def _(pe):
            pe.wait_ge(s_in, 112)
            for c in range(NT):
                mm = pe.transpose(ps[:, c // 16, (c % 16) * H2:(c % 16 + 1) * H2], raw[:, c * P:(c + 1) * P],
                                  ssd["ident"][0:H2, 0:H2])
            mm.then_inc(s_t, 1)
            pe.wait_ge(s_v, LAST_DT)
            for i, (mask, d) in enumerate(((0, 0), (1, 0), (2, 1), (3, 1))):
                mm = pe.matmul(sums[i][:, 0:NT * HEADS], ssd["masks"][:, mask, :],
                               a[:, :, d * HEADS:(d + 1) * HEADS], start=True, stop=True)
            for d in range(2):
                mm = pe.matmul(sums[4 + d][:, 0:NT * HEADS], ssd["masks"][:, 4, :],
                               a[:, :, d * HEADS:(d + 1) * HEADS], start=True, stop=True)
            mm.then_inc(s_mm, 1)

        n_v = [0]

        @block.vector
        def _(dve):
            def step(ins):
                n_v[0] += 1
                ins.then_inc(s_v, 1)
                dve.wait_ge(s_v, n_v[0])

            dve.wait_ge(s_in, 112)
            dve.wait_ge(s_t, 1)
            bc = bias[:, None, :]
            step(nc.vector.tensor_tensor(x[:, 0:16, :], ps[:, 0, :].rearrange("p (c h) -> p c h", h=H2),
                                         bc.to_broadcast([P, 16, H2]), ALU.add))
            step(nc.vector.tensor_tensor(x[:, 16:NT, :], ps[:, 1, 0:(NT - 16) * H2].rearrange("p (c h) -> p c h", h=H2),
                                         bc.to_broadcast([P, NT - 16, H2]), ALU.add))
            step(nc.vector.tensor_scalar(w[:], x[:], -1.0, None, ALU.mult))
            step(nc.vector.tensor_tensor(w[:], w[:], x[:], ALU.min))
            dve.wait_ge(s_a, 3)
            step(nc.vector.tensor_scalar(a[:], e[:], -0.25, 1.0 / 3, ALU.mult, ALU.add))
            step(nc.vector.tensor_tensor(a[:], a[:], e[:], ALU.mult))
            step(nc.vector.tensor_scalar(a[:], a[:], -0.5, None, ALU.add))
            step(nc.vector.tensor_tensor(a[:], a[:], e[:], ALU.mult))
            step(nc.vector.scalar_tensor_tensor(out=a[:], in0=a[:], scalar=1.0, in1=e[:], op0=ALU.add, op1=ALU.mult))
            step(nc.vector.tensor_scalar(m[:], e[:], 1.0 / 128, None, ALU.is_lt))
            step(nc.vector.tensor_tensor(a[:], a[:], w[:], ALU.subtract))
            step(nc.vector.tensor_tensor(a[:], a[:], m[:], ALU.mult))
            step(nc.vector.tensor_tensor(a[:], a[:], w[:], ALU.add))
            step(nc.vector.scalar_tensor_tensor(out=dt[:], in0=x[:], scalar=0.0, in1=a[:], op0=ALU.max, op1=ALU.add))
            step(nc.vector.scalar_tensor_tensor(out=a[:], in0=dt[:], scalar=-1.0,
                                                in1=a_neg[:, None, :].to_broadcast([P, NT, H2]),
                                                op0=ALU.mult, op1=ALU.mult))
            assert n_v[0] == LAST_DT
            dve.wait_ge(s_a, 9)
            for d in range(2):
                step(nc.vector.tensor_tensor(ssd["tail"][:, :, d, :], ssd["tail"][:, :, d, :],
                                             dt[:, :, d * HEADS:(d + 1) * HEADS], ALU.mult))

        @block.scalar
        def _(act):
            act.wait_ge(s_in, 112)
            nc.scalar.activation(a_neg[:], a_neg[:], ACT.Exp).then_inc(s_a, 1)
            act.wait_ge(s_v, 4)
            nc.scalar.activation(e[:], w[:], ACT.Exp).then_inc(s_a, 1)
            act.wait_ge(s_a, 2)
            nc.scalar.activation(w[:], e[:], ACT.Ln, bias=1.0).then_inc(s_a, 1)
            act.wait_ge(s_mm, 1)
            for i, (name, d) in enumerate((("edge", 0), ("tail", 0), ("edge", 1), ("tail", 1), ("whole", 0),
                                           ("whole", 1))):
                nc.scalar.activation(ssd[name][:, :, d, :], sums[i][:, 0:NT * HEADS].rearrange("p (c h) -> p c h", h=HEADS),
                                     ACT.Exp).then_inc(s_a, 1)


LAST_DT = 15


def phase_token_major(nc, t, xbc_c, xbc_s, tok_s, ssd):
    NM = KT + GROUPS
    with ExitStack() as ctx:
        ph = Phase(nc, "tok", ctx)
        xin = ph.sb("in", [P, 2, NM, P])
        res = ph.sb("res", [P, 2, NM * P])
        bank = [ph.ps(f"b{i}", [P, 512]) for i in range(6)]
        s_ld, s_t, s_ev, s_st = ph.sems("ld", 2), ph.sem("t"), ph.sems("ev", 2), ph.sems("st", 2)
        dst = tok_s.rearrange("(c p) n -> c p n", p=P)
        block = ctx.enter_context(nc.Block())

        def chunks(eng, body):
            for src, n, done in ((xbc_c, NCC, 0), (xbc_s, NCH, NCC)):
                view = src[0:NM * P, :].rearrange("(m p) t -> p m t", p=P)
                with eng.Fori(0, n // 2) as i:
                    for q in range(2):
                        body(view, 2 * i + q, 2 * i + (done + q), i + done // 2, q)

        @block.sync
        def _(sp):
            def body(view, c, n, half, q):
                sp.wait_ge(s_t, n + 1)
                sp.dma_start(xin[:, q], view[:, :, bass.ds(c * P, P)]).then_inc(s_ld[q], 16)
            chunks(sp, body)

        @block.tensor
        def _(pe):
            pe.nop().then_inc(s_t, 2)

            def body(view, c, n, half, q):
                pe.wait_ge(s_ld[q], 16 * half + 16)
                pe.wait_ge(s_ev[0], 2 * n + 2)
                pe.wait_ge(s_ev[1], n + 1)
                for m in range(NM):
                    mm = pe.transpose(bank[3 * q + m // 4][:, (m % 4) * P:(m % 4 + 1) * P], xin[:, q, m, :],
                                      ssd["ident"][:])
                mm.then_inc(s_t, 1)
            chunks(pe, body)

        @block.scalar
        def _(act):
            act.nop().then_inc(s_ev[0], 4)
            for q in range(2):
                act.nop().then_inc(s_st[q], 16)

            def body(view, c, n, half, q):
                act.wait_ge(s_t, n + 3)
                act.wait_ge(s_st[q], 16 * half + 16)
                for b in (0, 2):
                    nc.scalar.copy(res[:, q, b * 512:(b + 1) * 512], bank[3 * q + b][:]).then_inc(s_ev[0], 1)
                act.wait_ge(s_ev[0], 2 * n + 6)
                act.wait_ge(s_ev[1], n + 3)
                act.dma_start(dst[bass.ds(n, 1)].rearrange("a p n -> p (a n)"), res[:, q, :]).then_inc(s_st[q], 16)
            chunks(act, body)
            for q in range(2):
                act.wait_ge(s_st[q], 16 * ((NCC + NCH) // 2 + 1))

        @block.vector
        def _(dve):
            dve.nop().then_inc(s_ev[1], 2)

            def body(view, c, n, half, q):
                dve.wait_ge(s_t, n + 3)
                dve.wait_ge(s_st[q], 16 * half + 16)
                nc.vector.tensor_copy(res[:, q, 512:1024], bank[3 * q + 1][:]).then_inc(s_ev[1], 1)
            chunks(dve, body)


def phase_states(nc, tok_s, st_s, ssd):
    XB = D + GROUPS * P
    with ExitStack() as ctx:
        ph = Phase(nc, "st", ctx)
        xb = ph.sb("xb", [P, 2, 2, XB])
        wx = ph.sb("wx", [P, 2, D])
        state = ph.sb("state", [P, 2, 2, D])
        faded = ph.sb("faded", [P, 2, D])
        ps = [ph.ps(f"s{d}", [P, 2, 512]) for d in range(2)]
        s_ld, s_wx, s_mm = [ph.sems(f"ld{d}", 2) for d in range(2)], ph.sems("wx", 2), ph.sems("mm", 2)
        s_fade, s_new = ph.sems("fade", 2), ph.sems("new", 2)
        s_st = [ph.sems(f"st{d}", 2) for d in range(2)]
        src = tok_s.rearrange("(c p) n -> c p n", p=P)
        dst = st_s.rearrange("(d c p) n -> d c p n", d=2, p=P)
        block = ctx.enter_context(nc.Block())

        def steps(eng, body):
            for s in range(NCC):
                body(s, 0, s, (s, NCC - 1 - s), None)
            with eng.Fori(0, NCH // 2) as i:
                for q in range(2):
                    f = 2 * i + q
                    b = i * (-2) + (NCH - 1 - q)
                    body(2 * i + (NCC + q), i + 1, q, (f + NCC, b + NCC), (f, b))

        @block.sync
        def _(sp):
            def body(s, half, q, chunk, latent):
                for d in range(2):
                    sp.wait_ge(s_mm[d], s + 1)
                    sp.dma_start(xb[:, q, d, :], src[bass.ds(chunk[d], 1)].rearrange("a p n -> p (a n)")
                                 ).then_inc(s_ld[d][q], 16)
            steps(sp, body)

        @block.tensor
        def _(pe):
            for d in range(2):
                pe.nop().then_inc(s_mm[d], 2)

            def body(s, half, q, chunk, latent):
                for d in range(2):
                    pe.wait_ge(s_wx[d], s + 1)
                    pe.wait_ge(s_new[d], s + 1)
                    for g in range(GROUPS):
                        mm = pe.matmul(ps[d][:, g // 2, (g % 2) * 256:(g % 2 + 1) * 256],
                                       xb[:, q, d, D + g * P:D + (g + 1) * P], wx[:, d, g * 256:(g + 1) * 256],
                                       start=True, stop=True)
                    mm.then_inc(s_mm[d], 1)
            steps(pe, body)

        @block.gpsimd
        def _(pool):
            def body(s, half, q, chunk, latent):
                for d in range(2):
                    pool.wait_ge(s_new[d], s + 1)
                    nc.gpsimd.tensor_tensor(faded[:, d, :].rearrange("p (h n) -> p h n", h=HEADS),
                                            state[:, d, q, :].rearrange("p (h n) -> p h n", h=HEADS),
                                            ssd["whole"][:, bass.ds(chunk[d], 1), d, :].rearrange("p a h -> p (a h)")
                                            [:, :, None].to_broadcast([P, HEADS, HD]), ALU.mult).then_inc(s_fade[d], 1)
            steps(pool, body)

        @block.scalar
        def _(act):
            for d in range(2):
                for q in range(2):
                    act.nop().then_inc(s_st[d][q], 16)

            def body(s, half, q, chunk, latent):
                if latent is None:
                    return
                for d in range(2):
                    act.wait_ge(s_new[d], s + 1)
                    act.dma_start(dst[d, bass.ds(latent[d], 1)].rearrange("a p n -> p (a n)"),
                                  state[:, d, q, :]).then_inc(s_st[d][q], 16)
            steps(act, body)
            for d in range(2):
                for q in range(2):
                    act.wait_ge(s_st[d][q], 16 * (NCH // 2 + 1))

        @block.vector
        def _(dve):
            for d in range(2):
                nc.vector.memset(state[:, d, 0, :], 0.0).then_inc(s_new[d], 1)

            def body(s, half, q, chunk, latent):
                for d in range(2):
                    dve.wait_ge(s_ld[d][q], 16 * half + 16)
                    dve.wait_ge(s_mm[d], s + 2)
                    nc.vector.tensor_tensor(wx[:, d, :].rearrange("p (h n) -> p h n", h=HEADS),
                                            xb[:, q, d, 0:D].rearrange("p (h n) -> p h n", h=HEADS),
                                            ssd["tail"][:, bass.ds(chunk[d], 1), d, :].rearrange("p a h -> p (a h)")
                                            [:, :, None].to_broadcast([P, HEADS, HD]), ALU.mult).then_inc(s_wx[d], 1)
                for d in range(2):
                    dve.wait_ge(s_mm[d], s + 3)
                    dve.wait_ge(s_fade[d], s + 1)
                    if latent is not None:
                        dve.wait_ge(s_st[d][1 - q], 16 * (half + q - 1) + 16)
                    nc.vector.tensor_tensor(state[:, d, 1 - q, :], faded[:, d, :], ps[d][:].rearrange("p a n -> p (a n)"),
                                            ALU.add).then_inc(s_new[d], 1)
            steps(dve, body)


def phase_ssd_outputs(nc, t, xbc_s, tok_s, st_s, z_s, g_s, ssd):
    with ExitStack() as ctx:
        ph = Phase(nc, "y", ctx)
        bc = ph.sb("bc", [P, 2, 2 * GROUPS, P])
        x = ph.sb("x", [P, 2, D])
        st = ph.sb("st", [P, 2, 2, D])
        z = ph.sb("z", [P, 2, KT, P])
        spread = ph.sb("spread", [P, 2, HEADS, P])
        decay = ph.sb("decay", [P, 2, HEADS, P])
        sc = ph.sb("sc", [P, 2, GROUPS, P])
        xdt = ph.sb("xdt", [P, 3, D])
        off = ph.sb("off", [P, 2, D])
        y = ph.sb("y", [P, D])
        res = ph.sb("res", [P, 2, KT, P])
        p_sc = ph.ps("p_sc", [P, 512])
        p_seg = [ph.ps(f"p_seg{i}", [P, 512]) for i in range(2)]
        p_y = ph.ps("p_y", [P, 2, 512])
        p_off = ph.ps("p_off", [P, 2, 512])
        p_t = ph.ps("p_t", [P, 512])
        s_ld, s_stl, s_zl, s_gst = ph.sems("ld", 2), ph.sems("stl", 2), ph.sems("zl", 2), ph.sems("gst", 2)
        s_spread, s_xdt, s_scm, s_scs = ph.sem("spread"), ph.sem("xdt"), ph.sem("scm"), ph.sem("scs")
        s_seg, s_exp, s_dec = ph.sem("seg"), ph.sem("exp"), ph.sem("dec")
        s_diag, s_offm, s_off, s_offs = ph.sem("diag"), ph.sem("offm"), ph.sem("off"), ph.sem("offs")
        s_y, s_turn, s_res = ph.sem("ysum"), ph.sem("turn"), ph.sem("res")
        bc_v = xbc_s[D:, :].rearrange("(m p) t -> p m t", p=P)
        z_v, g_v = (v.rearrange("(m p) t -> p m t", p=P) for v in (z_s, g_s))
        x_v = tok_s.rearrange("(c p) n -> c p n", p=P)
        st_v = st_s.rearrange("(d c p) n -> c p d n", d=2, p=P)
        heads = lambda ap: ap.rearrange("p (h n) -> p h n", h=HEADS)
        per_head = lambda name, c, d: (ssd[name][:, bass.ds(c + NCC, 1), d, :].rearrange("p a h -> p (a h)"))
        block = ctx.enter_context(nc.Block())

        def chunks(eng, body):
            with eng.Fori(0, NCH // 2 - 1) as i:
                for q in range(2):
                    body(2 * i + q, i, q, False)
            for q in range(2):
                body(NCH - 2 + q, NCH // 2 - 1, q, q == 1)

        @block.sync
        def _(sp):
            def body(c, half, q, last):
                sp.wait_ge(s_offm, 4 * c + 4)
                sp.wait_ge(s_xdt, 3 * c + 3)
                sp.dma_start(bc[:, q], bc_v[:, :, bass.ds(c * P, P)]).then_inc(s_ld[q], 16)
                sp.dma_start(x[:, q, :], x_v[bass.ds(c + NCC, 1), :, 0:D].rearrange("a p n -> p (a n)")
                             ).then_inc(s_ld[q], 16)
                sp.dma_start(st[:, q], st_v[bass.ds(c, 1)].rearrange("a p d n -> p (a d) n")).then_inc(s_stl[q], 16)
                sp.wait_ge(s_res, 2 * c + 2)
                sp.dma_start(z[:, q], z_v[:, :, bass.ds(half * (2 * P) + q * P, P)]).then_inc(s_zl[q], 16)
            chunks(sp, body)

        @block.gpsimd
        def _(pool):
            pool.nop().then_inc(s_xdt, 6)

            def prepare(c, half, q):
                for d in range(2):
                    pool.wait_ge(s_seg, 8 * c + 4 * d + 4)
                    nc.gpsimd.tensor_tensor(spread[:, d], ssd["masks"][:, 2 * d, None, :].to_broadcast([P, HEADS, P]),
                                            ssd["a"][:, bass.ds(c + NCC, 1), d * HEADS:(d + 1) * HEADS]
                                            .rearrange("p a h -> p (a h)")[:, :, None].to_broadcast([P, HEADS, P]),
                                            ALU.mult).then_inc(s_spread, 1)
                pool.wait_ge(s_ld[q], 32 * half + 32)
                pool.wait_ge(s_diag, c + 1)
                if not (isinstance(c, int) and c == 0):
                    pool.wait_ge(s_offs, 2 * c)
                for n in range(3):
                    f = (ssd["dt"][:, bass.ds(c + NCC, 1), n * HEADS:(n + 1) * HEADS].rearrange("p a h -> p (a h)")
                         if n < 2 else ssd["d_row"][:])
                    nc.gpsimd.tensor_tensor(heads(xdt[:, n, :]), heads(x[:, q, :]),
                                            f[:, :, None].to_broadcast([P, HEADS, HD]), ALU.mult).then_inc(s_xdt, 1)

            prepare(0, 0, 0)

            def body(c, half, q, last):
                if not last:
                    prepare(c + 1, half + q, 1 - q)
            chunks(pool, body)

        @block.tensor
        def _(pe):
            pe.nop().then_inc(s_seg, 8)
            pe.nop().then_inc(s_diag, 1)
            pe.nop().then_inc(s_offm, 8)
            pe.nop().then_inc(s_turn, 2)

            def turn(c, b):
                pe.wait_ge(s_y, c + 2)
                pe.wait_ge(s_res, 2 * c + b + 4)
                for m in range(4):
                    mm = pe.transpose(p_t[:, m * P:(m + 1) * P], y[:, (4 * b + m) * P:(4 * b + m + 1) * P],
                                      ssd["ident"][:])
                mm.then_inc(s_turn, 1)

            def scores(c, half, q, before=None):
                pe.wait_ge(s_ld[q], 32 * half + 32)
                pe.wait_ge(s_scs, 2 * c + 2)
                for g in range(GROUPS):
                    mm = pe.matmul(p_sc[:, g * P:(g + 1) * P], bc[:, q, g, :], bc[:, q, GROUPS + g, :], start=True,
                                   stop=True)
                mm.then_inc(s_scm, 1)
                for d in range(2):
                    pe.wait_ge(s_spread, 2 * c + d + 1)
                    for b in range(4):
                        n = 4 * d + b
                        pe.wait_ge(s_exp, 8 * c + n + 1)
                        pe.matmul(p_seg[n % 2][:], ssd["masks"][:, (1, 3)[d], :],
                                  spread[:, d, 4 * b:4 * b + 4, :].rearrange("p h q -> p (h q)"), start=True,
                                  stop=True).then_inc(s_seg, 1)
                    if before is not None:
                        turn(before, d)

            scores(0, 0, 0)

            def body(c, half, q, last):
                pe.wait_ge(s_stl[q], 16 * half + 16)
                for u in range(4):
                    d, b = u // 2, u % 2
                    pe.wait_ge(s_off, 4 * c + u + 1)
                    for g in (2 * b, 2 * b + 1):
                        mm = pe.matmul(p_off[:, b, (g % 2) * 256:(g % 2 + 1) * 256], bc[:, q, GROUPS + g, :],
                                       st[:, q, d, g * 256:(g + 1) * 256], start=True, stop=True)
                    mm.then_inc(s_offm, 1)
                pe.wait_ge(s_xdt, 3 * c + 9)
                pe.wait_ge(s_y, c + 1)
                pe.wait_ge(s_dec, 8 * c + 9)
                for h in range(HEADS):
                    for d in range(2):
                        mm = pe.matmul(p_y[:, h // 8, (h % 8) * HD:(h % 8 + 1) * HD], decay[:, d, h, :],
                                       xdt[:, d, h * HD:(h + 1) * HD], start=(d == 0), stop=(d == 1))
                mm.then_inc(s_diag, 1)
                if not last:
                    scores(c + 1, half + q, 1 - q, c)
                else:
                    turn(c, 0)
                    turn(c, 1)
            chunks(pe, body)

        @block.scalar
        def _(act):
            act.nop().then_inc(s_exp, 2)
            for q in range(2):
                act.nop().then_inc(s_gst[q], 16)

            def decays(c):
                for n in range(8):
                    act.wait_ge(s_seg, 8 * c + n + 9)
                    act.wait_ge(s_diag, c + 1)
                    nc.scalar.activation(decay[:, n // 4, 4 * (n % 4):4 * (n % 4) + 4, :].rearrange("p h q -> p (h q)"),
                                         p_seg[n % 2][:], ACT.Exp).then_inc(s_exp, 1)

            decays(0)

            def body(c, half, q, last):
                if not last:
                    decays(c + 1)
                act.wait_ge(s_res, 2 * c + 6)
                act.dma_start(g_v[:, :, bass.ds(c * P, P)], res[:, q]).then_inc(s_gst[q], 16)
            chunks(act, body)
            for q in range(2):
                act.wait_ge(s_gst[q], 16 * (NCH // 2 + 1))

        @block.vector
        def _(dve):
            for s, n in ((s_scs, 2), (s_off, 2), (s_y, 1), (s_res, 4), (s_dec, 1)):
                dve.nop().then_inc(s, n)

            def gated(c, half, q, b):
                if b == 0:
                    dve.wait_ge(s_zl[q], 16 * half + 16)
                    dve.wait_ge(s_gst[q], 16 * half + 16)
                dve.wait_ge(s_turn, 2 * c + b + 3)
                nc.vector.tensor_tensor(res[:, q, 4 * b:4 * b + 4, :].rearrange("p m n -> p (m n)"), p_t[:],
                                        z[:, q, 4 * b:4 * b + 4, :].rearrange("p m n -> p (m n)"),
                                        ALU.mult).then_inc(s_res, 1)

            def weigh(c, before=None):
                dve.wait_ge(s_scm, c + 1)
                for d in range(2):
                    dve.wait_ge(s_dec, 8 * c + 1)
                    nc.vector.tensor_tensor(sc[:, d], p_sc[:].rearrange("p (g q) -> p g q", g=GROUPS),
                                            ssd["masks"][:, 2 * d, None, :].to_broadcast([P, GROUPS, P]),
                                            ALU.mult).then_inc(s_scs, 1)
                dve.wait_ge(s_scs, 2 * c + 4)
                for n in range(8):
                    d, g = n // 4, n % 4
                    dve.wait_ge(s_exp, 8 * c + n + 3)
                    nc.vector.tensor_tensor(decay[:, d, 4 * g:4 * g + 4, :], decay[:, d, 4 * g:4 * g + 4, :],
                                            sc[:, d, g, None, :].to_broadcast([P, HPG, P]), ALU.mult).then_inc(s_dec, 1)
                    if before is not None and n >= 6:
                        gated(*before, n - 6)

            weigh(0)

            def body(c, half, q, last):
                dve.wait_ge(s_y, c + 1)
                for u in range(4):
                    d, b = u // 2, u % 2
                    dve.wait_ge(s_offm, 4 * c + u + 9)
                    nc.vector.tensor_tensor(off[:, d, b * 512:(b + 1) * 512].rearrange("p (h n) -> p h n", n=HD),
                                            p_off[:, b, :].rearrange("p (h n) -> p h n", n=HD),
                                            per_head("edge", c, d)[:, 8 * b:8 * b + 8, None]
                                            .to_broadcast([P, HEADS // 2, HD]), ALU.mult).then_inc(s_off, 1)
                dve.wait_ge(s_off, 4 * c + 6)
                dve.wait_ge(s_turn, 2 * c + 2)
                nc.vector.tensor_tensor(y[:], off[:, 0, :], off[:, 1, :], ALU.add).then_inc(s_offs, 1)
                dve.wait_ge(s_offs, 2 * c + 1)
                dve.wait_ge(s_xdt, 3 * c + 9)
                nc.vector.tensor_tensor(y[:], y[:], xdt[:, 2, :], ALU.add).then_inc(s_offs, 1)
                dve.wait_ge(s_offs, 2 * c + 2)
                dve.wait_ge(s_diag, c + 2)
                nc.vector.tensor_tensor(y[:], y[:], p_y[:].rearrange("p a n -> p (a n)"), ALU.add).then_inc(s_y, 1)
                if not last:
                    weigh(c + 1, (c, half, q))
                else:
                    gated(c, half, q, 0)
                    gated(c, half, q, 1)
            chunks(dve, body)


def phase_merge(nc, keep, w_br, ym_s, z2_s, hg_s, gates_s, mix_s):
    BW = 256
    NB = SEQ // BW
    HK = KT // 2
    scale = keep["par"][:, PAR["m_norm_w"]:PAR["m_norm_w"] + KT]
    with ExitStack() as ctx:
        ph = Phase(nc, "mg", ctx)
        w_hi, w_lo = ph.sb("w_hi", [P, 2 * KT, D], F32R), ph.sb("w_lo", [P, 2 * KT, D], F32R)
        ym = ph.sb("ym", [P, KT, BW])
        m_hi, m_lo = ph.sb("m_hi", [P, KT, BW], F32R), ph.sb("m_lo", [P, KT, BW], F32R)
        h_hi, h_lo = ph.sb("h_hi", [P, KT, BW], F32R), ph.sb("h_lo", [P, KT, BW], F32R)
        z2 = ph.sb("z2", [P, KT, BW])
        hg = ph.sb("hg", [P, 2, 2, BW])
        gate = ph.sb("gates", [P, 2, HK, BW])
        mix = ph.sb("mix", [P, KT, BW])
        w_raw = [buf[:, n].rearrange("p k t -> p (k t)") for buf in
                 (mix[:].rearrange("p (a k) t -> p a k t", a=2), gate) for n in range(2)]
        odd = ph.sb("odd", [P, BW])
        ms = ph.sb("ms", [P, GROUPS, BW])
        gated = ph.sb("gated", [P, BW])
        ones = ph.sb("ones", [P, P])
        ssq = ph.ps("ssq", [P, GROUPS, BW])
        bank = [ph.ps(f"bank{b}", [P, 512]) for b in range(4)]
        s_w, s_whi, s_wlo, s_hgl = ph.sems("w", 4), ph.sem("whi"), ph.sems("wlo", 2), ph.sems("hgl", 2)
        s_yml, s_zl, s_gl, s_st = ph.sems("yml", 2), ph.sems("zl", 2), ph.sems("gl", 2), ph.sems("st", 2)
        s_one, s_sq, s_add, s_ss, s_ms, s_root, s_rec = (ph.sem(n) for n in (
            "one", "sq", "add", "ss", "ms_done", "root", "rec"))
        s_v, s_mhi, s_mlo = ph.sem("v"), ph.sem("mhi"), ph.sem("mlo")
        s_hv, s_hhi, s_hlo = ph.sem("hv"), ph.sem("hhi"), ph.sem("hlo")
        s_mm, s_ev, s_mix = ph.sem("mm"), ph.sem("ev"), ph.sem("mixed")
        half = lambda n: slice(n * HK, (n + 1) * HK)
        ym_v, z2_v, hg_v, mix_v = (s.rearrange("(k p) t -> p k t", p=P) for s in (ym_s, z2_s, hg_s, mix_s))
        g_v = gates_s.rearrange("(b k p) t -> b p k t", b=2, p=P)
        block = ctx.enter_context(nc.Block())

        def blocks(eng, body):
            with eng.Fori(0, NB - 1) as c:
                body(c, False)
            body(NB - 1, True)

        @block.sync
        def _(sp):
            def load_ym(c):
                for n in range(2):
                    sp.dma_start(ym[:, half(n)], ym_v[:, half(n), bass.ds(c * BW, BW)]).then_inc(s_yml[n], 16)

            def load_z2(c):
                for n in range(2):
                    sp.dma_start(z2[:, half(n)], z2_v[:, half(n), bass.ds(c * BW, BW)]).then_inc(s_zl[n], 16)

            def load_hg(c, i):
                sp.wait_ge(s_hv, 4 * c + (i + 1))
                sp.dma_start(hg[:, i % 2], hg_v[:, 2 * i:2 * i + 2, bass.ds(c * BW, BW)]).then_inc(s_hgl[i % 2], 16)

            def load_gate(c, b, n):
                sp.dma_start(gate[:, n], g_v[b, :, half(n), bass.ds(c * BW, BW)]).then_inc(s_gl[n], 16)

            def load_weights(first, last):
                for n in range(first, last):
                    if n >= 4:
                        sp.wait_ge(s_wlo[n % 2], n // 2 - 1)
                    sp.dma_start(w_raw[n % 4], w_br[n]).then_inc(s_w[n % 4], 16)

            load_ym(0)
            load_weights(0, 2)
            load_z2(0)
            load_hg(0, 0)
            load_hg(0, 1)
            load_weights(2, KT)
            load_hg(0, 2)
            load_hg(0, 3)
            load_weights(KT, 2 * KT)
            for n in range(2):
                sp.wait_ge(s_wlo[n], KT)
            load_gate(0, 0, 0)
            load_gate(0, 0, 1)

            def body(c, last):
                if not last:
                    sp.wait_ge(s_mlo, 2 * c + 2)
                    load_ym(c + 1)
                for n in range(2):
                    sp.wait_ge(s_ev, 16 * c + (4 * n + 8))
                    load_gate(c, 1, n)
                if not last:
                    sp.wait_ge(s_hlo, 2 * c + 2)
                    load_z2(c + 1)
                    load_hg(c + 1, 0)
                    load_hg(c + 1, 1)
                    for n in range(2):
                        sp.wait_ge(s_ev, 16 * c + (4 * n + 16))
                        load_gate(c + 1, 0, n)
                    load_hg(c + 1, 2)
                    load_hg(c + 1, 3)
            blocks(sp, body)

        @block.tensor
        def _(pe):
            pe.wait_ge(s_one, 1)

            def sums(c):
                pe.wait_ge(s_add, 4 * c + 5)
                for g in range(GROUPS):
                    mm = pe.matmul(ssq[:, g, :], ones[:], ms[:, g, :], start=True, stop=True)
                mm.then_inc(s_ss, 1)

            def branch(c, b, hi, lo, ready):
                pe.wait_ge(ready, 2 * c + 2)
                for j in range(KT):
                    n = 8 * b + j
                    pe.wait_ge(s_wlo[n % 2], n // 2 + 1)
                    pe.wait_ge(s_ev, 16 * c + (n + 1))
                    o = bank[n % 4][:, 0:BW]
                    for k in range(KT):
                        m = slice(k * P, (k + 1) * P)
                        pe.matmul(o, w_hi[:, n, m], hi[:, k, :], start=(k == 0), stop=False)
                        pe.matmul(o, w_hi[:, n, m], lo[:, k, :], start=False, stop=False)
                        mm = pe.matmul(o, w_lo[:, n, m], hi[:, k, :], start=False, stop=(k == KT - 1))
                    mm.then_inc(s_mm, 1)

            sums(0)

            def body(c, last):
                branch(c, 0, m_hi, m_lo, s_mlo)
                if not last:
                    sums(c + 1)
                branch(c, 1, h_hi, h_lo, s_hlo)
            blocks(pe, body)

        @block.scalar
        def _(act):
            def squares(c):
                for k in range(KT):
                    act.wait_ge(s_yml[k // HK], 16 * c + 16)
                    if k % 2 == 0:
                        act.wait_ge(s_v, 8 * c + 8)
                    else:
                        act.wait_ge(s_add, 4 * c + (k // 2 + 1))
                    dst = ms[:, k // 2, :] if k % 2 == 0 else odd[:]
                    nc.scalar.activation(dst, ym[:, k, :], ACT.Square).then_inc(s_sq, 1)

            def root(c):
                act.wait_ge(s_ms, c + 1)
                nc.scalar.activation(ms[:], ms[:], ACT.Sqrt).then_inc(s_root, 1)

            def m_high(c):
                for n in range(2):
                    act.wait_ge(s_v, 8 * c + (4 * n + 12))
                    if not (isinstance(c, int) and c == 0):
                        act.wait_ge(s_mm, 16 * c - 8)
                    nc.scalar.activation(m_hi[:, half(n)], ym[:, half(n)], ACT.Copy).then_inc(s_mhi, 1)

            def h_high(c):
                for n in range(2):
                    act.wait_ge(s_hv, 4 * c + (2 * n + 4))
                    if not (isinstance(c, int) and c == 0):
                        act.wait_ge(s_mm, 16 * c)
                    nc.scalar.activation(h_hi[:, half(n)], z2[:, half(n)], ACT.Copy).then_inc(s_hhi, 1)

            def weights_high(first, last):
                for n in range(first, last):
                    act.wait_ge(s_w[n % 4], 16 * (n // 4 + 1))
                    nc.scalar.activation(w_hi[:, n], w_raw[n % 4], ACT.Copy).then_inc(s_whi, 1)

            for n in range(2):
                act.nop().then_inc(s_st[n], 16)
            squares(0)
            root(0)
            m_high(0)
            weights_high(0, KT)
            h_high(0)
            weights_high(KT, 2 * KT)

            def body(c, last):
                if not last:
                    squares(c + 1)
                    root(c + 1)
                    m_high(c + 1)
                for n in range(2):
                    act.wait_ge(s_mix, 8 * c + (4 * n + 5))
                    act.dma_start(mix_v[:, half(n), bass.ds(c * BW, BW)], mix[:, half(n)]).then_inc(s_st[n], 16)
                if not last:
                    h_high(c + 1)
            blocks(act, body)
            for n in range(2):
                act.wait_ge(s_st[n], 16 * (NB + 1))

        @block.gpsimd
        def _(pool):
            pool.nop().then_inc(s_add, 1)
            pool.nop().then_inc(s_mix, 1)

            def adds(c):
                for g in range(GROUPS):
                    pool.wait_ge(s_sq, 8 * c + (2 * g + 2))
                    nc.gpsimd.tensor_tensor(ms[:, g, :], ms[:, g, :], odd[:], ALU.add).then_inc(s_add, 1)

            def h_low(c):
                for n in range(2):
                    pool.wait_ge(s_hhi, 2 * c + (n + 1))
                    nc.gpsimd.tensor_tensor(h_lo[:, half(n)], z2[:, half(n)],
                                            h_hi[:, half(n)].bitcast(F32), ALU.subtract).then_inc(s_hlo, 1)

            def weights_low(first, last):
                for n in range(first, last, 2):
                    pool.wait_ge(s_whi, n + 1)
                    nc.gpsimd.tensor_tensor(w_lo[:, n], w_raw[n % 4], w_hi[:, n].bitcast(F32),
                                            ALU.subtract).then_inc(s_wlo[0], 1)

            adds(0)
            weights_low(0, KT)
            h_low(0)
            weights_low(KT, 2 * KT)

            def body(c, last):
                if not last:
                    adds(c + 1)
                for j in range(KT):
                    pool.wait_ge(s_ev, 16 * c + (8 + j + 5))
                    nc.gpsimd.tensor_tensor(mix[:, j, :], mix[:, j, :], gated[:], ALU.add).then_inc(s_mix, 1)
                if not last:
                    h_low(c + 1)
            blocks(pool, body)

        @block.vector
        def _(dve):
            nc.vector.memset(ones[:], 1.0).then_inc(s_one, 1)
            dve.nop().then_inc(s_v, 8)
            dve.nop().then_inc(s_ev, 4)
            dve.nop().then_inc(s_hv, 2)

            def mean(c):
                dve.wait_ge(s_ss, c + 1)
                nc.vector.tensor_scalar(ms[:], ssq[:], 1.0 / (D // GROUPS), EPS, ALU.mult, ALU.add).then_inc(s_ms, 1)

            def inverse(c):
                dve.wait_ge(s_root, c + 1)
                nc.vector.reciprocal(ms[:], ms[:]).then_inc(s_rec, 1)
                dve.wait_ge(s_rec, c + 1)

            def norm(c, k):
                nc.vector.scalar_tensor_tensor(out=ym[:, k, :], in0=ym[:, k, :], scalar=scale[:, k:k + 1],
                                               in1=ms[:, k // 2, :], op0=ALU.mult, op1=ALU.mult).then_inc(s_v, 1)

            def m_low(c, n):
                dve.wait_ge(s_mhi, 2 * c + (n + 1))
                nc.vector.tensor_tensor(m_lo[:, half(n)], ym[:, half(n)], m_hi[:, half(n)].bitcast(F32),
                                        ALU.subtract).then_inc(s_mlo, 1)

            def h_value(c):
                for i in range(4):
                    dve.wait_ge(s_zl[i // 2], 16 * c + 16)
                    dve.wait_ge(s_hgl[i % 2], 32 * c + (16 * (i // 2) + 16))
                    nc.vector.tensor_tensor(z2[:, 2 * i:2 * i + 2], z2[:, 2 * i:2 * i + 2], hg[:, i % 2],
                                            ALU.mult).then_inc(s_hv, 1)

            def weights_low(first, last):
                for n in range(first, last, 2):
                    dve.wait_ge(s_whi, n + 1)
                    nc.vector.tensor_tensor(w_lo[:, n], w_raw[n % 4], w_hi[:, n].bitcast(F32),
                                            ALU.subtract).then_inc(s_wlo[1], 1)

            mean(0)
            inverse(0)
            for k in range(KT):
                norm(0, k)
            m_low(0, 0)
            m_low(0, 1)
            weights_low(1, KT)
            h_value(0)
            weights_low(KT + 1, 2 * KT)
            dve.wait_ge(s_wlo[0], KT)
            dve.wait_ge(s_wlo[1], KT)

            def body(c, last):
                for j in range(KT):
                    n = j // HK
                    dve.wait_ge(s_mm, 16 * c + (j + 1))
                    dve.wait_ge(s_gl[n], 32 * c + 16)
                    dve.wait_ge(s_st[n], 16 * c + 16)
                    nc.vector.tensor_tensor(mix[:, j, :], bank[j % 4][:, 0:BW], gate[:, n, j % HK, :],
                                            ALU.mult).then_inc(s_ev, 1)
                if not last:
                    mean(c + 1)
                for j in range(KT):
                    n = j // HK
                    dve.wait_ge(s_mm, 16 * c + (8 + j + 1))
                    dve.wait_ge(s_gl[n], 32 * c + 32)
                    dve.wait_ge(s_mix, 8 * c + (j + 1))
                    nc.vector.tensor_tensor(gated[:], bank[j % 4][:, 0:BW], gate[:, n, j % HK, :],
                                            ALU.mult).then_inc(s_ev, 1)
                    if last:
                        continue
                    if j == 0:
                        inverse(c + 1)
                    elif j <= 4:
                        norm(c + 1, 2 * j - 2)
                        norm(c + 1, 2 * j - 1)
                    elif j <= 6:
                        m_low(c + 1, j - 5)
                if not last:
                    h_value(c + 1)
            blocks(dve, body)


def phase_output(nc, t, keep, mix_s, out):
    NT = SEQ // P
    with ExitStack() as ctx:
        ph = Phase(nc, "out", ctx)
        w = ph.sb("w", [P, 4, D])
        wg = ph.sb("wg", [P, 4, D])
        w_hi, w_lo = ph.sb("w_hi", [P, KT, D], F32R), ph.sb("w_lo", [P, KT, D], F32R)
        mix = ph.sb("mix", [P, 2, KT, P])
        m_hi, m_lo = ph.sb("m_hi", [P, 2, KT, P], F32R), ph.sb("m_lo", [P, 2, KT, P], F32R)
        x = ph.sb("x", [P, 2, D])
        y = ph.sb("y", [P, 2, D])
        sq = ph.sb("sq", [P, D])
        ss = ph.sb("ss", [P, 4])
        fw = ph.sb("fw", [P, D])
        res = ph.sb("res", [P, 2, D])
        bank = [ph.ps(f"bank{b}", [P, 2, 512]) for b in range(2)]
        s_w, s_wg, s_whi, s_wlo, s_in = ph.sems("w", 4), ph.sem("wg"), ph.sem("whi"), ph.sem("wlo"), ph.sem("in")
        s_mix, s_x, s_mhi, s_mlo, s_mm = ph.sems("mix", 2), ph.sems("x", 2), ph.sem("mhi"), ph.sem("mlo"), ph.sem("mm")
        s_y, s_sq, s_ms, s_root, s_rec, s_res = (ph.sem(n) for n in ("y", "sq", "ms", "root", "rec", "res"))
        s_st = ph.sems("st", 2)
        mix_v = mix_s.rearrange("(k p) t -> p k t", p=P)
        block = ctx.enter_context(nc.Block())

        def tiles(eng, body):
            with eng.Fori(0, NT // 2) as i:
                for q in range(2):
                    body(2 * i + q, i, q)

        @block.sync
        def _(sp):
            sp.dma_start(fw[:], t["final_norm_w"].to_broadcast([P, D])).then_inc(s_in, 16)
            for k in range(KT):
                if k >= 4:
                    sp.wait_ge(s_wg, k - 3)
                sp.dma_start(w[:, k % 4, :], t["w_out"][k * P:(k + 1) * P, :]).then_inc(s_w[k % 4], 16)

            def body(n, half, q):
                sp.wait_ge(s_mlo, n + 1)
                sp.dma_start(mix[:, q], mix_v[:, :, bass.ds(n * P, P)]).then_inc(s_mix[q], 16)
                sp.wait_ge(s_y, n + 1)
                sp.dma_start(x[:, q, :], t["x"][bass.ds(n * P, P), :]).then_inc(s_x[q], 16)
            tiles(sp, body)

        @block.gpsimd
        def _(pool):
            pool.nop().then_inc(s_mlo, 2)
            for k in range(KT):
                pool.wait_ge(s_whi, k + 1)
                nc.gpsimd.tensor_tensor(w_lo[:, k, :], wg[:, k % 4, :], w_hi[:, k, :].bitcast(F32),
                                        ALU.subtract).then_inc(s_wlo, 1)

            def body(n, half, q):
                pool.wait_ge(s_mhi, n + 1)
                pool.wait_ge(s_mm, n + 1)
                nc.gpsimd.tensor_tensor(m_lo[:, q], mix[:, q], m_hi[:, q].bitcast(F32),
                                        ALU.subtract).then_inc(s_mlo, 1)
            tiles(pool, body)

        @block.tensor
        def _(pe):
            pe.nop().then_inc(s_mm, 2)
            pe.wait_ge(s_wlo, KT)

            def body(n, half, q):
                pe.wait_ge(s_mlo, n + 3)
                pe.wait_ge(s_y, n + 1)
                for b in range(2):
                    r = slice(b * 512, (b + 1) * 512)
                    for k in range(KT):
                        o = bank[q][:, b, :]
                        pe.matmul(o, m_hi[:, q, k, :], w_hi[:, k, r], start=(k == 0), stop=False)
                        pe.matmul(o, m_hi[:, q, k, :], w_lo[:, k, r], start=False, stop=False)
                        mm = pe.matmul(o, m_lo[:, q, k, :], w_hi[:, k, r], start=False, stop=(k == KT - 1))
                mm.then_inc(s_mm, 1)
            tiles(pe, body)

        @block.scalar
        def _(act):
            for k in range(KT):
                act.wait_ge(s_wg, k + 1)
                nc.scalar.activation(w_hi[:, k, :], wg[:, k % 4, :], ACT.Copy).then_inc(s_whi, 1)
            for q in range(2):
                act.nop().then_inc(s_st[q], 16)
            act.wait_ge(s_mix[0], 16)
            nc.scalar.activation(m_hi[:, 0], mix[:, 0], ACT.Copy).then_inc(s_mhi, 1)

            def body(n, half, q, last=False):
                if not last:
                    act.wait_ge(s_mix[1 - q], 16 * (half + q) + 16)
                    act.wait_ge(s_mm, n + 2)
                    nc.scalar.activation(m_hi[:, 1 - q], mix[:, 1 - q], ACT.Copy).then_inc(s_mhi, 1)
                act.wait_ge(s_y, n + 3)
                nc.scalar.activation(sq[:], y[:, q, :], ACT.Square, accum_out=ss[:, 0:1]).then_inc(s_sq, 1)
                act.wait_ge(s_ms, n + 1)
                nc.scalar.activation(ss[:, 2:3], ss[:, 1:2], ACT.Sqrt).then_inc(s_root, 1)
                act.wait_ge(s_res, n + 1)
                act.dma_start(out[bass.ds(n * P, P), :], res[:, q, :]).then_inc(s_st[q], 16)
            with act.Fori(0, NT // 2 - 1) as i:
                for q in range(2):
                    body(2 * i + q, i, q)
            body(NT - 2, NT // 2 - 1, 0)
            body(NT - 1, NT // 2 - 1, 1, last=True)
            for q in range(2):
                act.wait_ge(s_st[q], 16 * (NT // 2 + 1))

        @block.vector
        def _(dve):
            dve.wait_ge(s_in, 16)
            dve.nop().then_inc(s_y, 2)
            for k in range(KT):
                dve.wait_ge(s_w[k % 4], 16 * (k // 4 + 1))
                if k >= 4:
                    dve.wait_ge(s_wlo, k - 3)
                nc.vector.tensor_tensor(wg[:, k % 4, :], w[:, k % 4, :], keep["gate"][:], ALU.mult).then_inc(s_wg, 1)

            def body(n, half, q):
                dve.wait_ge(s_x[q], 16 * half + 16)
                dve.wait_ge(s_mm, n + 3)
                nc.vector.tensor_tensor(y[:, q, :], x[:, q, :], bank[q][:].rearrange("p a n -> p (a n)"),
                                        ALU.add).then_inc(s_y, 1)
                dve.wait_ge(s_sq, n + 1)
                nc.vector.tensor_scalar(ss[:, 1:2], ss[:, 0:1], 1.0 / D, EPS, ALU.mult, ALU.add).then_inc(s_ms, 1)
                dve.wait_ge(s_root, n + 1)
                nc.vector.reciprocal(ss[:, 3:4], ss[:, 2:3]).then_inc(s_rec, 1)
                dve.wait_ge(s_rec, n + 1)
                dve.wait_ge(s_st[q], 16 * half + 16)
                nc.vector.scalar_tensor_tensor(out=res[:, q, :], in0=y[:, q, :], scalar=ss[:, 3:4], in1=fw[:],
                                               op0=ALU.mult, op1=ALU.mult).then_inc(s_res, 1)
            tiles(dve, body)


PAR_LAYOUT = (("shift_b", KT), ("scale_b", KT), ("norm_w", KT), ("m_norm_w", KT), ("h_bias", 2 * KT),
              ("delta", KT), ("zero", KT))
PAR, _at = {}, 0
for _name, _n in PAR_LAYOUT:
    PAR[_name] = _at
    _at += _n
NPAR = _at


def columns(v):
    return np.ascontiguousarray(np.reshape(v, (-1, P)).T)


def layout(inputs):
    a = {k: np.asarray(v) for k, v in inputs.items()}
    f = np.float32
    out = {}
    out["x"] = a["x"][0]
    out["xT"] = a["x"][0].T
    out["ctxT"] = a["ctx"][0].T
    out["c_cols"] = np.stack([a["c"][0].reshape(P, KT), a["c_ctx"].reshape(P, KT)], axis=2)
    out["ada_w"] = a["ada_w"][0]
    out["gate_bias"] = a["ada_b"][:, 2 * D:]
    w = a["w_in"][0]
    o_xbc = D
    o_dt = o_xbc + 2 * D
    o_rest = o_dt + 2 * HEADS
    dt = np.concatenate([w[:, o_dt:o_rest], np.zeros((D, P - 2 * HEADS), f)], axis=1)
    w = np.concatenate([w[:, :o_dt], dt, w[:, o_rest:]], axis=1)
    nt = w.shape[1] // P
    out["w_rec"] = w.reshape(KT, P, nt, P).transpose(2, 1, 0, 3).reshape(nt, P, D)
    taps = np.concatenate([np.concatenate([a[s + "_w"][0], a[s + "_b"]]) for s in ("m_conv", "h_conv")], axis=1)
    out["conv_taps"] = taps.reshape(NTAP, N_CONV, P).transpose(2, 1, 0).reshape(P, N_CONV * NTAP)
    lo, hi = np.log(f(1e-2)) / f(1.5), np.log(f(1e-2)) / f(0.3)
    ds = np.arange(D, dtype=f) / f(D - 1)
    delta = np.abs(f(lo) * (f(1) - ds) + f(hi) * ds).astype(f)
    out["par"] = np.concatenate([columns(v) for v in (
        a["ada_b"][0, :D], a["ada_b"][0, D:2 * D], a["norm_w"][0], a["m_norm_w"][0],
        a["h_bias"][0].reshape(-1), delta, np.zeros(D, f))], axis=1)
    out["w_br"] = np.concatenate([
        a[k][0].reshape(KT, P, KT, P).transpose(2, 1, 0, 3).reshape(KT, P, D) for k in ("w_branch_m", "w_branch_h")])
    out["w_out"] = a["w_out"][0]
    out["final_norm_w"] = a["final_norm_w"][None]
    out["m_dt_bias"] = a["m_dt_bias"][0].reshape(1, -1)
    out["m_a_log"] = a["m_a_log"][0].reshape(1, -1)
    out["d_row"] = a["m_d"]
    out["h_pm"] = np.stack([a[k][0] for k in ("h_b1", "h_b2", "h_b3", "h_freq")], axis=1)
    for k in ("h_w1", "h_w2", "h_w3", "h_w_out"):
        out[k] = a[k][0]
    out.update(constants())
    return {k: np.ascontiguousarray(v) for k, v in out.items()}


def constants():
    f = np.float32
    out = {}
    t = np.arange(SEQ, dtype=f) / f(SEQ - 1)
    bands = (H_EMB - 1) // 2
    bstep = np.arange(bands, dtype=f) / f(bands - 1)
    bf = f(1e-4) * (f(1) - bstep) + f(bands - 1) * bstep
    w = f(2.0 * np.pi / SEQ) * np.arange(SEQ, dtype=f)
    fw = (bf[:, None] * w[None, :]).astype(f).astype(np.float64)
    out["feats"] = np.concatenate([t[None], np.cos(fw), -np.sin(fw)], axis=0).astype(f)
    out["trow"] = -t[None]
    n1 = np.arange(N1D)[:, None]
    k1 = np.arange(NK1)[None, :]
    ang = 2 * np.pi * n1 * k1 / N1
    fwd = np.concatenate([np.cos(ang), -np.sin(ang)[:, 1:NK1 - 1]], axis=1)
    out["f1"] = np.einsum("ar,cd->card", fwd, np.eye(CG)).reshape(P, NR * CG).astype(f)
    al = np.where((np.arange(NK1) == 0) | (np.arange(NK1) == NK1 - 1), 1.0, 2.0) / NF
    inv = np.concatenate([np.cos(ang) * al, (-np.sin(ang) * al)[:, 1:NK1 - 1]], axis=1)
    eye = np.eye(CG).reshape(2, 4, CG)
    out["back"] = np.einsum("ar,hcd->crhda", inv, eye).reshape(P, 2, P).astype(f)
    n2 = np.arange(N2)[:, None, None]
    k2 = np.arange(N2)[None, None, :]
    kk = np.arange(NK1)[None, :, None] + N1 * k2
    th = 2 * np.pi * ((n2 * kk) % NF) / NF
    tw = np.stack([np.cos(th), np.sin(th), -np.sin(th)], axis=2)
    out["tw_fwd"] = tw.astype(f)
    out["tw_inv"] = tw.transpose(3, 1, 2, 0).astype(f)
    out["ident"] = np.eye(P, dtype=f)
    r, c = np.arange(P)[:, None], np.arange(P)[None, :]
    out["masks"] = np.stack([r <= c, r > c, r >= c, r < c, r >= 0 * c], axis=1).astype(f)
    return out


T_Z, T_XBC = 0, KT
T_DT = T_XBC + 2 * KT
T_HG = T_DT + 1
T_PROJ = T_HG + KT
T_G = T_PROJ + 3 * KT
N_CONV = 5 * KT


def program(nc, t, out):
    def scratch(name, rows, cols):
        return nc.dram_tensor(name, [rows, cols], F32).ap()

    z_s = scratch("z_s", D, SEQ)
    xbc_s = scratch("xbc_s", 2 * D, SEQ)
    xbc_c = scratch("xbc_c", 2 * D, CTX)
    dt_s = scratch("dt_s", P, SEQ)
    dt_c = scratch("dt_c", P, CTX)
    hg_s = scratch("hg_s", D, SEQ)
    u_s = scratch("u_s", 3 * D, SEQ)
    g_s = scratch("g_s", 2 * D, SEQ)
    hid_s = scratch("hid_s", P, SEQ)
    taps_s = scratch("taps_s", 4 * D, SEQ)
    spec_s = scratch("spec_s", 2 * NBK * NK1 * P, 2 * CB)
    z1_s = scratch("z1_s", D, SEQ)
    z2_s = scratch("z2_s", D, SEQ)
    tok_s = scratch("tok_s", (NCC + NCH) * P, D + GROUPS * P)
    st_s = scratch("st_s", 2 * NCH * P, D)
    ym_s = scratch("ym_s", D, SEQ)
    mix_s = scratch("mix_s", D, SEQ)
    with ExitStack() as ctx:
        ph = Phase(nc, "keep", ctx)
        keep = {"par": ph.sb("par", [P, NPAR]), "mod": ph.sb("mod", [P, 2, 2, KT]), "gate": ph.sb("gate", [P, D])}
        mod = keep["mod"]
        phase_modulation(nc, t, keep, hid_s)
        with ExitStack() as hctx:
            h = Phase(nc, "hc", hctx)
            hi, lo = h.sb("hi", [P, KT, CTX], F32R), h.sb("lo", [P, KT, CTX], F32R)
            phase_norm(nc, "nc", t["ctxT"], CTX, mod[:, 1, 0, :], mod[:, 1, 1, :], hi, lo)
            phase_in_projection(nc, "pc", t["w_rec"], t["conv_taps"], [
                (T_XBC, 2 * KT, "conv_silu", xbc_c, 0), (T_DT, 1, "raw", dt_c)],
                                CTX, hi, lo)
        with ExitStack() as hctx:
            h = Phase(nc, "hl", hctx)
            hi, lo = h.sb("hi", [P, KT, SEQ], F32R), h.sb("lo", [P, KT, SEQ], F32R)
            phase_norm(nc, "nl", t["xT"], SEQ, mod[:, 0, 0, :], mod[:, 0, 1, :], hi, lo)
            phase_in_projection(nc, "pl", t["w_rec"], t["conv_taps"], [
                (T_Z, KT, "silu", z_s), (T_XBC, 2 * KT, "conv_silu", xbc_s, 0), (T_DT, 1, "raw", dt_s),
                (T_HG, KT, "silu", hg_s), (T_PROJ, 3 * KT, "conv", u_s, 2 * KT), (T_G, 2 * KT, "sigmoid", g_s)],
                SEQ, hi, lo)
        with ExitStack() as tctx:
            tables = hyena_tables(Phase(nc, "tab", tctx))
            phase_filter_taps(nc, t, keep, tables, hid_s, taps_s)
            phase_filter_spectra(nc, tables, taps_s, spec_s)
            phase_long_conv(nc, "c0", tables, u_s[0:D, :], u_s[D:2 * D, :], z1_s, spec_s, 0)
            phase_long_conv(nc, "c1", tables, z1_s, u_s[2 * D:3 * D, :], z2_s, spec_s, 1)
        with ExitStack() as sctx:
            ssd = ssd_buffers(Phase(nc, "ssd", sctx))
            phase_step_sizes(nc, t, dt_c, dt_s, ssd)
            phase_token_major(nc, t, xbc_c, xbc_s, tok_s, ssd)
            phase_states(nc, tok_s, st_s, ssd)
            phase_ssd_outputs(nc, t, xbc_s, tok_s, st_s, z_s, ym_s, ssd)
        phase_merge(nc, keep, t["w_br"], ym_s, z2_s, hg_s, g_s, mix_s)
        phase_output(nc, t, keep, mix_s, out)


def hyena_tables(ph):
    return {"f1": ph.sb("f1", [P, NR * CG]), "tw_fwd": ph.sb("tw_fwd", [P, NK1, 3, P]),
            "tw_inv": ph.sb("tw_inv", [P, NK1, 3, P]), "back": ph.sb("back", [P, 2, P]),
            "ident": ph.sb("ident", [P, P])}


def ssd_buffers(ph):
    NT = NCC + NCH
    ssd = {n: ph.sb(n, [P, NT, 2 * HEADS]) for n in ("dt", "a")}
    ssd.update({n: ph.sb(n, [P, NT, 2, HEADS]) for n in ("edge", "tail", "whole")})
    ssd.update(ident=ph.sb("ident", [P, P]), masks=ph.sb("masks", [P, 5, P]), d_row=ph.sb("d_row", [P, HEADS]))
    return ssd


def kernel(**inputs):
    import concourse.bacc as bacc
    from concourse.bass_utils import run_bass_kernel_spmd

    nc = bacc.Bacc("TRN2", target_bir_lowering=False, num_devices=1)
    arrays = {f"in_{k}": v for k, v in layout(inputs).items()}
    t = {k[3:]: nc.dram_tensor(k, v.shape, mybir.dt.from_np(v.dtype), kind="ExternalInput").ap()
         for k, v in arrays.items()}
    out = nc.dram_tensor("out", [SEQ, D], F32, kind="ExternalOutput").ap()
    program(nc, t, out)
    r = run_bass_kernel_spmd(nc, [arrays], core_ids=[0])
    return np.reshape(r.results[0]["out"], (1, SEQ, D))
```
